# Optimizing a Trainium2 kernel written in Bass

```python
import jax, jax.numpy as jnp
from jax import lax
import numpy as np

D_MODEL = 2048
BATCH = 1
SEQ = 2048
DEPTH = 1

EPS = 1e-6

N_ATT_HEADS = 8
ATT_HEAD_DIM = 128
Q_RANK = 512
KV_RANK = 256
N_IDX_HEADS = 8
IDX_DIM = 64
TOPK_MAX = 256
Q_BLOCK = 128

N_MLSTM_HEADS = 4
MLSTM_QK_DIM = 128
MLSTM_V_DIM = 256
MLSTM_CHUNK = 64
F_BIAS_INIT = 3.0

ATT_WIDTH = N_ATT_HEADS * ATT_HEAD_DIM
MLSTM_WIDTH = N_MLSTM_HEADS * MLSTM_V_DIM
MIX_WIDTH = ATT_WIDTH + MLSTM_WIDTH

IN_SPLITS = (Q_RANK, KV_RANK, IDX_DIM, N_IDX_HEADS,
             N_MLSTM_HEADS * MLSTM_QK_DIM, N_MLSTM_HEADS * MLSTM_QK_DIM,
             MLSTM_WIDTH, MLSTM_WIDTH, N_MLSTM_HEADS, N_MLSTM_HEADS)
D_IN = Q_RANK + KV_RANK + IDX_DIM + N_IDX_HEADS + 2 * N_MLSTM_HEADS * MLSTM_QK_DIM + 2 * MLSTM_WIDTH + 2 * N_MLSTM_HEADS

N_EXPERT_GROUPS = 4
EXPERTS_PER_GROUP = 8
N_EXPERTS = N_EXPERT_GROUPS * EXPERTS_PER_GROUP
TOP_K_EXPERTS = 2
D_FF_EXPERT = 512

kernel_name = "hybrid_dsa_mlstm_grouped_moe_adaln"

def rmsnorm(x, g):
    x32 = x.astype(jnp.float32)
    y = x32 * lax.rsqrt(jnp.mean(x32 * x32, axis=-1, keepdims=True) + EPS)
    return y.astype(x.dtype) * g

def dsa_attention(cq, ckv, k_idx, w_idx, w_uq, w_uk, w_uv, w_qidx):
    B, S, _ = cq.shape
    k_sel = min(TOPK_MAX, S // 4)
    nb = S // Q_BLOCK
    q = (cq @ w_uq).reshape(B, S, N_ATT_HEADS, ATT_HEAD_DIM)
    q_lat = jnp.einsum('bshd,rhd->bshr', q, w_uk)
    q_idx = (cq @ w_qidx).reshape(B, S, N_IDX_HEADS, IDX_DIM)
    w = w_idx * (N_IDX_HEADS ** -0.5 * IDX_DIM ** -0.5)
    scale = ATT_HEAD_DIM ** -0.5
    key_pos = jnp.arange(S)

    def to_blocks(a):
        return a.reshape(B, nb, Q_BLOCK, *a.shape[2:]).swapaxes(0, 1)

    def block(args):
        blk, ql, qi, wb = args
        t = blk * Q_BLOCK + jnp.arange(Q_BLOCK)
        isc = jax.nn.relu(jnp.einsum('bqhd,bsd->bqhs', qi, k_idx).astype(jnp.float32))
        isc = jnp.einsum('bqh,bqhs->bqs', wb.astype(jnp.float32), isc)
        causal = key_pos[None, :] <= t[:, None]
        isc = jnp.where(causal[None], isc, -jnp.inf)
        _, idx = lax.top_k(isc, k_sel)
        kv = jax.vmap(lambda c_b, i_b: c_b[i_b])(ckv, idx)
        s = jnp.einsum('bqhr,bqkr->bqhk', ql, kv).astype(jnp.float32) * scale
        valid = (idx <= t[None, :, None])[:, :, None, :]
        p = jax.nn.softmax(jnp.where(valid, s, -jnp.inf), axis=-1).astype(kv.dtype)
        o_lat = jnp.einsum('bqhk,bqkr->bqhr', p, kv)
        o = jnp.einsum('bqhr,rhd->bqhd', o_lat, w_uv)
        return o.reshape(B, Q_BLOCK, ATT_WIDTH)

    out = lax.map(block, (jnp.arange(nb), to_blocks(q_lat), to_blocks(q_idx), to_blocks(w)))
    return out.swapaxes(0, 1).reshape(B, S, ATT_WIDTH)

def mlstm(q, k, v, ig, fg):
    dtype = v.dtype
    B, S, NH, dk = q.shape
    dv = v.shape[-1]
    L = MLSTM_CHUNK
    nc = S // L

    def chunk4(a):
        return a.astype(jnp.float32).reshape(B, nc, L, NH, a.shape[-1]).transpose(1, 0, 3, 2, 4)

    def chunk3(a):
        return a.astype(jnp.float32).reshape(B, nc, L, NH).transpose(1, 0, 3, 2)

    qc = chunk4(q) * (dk ** -0.5)
    kc, vc = chunk4(k), chunk4(v)
    igc = chunk3(ig)
    lfc = jax.nn.log_sigmoid(chunk3(fg))
    causal = jnp.tril(jnp.ones((L, L), dtype=bool))

    def step(carry, xs):
        C, n, m = carry
        qb, kb, vb, ib, lf = xs
        b = lax.cumsum(lf, axis=2)
        dmat = b[..., :, None] - b[..., None, :] + ib[..., None, :]
        dmat = jnp.where(causal, dmat, -jnp.inf)
        m_inter = b + m[..., None]
        m_j = jnp.maximum(m_inter, dmat.max(-1))
        w_inter = jnp.exp(m_inter - m_j)
        sc = jnp.einsum('bhjd,bhsd->bhjs', qb, kb) * jnp.exp(dmat - m_j[..., None])
        num = w_inter[..., None] * jnp.einsum('bhjd,bhde->bhje', qb, C) + jnp.einsum('bhjs,bhse->bhje', sc, vb)
        den = w_inter * jnp.einsum('bhjd,bhd->bhj', qb, n) + sc.sum(-1)
        h = num / jnp.maximum(jnp.abs(den), jnp.exp(-m_j))[..., None]
        b_last = b[..., -1]
        g = b_last[..., None] - b + ib
        m_new = jnp.maximum(b_last + m, g.max(-1))
        w_old = jnp.exp(b_last + m - m_new)
        w_s = jnp.exp(g - m_new[..., None])
        C_new = w_old[..., None, None] * C + jnp.einsum('bhs,bhsd,bhse->bhde', w_s, kb, vb)
        n_new = w_old[..., None] * n + jnp.einsum('bhs,bhsd->bhd', w_s, kb)
        return (C_new, n_new, m_new), h

    init = (jnp.zeros((B, NH, dk, dv), jnp.float32),
            jnp.zeros((B, NH, dk), jnp.float32),
            jnp.zeros((B, NH), jnp.float32))
    _, h = lax.scan(step, init, (qc, kc, vc, igc, lfc))
    return h.transpose(1, 0, 3, 2, 4).reshape(B, S, NH, dv).astype(dtype)

def grouped_moe(h, router_w, router_b, w_gate_up, w_down):
    B, S, D = h.shape
    T = B * S
    xt = h.reshape(T, D)
    aff = jax.nn.sigmoid((xt @ router_w).astype(jnp.float32))
    sel = aff + router_b.astype(jnp.float32)
    grp = sel.reshape(T, N_EXPERT_GROUPS, EXPERTS_PER_GROUP)
    grp_score = lax.top_k(grp, TOP_K_EXPERTS)[0].sum(-1)
    g_idx = jnp.argmax(grp_score, axis=-1)
    in_grp = jnp.take_along_axis(grp, g_idx[:, None, None], axis=1)[:, 0]
    _, loc = lax.top_k(in_grp, TOP_K_EXPERTS)
    e_idx = g_idx[:, None] * EXPERTS_PER_GROUP + loc
    a = jnp.take_along_axis(aff, e_idx, axis=1)
    gates = a / a.sum(-1, keepdims=True)
    e_flat = e_idx.reshape(-1)
    tok = jnp.repeat(jnp.arange(T), TOP_K_EXPERTS)
    order = jnp.argsort(e_flat)
    tok_s = tok[order]
    gate_s = gates.reshape(-1)[order]
    group_sizes = jnp.bincount(e_flat, length=N_EXPERTS).astype(jnp.int32)
    xs = xt[tok_s]
    gu = lax.ragged_dot(xs, w_gate_up, group_sizes)
    gt, up = jnp.split(gu, 2, axis=-1)
    ys = lax.ragged_dot(jax.nn.silu(gt) * up, w_down, group_sizes) * gate_s[:, None].astype(xt.dtype)
    out = jnp.zeros_like(xt).at[tok_s].add(ys)
    return out.reshape(B, S, D)

def setup_inputs(seed: int = 0) -> dict:
    key = jax.random.key(seed)
    ks = jax.random.split(key, 24)

    def nrm(k, shape, scale):
        return jax.random.normal(k, shape, jnp.float32) * scale

    def gain(k, shape):
        return 1.0 + 0.01 * jax.random.normal(k, shape, jnp.float32)

    return {
        "x": nrm(ks[0], (BATCH, SEQ, D_MODEL), 1.0),
        "c": nrm(ks[1], (BATCH, D_MODEL), 1.0),
        "ada_w": nrm(ks[2], (DEPTH, D_MODEL, 6 * D_MODEL), 0.5 * D_MODEL ** -0.5),
        "ada_b": nrm(ks[3], (DEPTH, 6 * D_MODEL), 0.01),
        "mix_norm_g": gain(ks[4], (DEPTH, D_MODEL)),
        "w_in": nrm(ks[5], (DEPTH, D_MODEL, D_IN), D_MODEL ** -0.5),
        "cq_norm_g": gain(ks[6], (DEPTH, Q_RANK)),
        "ckv_norm_g": gain(ks[7], (DEPTH, KV_RANK)),
        "w_uq": nrm(ks[8], (DEPTH, Q_RANK, ATT_WIDTH), Q_RANK ** -0.5),
        "w_uk": nrm(ks[9], (DEPTH, KV_RANK, N_ATT_HEADS, ATT_HEAD_DIM), KV_RANK ** -0.5),
        "w_uv": nrm(ks[10], (DEPTH, KV_RANK, N_ATT_HEADS, ATT_HEAD_DIM), KV_RANK ** -0.5),
        "w_qidx": nrm(ks[11], (DEPTH, Q_RANK, N_IDX_HEADS * IDX_DIM), Q_RANK ** -0.5),
        "mlstm_i_b": nrm(ks[12], (DEPTH, N_MLSTM_HEADS), 0.1),
        "mlstm_f_b": F_BIAS_INIT + 3.0 * jax.random.uniform(ks[13], (DEPTH, N_MLSTM_HEADS), jnp.float32),
        "mlstm_norm_g": gain(ks[14], (DEPTH, N_MLSTM_HEADS, MLSTM_V_DIM)),
        "w_out": nrm(ks[15], (DEPTH, MIX_WIDTH, D_MODEL), MIX_WIDTH ** -0.5),
        "ffn_norm_g": gain(ks[16], (DEPTH, D_MODEL)),
        "router_w": nrm(ks[17], (D_MODEL, N_EXPERTS), D_MODEL ** -0.5),
        "router_b": nrm(ks[18], (N_EXPERTS,), 0.01),
        "w_gate_up": nrm(ks[19], (DEPTH, N_EXPERTS, D_MODEL, 2 * D_FF_EXPERT), D_MODEL ** -0.5),
        "w_down": nrm(ks[20], (DEPTH, N_EXPERTS, D_FF_EXPERT, D_MODEL), D_FF_EXPERT ** -0.5),
        "final_norm_g": gain(ks[21], (D_MODEL,)),
    }

def reference(x, c, ada_w, ada_b, mix_norm_g, w_in, cq_norm_g, ckv_norm_g, w_uq, w_uk, w_uv,
              w_qidx, mlstm_i_b, mlstm_f_b, mlstm_norm_g, w_out, ffn_norm_g, router_w, router_b,
              w_gate_up, w_down, final_norm_g):
    B, S, _ = x.shape
    NH = N_MLSTM_HEADS
    split_pts = np.cumsum(IN_SPLITS)[:-1].tolist()
    c_act = jax.nn.silu(c)
    for l in range(DEPTH):
        mod = (c_act @ ada_w[l] + ada_b[l])[:, None, :]
        sh1, sc1, g1, sh2, sc2, g2 = jnp.split(mod, 6, axis=-1)
        h = rmsnorm(x, mix_norm_g[l]) * (1 + sc1) + sh1
        z = h @ w_in[l]
        cq, ckv, k_idx, w_idx, mq, mk, mv, mo, mi, mf = jnp.split(z, split_pts, axis=-1)
        att = dsa_attention(rmsnorm(cq, cq_norm_g[l]), rmsnorm(ckv, ckv_norm_g[l]), k_idx, w_idx,
                            w_uq[l], w_uk[l], w_uv[l], w_qidx[l])
        hm = mlstm(mq.reshape(B, S, NH, MLSTM_QK_DIM), mk.reshape(B, S, NH, MLSTM_QK_DIM),
                   mv.reshape(B, S, NH, MLSTM_V_DIM), mi + mlstm_i_b[l], mf + mlstm_f_b[l])
        hm = rmsnorm(hm, mlstm_norm_g[l]).reshape(B, S, MLSTM_WIDTH) * jax.nn.sigmoid(mo)
        y = jnp.concatenate([att, hm], axis=-1) @ w_out[l]
        x = x + g1 * y
        h2 = rmsnorm(x, ffn_norm_g[l]) * (1 + sc2) + sh2
        x = x + g2 * grouped_moe(h2, router_w, router_b, w_gate_up[l], w_down[l])
    return rmsnorm(x, final_norm_g)


_drawn_inputs = setup_inputs


def setup_inputs(seed=0):
    import zlib

    import numpy as np

    out = dict(_drawn_inputs(seed))
    spreads = {}
    factors = {'mix_norm_g': 4.888,
     'cq_norm_g': 8.0,
     'ckv_norm_g': 8.0,
     'mlstm_i_b': 200.0,
     'mlstm_norm_g': 8.0,
     'ffn_norm_g': 2.849,
     'final_norm_g': 162.386}
    for name, (base, spread) in spreads.items():
        noise = np.random.default_rng([zlib.crc32(name.encode()), seed]).standard_normal(out[name].shape)
        drawn = base * np.exp(spread * noise) if base else spread * noise
        out[name] = __import__('jax').numpy.asarray(drawn.astype(out[name].dtype))
    for name, factor in factors.items():
        out[name] = (out[name] * factor).astype(out[name].dtype)
    return out
```

```python
from contextlib import ExitStack

import concourse.bass as bass
from concourse import mybir
F32=mybir.dt.float32
ALU=mybir.AluOpType; ACT=mybir.ActivationFunctionType; AX=mybir.AxisListType
D=2048; KD=16

def semaphores(nc, ctx, stage):
    held = []

    def close():
        nc.clear_and_free_semaphores(held)
        nc.all_engine_barrier()

    def sem(name):
        held.append(nc.alloc_semaphore(f"{stage}_{name}"))
        return held[-1]

    ctx.callback(close)
    return sem

def modulation(nc, c, ada_w, ada_b, mod):
    N=512; NB=6*D//N; SLOTS=3
    w_view=ada_w.rearrange("l (p k) n -> p (l k) n",k=KD)
    with ExitStack() as ctx:
        sb=lambda n,s,d=F32: ctx.enter_context(nc.sbuf_tensor("mod_"+n,s,d))
        sem=semaphores(nc,ctx,"mod")
        c_col=sb("c_col",[128,KD]); e_col=sb("e_col",[128,KD]); s_col=sb("s_col",[128,KD])
        w=sb("ada_w_ring",[128,SLOTS,KD,N]); row=sb("mod_row",[1,6*D])
        acc=ctx.enter_context(nc.psum_tensor("mod_mod_acc",[128,SLOTS,512],F32))
        c_loaded=sem("c_loaded"); b_loaded=sem("b_loaded"); w_loaded=[sem(f"w_loaded{i}") for i in range(SLOTS)]
        w_used=sem("w_used"); acc_free=sem("acc_free"); c_exp=sem("c_exp"); c_step=sem("c_step"); mod_stored=sem("mod_stored")
        block=ctx.enter_context(nc.Block())
        @block.sync
        def _(sp):
            sp.dma_start(c_col[:],c.rearrange("b (p k) -> p (b k)",k=KD)).then_inc(c_loaded,16)
            sp.dma_start(row[:],ada_b).then_inc(b_loaded,16)
            for j in range(SLOTS):
                sp.dma_start(w[:,j],w_view[:,:,j*N:(j+1)*N]).then_inc(w_loaded[j],16)
            with sp.Fori(1,NB//SLOTS) as g:
                for j in range(SLOTS):
                    sp.wait_ge(w_used,g*SLOTS+(j-SLOTS+1))
                    sp.dma_start(w[:,j],w_view[:,:,bass.ds(g*(SLOTS*N)+j*N,N)]).then_inc(w_loaded[j],16)
            sp.wait_ge(acc_free,NB+SLOTS)
            sp.dma_start(mod,row[:]).then_inc(mod_stored,16)
            sp.wait_ge(mod_stored,16)
        @block.scalar
        def _(act):
            act.wait_ge(c_loaded,16)
            nc.scalar.activation(e_col[:],c_col[:],ACT.Exp,scale=-1.0).then_inc(c_exp,1)
        @block.vector
        def _(dve):
            dve.wait_ge(c_exp,1)
            nc.vector.tensor_scalar_add(e_col[:],e_col[:],1.0).then_inc(c_step,1)
            dve.wait_ge(c_step,1)
            nc.vector.reciprocal(e_col[:],e_col[:]).then_inc(c_step,1)
            dve.wait_ge(c_step,2)
            nc.vector.tensor_tensor(s_col[:],e_col[:],c_col[:],ALU.mult).then_inc(c_step,1)
            dve.wait_ge(b_loaded,16)
            dve.sem_inc(acc_free,SLOTS)
            with dve.Fori(0,NB//SLOTS) as g:
                for j in range(SLOTS):
                    dve.wait_ge(w_used,g*SLOTS+(j+1))
                    nc.vector.tensor_tensor(row[:,bass.ds(g*(SLOTS*N)+j*N,N)],acc[0:1,j],row[:,bass.ds(g*(SLOTS*N)+j*N,N)],ALU.add).then_inc(acc_free,1)
        @block.tensor
        def _(pe):
            pe.wait_ge(c_step,3)
            with pe.Fori(0,NB//SLOTS) as g:
                for j in range(SLOTS):
                    pe.wait_ge(w_loaded[j],g*16+16)
                    pe.wait_ge(acc_free,g*SLOTS+(j+1))
                    for k in range(KD):
                        mm=nc.tensor.matmul(acc[0:1,j],s_col[:,k:k+1],w[:,j,k],start=(k==0),stop=(k==KD-1))
                    mm.then_inc(w_used,1)

S=2048; TT=S//128
D_IN=3920; ZN=490; ZB=D_IN//ZN
EPS=1e-6

def identity_tile(nc, pool, ident, made):
    pool.memset(ident[:],0.0).then_inc(made,1)
    pool.wait_ge(made,1)
    pool.affine_select(out=ident[:],in_=ident[:],compare_op=ALU.not_equal,fill=1.0,base=0,pattern=[[-1,128]],channel_multiplier=1).then_inc(made,1)

def in_projection(nc, x, mod, norm_g, w_in, z):
    xt=x.rearrange("b (t p) d -> (b t) p d",p=128)
    zt=z.rearrange("(t p) n -> t p n",p=128)
    wv=w_in.rearrange("l (k p) n -> p (l k) n",p=128)
    modv=mod.rearrange("l (s k p) -> s (l k) p",s=6,p=128)
    with ExitStack() as ctx:
        sb=lambda n,s,d=F32: ctx.enter_context(nc.sbuf_tensor("in_"+n,s,d))
        sem=semaphores(nc,ctx,"in")
        hT=sb("hT",[128,KD,S]); w=sb("w_in_ring",[128,2,KD,ZN])
        ident=sb("ident",[128,128]); rows=sb("param_rows",[3*KD,128]); cols=sb("param_cols",[128,3*KD])
        xb=w[:,1].rearrange("p k n -> p (k n)")[:,0:2*D].rearrange("p (s d) -> p s d",s=2)
        stage=sb("z_stage",[128,4,ZN]); ss=sb("sum_squares",[128,2]); rstd=sb("rstd",[128,2]); eps=sb("eps",[128,1])
        squares_out=stage[:].rearrange("p s n -> p (s n)")[:,0:D//2].bitcast(mybir.dt.bfloat16)
        FREE=4
        acc=ctx.enter_context(nc.psum_tensor("in_acc",[128,8,512],F32))
        xn=xb
        params_loaded=sem("params_loaded"); ident_made=sem("ident_made"); params_turned=sem("params_turned"); params_ready=sem("params_ready")
        x_loaded=[sem(f"x_loaded{i}") for i in range(2)]; ss_ready=sem("ss_ready"); rms_ready=sem("rms_ready"); rstd_ready=sem("rstd_ready")
        xn_ready=sem("xn_ready"); turned=sem("turned"); hT_act=sem("hT_act"); hT_dve=sem("hT_dve")
        w_loaded=[sem(f"w_loaded{i}") for i in range(2)]; z_acc=sem("z_acc")
        z_act=sem("z_act"); z_dve=sem("z_dve"); stored=[sem(f"z_stored{i}") for i in range(4)]
        block=ctx.enter_context(nc.Block())
        HK=KD//2
        @block.gpsimd
        def _(pool):
            identity_tile(nc,pool,ident,ident_made)
            pool.memset(eps[:],EPS).then_inc(ident_made,1)
        @block.sync
        def _(sp):
            for s in stored: sp.sem_inc(s,16)
            sp.dma_start(rows[0:KD],norm_g.rearrange("l (k p) -> (l k) p",p=128)).then_inc(params_loaded,16)
            sp.dma_start(rows[KD:2*KD],modv[1]).then_inc(params_loaded,16)
            sp.dma_start(rows[2*KD:3*KD],modv[0]).then_inc(params_loaded,16)
            with sp.Fori(0,TT//2) as g:
                for j in range(2):
                    sp.wait_ge(turned,g*2+(j)+1)
                    sp.dma_start(xb[:,j],xt[g*2+j]).then_inc(x_loaded[j],16)
            with sp.Fori(0,ZB) as n:
                for m in range(TT):
                    sp.wait_ge((z_act,z_dve)[m%2],n*(TT//2)+(m//2+1+FREE))
                    sp.dma_start(zt[m,:,bass.ds(n*ZN,ZN)],stage[:,m%4]).then_inc(stored[m%4],16)
            for s in range(4): sp.wait_ge(stored[s],16*ZB*TT//4+16)
        @block.scalar
        def _(act):
            act.sem_inc(hT_act,1)
            act.dma_start(w[:,0],wv[:,:,0:ZN]).then_inc(w_loaded[0],16)
            act.wait_ge(ident_made,3)
            def squares(t,j):
                act.wait_ge(x_loaded[j],t*16+16)
                nc.scalar.activation(squares_out,xb[:,j],ACT.Square,accum_out=ss[:,j:j+1]).then_inc(ss_ready,1)
            def root(t2,j):
                act.wait_ge(ss_ready,t2*2+j+1)
                nc.scalar.activation(rstd[:,j:j+1],ss[:,j:j+1],ACT.Sqrt,bias=eps[:],scale=1.0/D).then_inc(rms_ready,1)
            def evac(t2,j):
                act.wait_ge(turned,t2*2+j+1+1)
                for k in range(HK):
                    i=nc.scalar.activation(hT[:,k,bass.ds(t2*256+j*128,128)],acc[:,4*j+k//4,(k%4)*128:(k%4)*128+128],ACT.Identity,scale=cols[:,k:k+1],bias=cols[:,2*KD+k:2*KD+k+1])
                i.then_inc(hT_act,1)
            act.wait_ge(params_ready,2)
            with act.Fori(0,TT//2) as g:
                for j in range(2):
                    squares(g,j); root(g,j); evac(g,j)
            act.wait_ge(turned,TT+1)
            act.dma_start(w[:,1],wv[:,:,ZN:2*ZN]).then_inc(w_loaded[1],16)
            act.sem_inc(z_act,FREE)
            def z_evac(n2,j):
                for m in range(0,TT,2):
                    act.wait_ge(z_acc,n2*(2*TT)+j*TT+m+1)
                    act.wait_ge(stored[m%4],n2*(16*TT//2)+16*(j*TT//4+m//4)+16)
                    nc.scalar.copy(stage[:,m%4],acc[:,m%8,0:ZN]).then_inc(z_act,1)
            with act.Fori(0,ZB//2-1) as g:
                for j in range(2):
                    z_evac(g,j)
                    act.wait_ge(z_acc,g*(2*TT)+(j+1)*TT)
                    act.dma_start(w[:,j],wv[:,:,bass.ds(g*(2*ZN)+(j+2)*ZN,ZN)]).then_inc(w_loaded[j],16)
            for j in range(2): z_evac(ZB//2-1,j)
        @block.vector
        def _(dve):
            dve.sem_inc(hT_dve,1)
            dve.wait_ge(params_turned,1)
            nc.vector.tensor_copy(cols[:],acc[:,0,0:3*KD]).then_inc(params_ready,1)
            dve.wait_ge(params_ready,1)
            nc.vector.scalar_tensor_tensor(out=cols[:,0:KD],in0=cols[:,KD:2*KD],scalar=1.0,in1=cols[:,0:KD],op0=ALU.add,op1=ALU.mult).then_inc(params_ready,1)
            dve.wait_ge(params_ready,2)
            with dve.Fori(0,TT//2) as g:
                for j in range(2):
                    dve.wait_ge(rms_ready,g*2+j+1)
                    nc.vector.reciprocal(rstd[:,j:j+1],rstd[:,j:j+1]).then_inc(rstd_ready,1)
                    dve.wait_ge(rstd_ready,g*2+j+1)
                    nc.vector.tensor_scalar(xn[:,j],xb[:,j],rstd[:,j:j+1],None,ALU.mult).then_inc(xn_ready,1)
                    dve.wait_ge(turned,g*2+j+1+1)
                    for k in range(HK,KD):
                        i=nc.vector.tensor_scalar(hT[:,k,bass.ds(g*256+j*128,128)],acc[:,4*j+k//4,(k%4)*128:(k%4)*128+128],cols[:,k:k+1],cols[:,2*KD+k:2*KD+k+1],ALU.mult,ALU.add)
                    i.then_inc(hT_dve,1)
            dve.sem_inc(z_dve,FREE)
            with dve.Fori(0,ZB) as n:
                for m in range(1,TT,2):
                    dve.wait_ge(z_acc,n*TT+m+1)
                    dve.wait_ge(stored[m%4],n*(16*TT//4)+16*(m//4)+16)
                    nc.vector.tensor_copy(stage[:,m%4],acc[:,m%8,0:ZN]).then_inc(z_dve,1)
        @block.tensor
        def _(pe):
            pe.sem_inc(turned,1)
            pe.wait_ge(ident_made,2); pe.wait_ge(params_loaded,48)
            nc.tensor.transpose(acc[:,0,0:3*KD],rows[:],ident[0:3*KD,0:3*KD]).then_inc(params_turned,1)
            pe.wait_ge(params_ready,1)
            with pe.Fori(0,TT//2) as g:
                for j in range(2):
                    pe.wait_ge(xn_ready,g*2+j+1)
                    pe.wait_ge(hT_act,g*2+1); pe.wait_ge(hT_dve,g*2+1)
                    for k in range(KD):
                        t=nc.tensor.transpose(acc[:,4*j+k//4,(k%4)*128:(k%4)*128+128],xn[:,j,k*128:(k+1)*128],ident[:])
                    t.then_inc(turned,1)
            pe.wait_ge(hT_act,TT+1); pe.wait_ge(hT_dve,TT+1)
            with pe.Fori(0,ZB//2) as g:
                for j in range(2):
                    pe.wait_ge(w_loaded[j],g*16+16)
                    for m in range(TT):
                        pe.wait_ge((z_act,z_dve)[m%2],g*TT+(j*(TT//2)+m//2+1))
                        for k in range(KD):
                            mm=nc.tensor.matmul(acc[:,m%8,0:ZN],hT[:,k,m*128:(m+1)*128],w[:,j,k],start=(k==0),stop=(k==KD-1))
                        mm.then_inc(z_acc,1)

NH=4; DK=128; DV=256; DVA=DV+1; C=128; NC=S//C
Z_CQ,Z_CKV,Z_KI,Z_WI,Z_MQ,Z_MK,Z_MV,Z_MO,Z_MI,Z_MF=0,512,768,832,840,1352,1864,2888,3912,3916
BIG=1e30

def mlstm(nc, z, i_b, f_b, norm_g, y):
    zt=z.rearrange("(t p) n -> p t n",p=128)
    zc=z.rearrange("(t p) n -> t p n",p=128)
    yc=y.rearrange("(t p) n -> t p n",p=128)
    with ExitStack() as ctx:
        sb=lambda n,s,d=F32: ctx.enter_context(nc.sbuf_tensor("ml_"+n,s,d))
        sem=semaphores(nc,ctx,"ml")
        ident=sb("ident",[128,128]); sel=sb("head_rows",[NH,NH,128]); mask=sb("future_mask",[128,128])
        A=sb("A",[NH,S]); gcols=sb("gate_cols",[128,4,NC,NH]); wold=sb("wold",[128,NH,NC])
        gbc=sb("norm_g_rows",[128,NH*DV])
        with ExitStack() as gctx:
            gsb=lambda n,s,d=F32: gctx.enter_context(nc.sbuf_tensor("mlg_"+n,s,d))
            gsem=semaphores(nc,gctx,"mlg")
            zg=gsb("gates_in",[128,NC,8]); bias=gsb("gate_bias",[NH,2]); I=gsb("I",[NH,S]); Fg=gsb("F",[NH,S]); E=gsb("E",[NH,S]); L=gsb("L",[NH,S])
            b=gsb("b",[NH,S]); reset=gsb("reset",[NH,S]); step=gsb("step",[NH,S]); a=gsb("a",[NH,S]); Mp=gsb("m_prev",[NH,NC]); Wo=gsb("w_old",[NH,NC])
            win=gsb("w_inter",[NH,S]); en=gsb("exp_neg_m",[NH,S]); ws=gsb("w_s",[NH,S])
            ps=gctx.enter_context(nc.psum_tensor("ml_gates_ps",[128,8,512],F32))
            loaded=gsem("gates_loaded"); made=gsem("consts_made"); turned=gsem("gates_turned"); biased=gsem("gates_biased"); absd=gsem("abs_ready"); ln1p=gsem("ln_ready")
            v=gsem("vector_done"); expd=gsem("exp_ready"); cols_ps=gsem("cols_in_psum"); cdone=gsem("cols_copied")
            block=gctx.enter_context(nc.Block())
            ch=lambda t: t[:].rearrange("h (c j) -> h c j",j=C)
            @block.sync
            def _(sp):
                with nc.allow_non_contiguous_dma(reason="short rows of gates"):
                    sp.dma_start(zg[:],zt[:,:,Z_MI:Z_MI+8]).then_inc(loaded,16)
                    sp.dma_start(bias[:,0:1],i_b.rearrange("l h -> h l")).then_inc(loaded,16)
                    sp.dma_start(bias[:,1:2],f_b.rearrange("l h -> h l")).then_inc(loaded,16)
                sp.dma_start(gbc[:],norm_g.rearrange("l h v -> l (h v)").to_broadcast([128,NH*DV])).then_inc(loaded,16)
                sp.wait_ge(loaded,64)
            @block.gpsimd
            def _(pool):
                identity_tile(nc,pool,ident,made)
                pool.memset(mask[:],0.0).then_inc(made,1)
                pool.memset(sel[:],1.0).then_inc(made,1)
                pool.wait_ge(made,4)
                pool.affine_select(out=mask[:],in_=mask[:],compare_op=ALU.is_ge,fill=BIG,base=0,pattern=[[1,128]],channel_multiplier=-1).then_inc(made,1)
                pool.affine_select(out=sel[:],in_=sel[:],compare_op=ALU.is_equal,fill=0.0,base=0,pattern=[[-1,NH],[0,128]],channel_multiplier=1).then_inc(made,1)
                pool.memset(reset[:],1.0).then_inc(made,1)
                pool.memset(step[:],0.0).then_inc(made,1)
                pool.memset(Mp[:],0.0).then_inc(made,1)
                pool.wait_ge(made,7)
                pool.memset(ch(reset)[:,:,0:1],0.0).then_inc(made,1)
            @block.tensor
            def _(pe):
                pe.wait_ge(loaded,64); pe.wait_ge(made,10)
                for c in range(NC):
                    nc.tensor.transpose(ps[0:NH,c//4,(c%4)*128:(c%4)*128+128],zg[:,c,0:4],ident[:])
                    t=nc.tensor.transpose(ps[0:NH,4+c//4,(c%4)*128:(c%4)*128+128],zg[:,c,4:8],ident[:])
                t.then_inc(turned,1)
                pe.wait_ge(expd,4); 
                for q,r in enumerate((a,win,en,ws)):
                    for c in range(NC):
                        nc.tensor.transpose(ps[:,0,(q*NC+c)*NH:(q*NC+c+1)*NH],r[:,c*C:(c+1)*C],ident[0:NH,0:NH])
                for h in range(NH):
                    t=nc.tensor.matmul(ps[:,1,h*NC:(h+1)*NC],sel[:,h],Wo[:],start=True,stop=True)
                t.then_inc(cols_ps,1)
            @block.scalar
            def _(act):
                act.wait_ge(loaded,64); act.wait_ge(turned,1)
                nc.scalar.activation(I[:],ps[0:NH,0:4].rearrange("h b n -> h (b n)"),ACT.Identity,bias=bias[:,0:1]).then_inc(biased,1)
                nc.scalar.activation(Fg[:],ps[0:NH,4:8].rearrange("h b n -> h (b n)"),ACT.Identity,bias=bias[:,1:2]).then_inc(biased,1)
                act.wait_ge(biased,2)
                nc.scalar.activation(E[:],Fg[:],ACT.Abs).then_inc(absd,1)
                act.wait_ge(absd,1)
                nc.scalar.activation(E[:],E[:],ACT.Exp,scale=-1.0).then_inc(ln1p,1)
                act.wait_ge(ln1p,1)
                nc.scalar.activation(L[:],E[:],ACT.Ln,bias=1.0).then_inc(ln1p,1)
                act.wait_ge(v,9)
                nc.scalar.activation(win[:],win[:],ACT.Exp).then_inc(expd,1)
                act.wait_ge(v,10)
                nc.scalar.activation(en[:],en[:],ACT.Exp,scale=-1.0).then_inc(expd,1)
                act.wait_ge(v,11)
                nc.scalar.activation(ws[:],ws[:],ACT.Exp).then_inc(expd,1)
                act.wait_ge(v,12)
                nc.scalar.activation(Wo[:],Wo[:],ACT.Exp).then_inc(expd,1)
            @block.vector
            def _(dve):
                dve.wait_ge(ln1p,2); dve.wait_ge(made,10)
                nc.vector.scalar_tensor_tensor(out=L[:],in0=Fg[:],scalar=0.0,in1=L[:],op0=ALU.min,op1=ALU.subtract).then_inc(v,1)
                dve.wait_ge(v,1)
                nc.vector.tensor_tensor_scan(b[:],reset[:],L[:],0.0,ALU.mult,ALU.add).then_inc(v,1)
                dve.wait_ge(v,2)
                nc.vector.tensor_tensor(a[:],I[:],b[:],ALU.subtract).then_inc(v,1)
                nc.vector.tensor_copy(ch(step)[:,1:NC,0:1],ch(b)[:,0:NC-1,C-1:C]).then_inc(v,1)
                dve.wait_ge(v,4)
                nc.vector.tensor_tensor_scan(A[:],step[:],a[:],0.0,ALU.add,ALU.max).then_inc(v,1)
                dve.wait_ge(v,5)
                nc.vector.tensor_tensor(Mp[:,1:NC],ch(b)[:,0:NC-1,C-1],ch(A)[:,0:NC-1,C-1],ALU.add).then_inc(v,1)
                nc.vector.tensor_copy(Wo[:],ch(A)[:,:,C-1]).then_inc(v,1)
                dve.wait_ge(v,7)
                nc.vector.tensor_copy(reset[:,0:1],b[:,0:1]).then_inc(v,1)
                nc.vector.tensor_tensor(ch(win),Mp[:].broadcast(2,C) if False else Mp[:].rearrange("h (c o) -> h c o",o=1).to_broadcast([NH,NC,C]),ch(A),ALU.subtract).then_inc(v,1)
                nc.vector.tensor_tensor(en[:],b[:],A[:],ALU.add).then_inc(v,1)
                nc.vector.tensor_tensor(ch(ws),ch(a),Wo[:].rearrange("h (c o) -> h c o",o=1).to_broadcast([NH,NC,C]),ALU.subtract).then_inc(v,1)
                dve.wait_ge(v,11)
                nc.vector.tensor_tensor(Wo[:],Mp[:],Wo[:],ALU.subtract).then_inc(v,1)
                dve.wait_ge(cols_ps,1)
                nc.vector.tensor_copy(gcols[:].rearrange("p q c h -> p (q c h)"),ps[:,0,0:4*NC*NH]).then_inc(cdone,1)
                nc.vector.tensor_copy(wold[:].rearrange("p h c -> p (h c)"),ps[:,1,0:NH*NC]).then_inc(cdone,1)
                dve.wait_ge(cdone,2)
        zq=sb("zq",[128,2,2*NH*DK]); va=sb("va",[128,2,NH,DVA]); zo=sb("zo",[128,2,NH*DV])
        qT=sb("qT",[128,NH,C]); kT=sb("kT",[128,NH,C]); kw=sb("kw",[128,NH,DK]); Dm=sb("Dm",[128,NH,C]); Ex=sb("Ex",[128,NH,C]); W=sb("W",[128,NH,C])
        Cst=sb("C_state",[128,NH,DVA]); intra=sb("intra",[128,NH,DVA]); num=sb("num",[128,NH,DVA]); hn=sb("hn",[128,NH,DV])
        den=sb("den",[128,NH]); ss=sb("ss",[128,NH]); f=sb("f",[128,NH]); sg=sb("sg",[128,NH*DV]); yo=sb("yo",[128,2,NH*DV]); eps=sb("eps",[128,1])
        ps=ctx.enter_context(nc.psum_tensor("ml_ps",[128,8,512],F32)); TQ,TK,AB,SC,OUT=0,1,2,3,4
        z_loaded=[sem(f"z_loaded{j}") for j in range(2)]; init=sem("state_zeroed"); sp_waited=sem("sp_waited")
        qk_turned=sem("qk_turned"); a_wide=sem("a_wide"); q_ready=sem("q_ready"); k_ready=sem("k_ready"); scores=sem("scores"); D_ready=sem("D_ready"); E_ready=sem("E_ready")
        W_ready=sem("W_ready"); kw_ready=sem("kw_ready"); out_ready=sem("out_ready"); intra_copied=sem("intra_copied"); inter_used=sem("inter_used"); state_used=sem("state_used")
        sg_exp=sem("sg_exp"); r_ready=sem("r_ready"); ss_ready=sem("ss_ready"); rs_ready=sem("rs_ready"); dchain=sem("dchain"); f_ready=sem("f_ready"); den_abs=sem("den_abs"); y_ready=sem("y_ready"); y_stored=[sem(f"y_stored{j}") for j in range(2)]
        block=ctx.enter_context(nc.Block())
        @block.sync
        def _(sp):
            for s in y_stored: sp.sem_inc(s,16)
            def load(c,j):
                sp.dma_start(zq[:,j],zc[c,:,Z_MQ:Z_MV]).then_inc(z_loaded[j],16)
                sp.dma_start(va[:,j,:,0:DV],zc[c,:,Z_MV:Z_MO].rearrange("p (h v) -> p h v",h=NH)).then_inc(z_loaded[j],16)
                sp.dma_start(zo[:,j],zc[c,:,Z_MO:Z_MI]).then_inc(z_loaded[j],16)
            for j in range(2): load(j,j)
            with sp.Fori(0,NC//2-1) as g:
                for j in range(2):
                    sp.wait_ge(y_ready,g*2+j+1+1)
                    sp.sem_inc(sp_waited,1)
                    load(g*2+j+2,j)
                    sp.dma_start(yc[g*2+j,:,1024:2048],yo[:,j]).then_inc(y_stored[j],16)
            for j in range(2):
                sp.wait_ge(y_ready,NC-1+j+1)
                sp.dma_start(yc[NC-2+j,:,1024:2048],yo[:,j]).then_inc(y_stored[j],16)
            for j in range(2): sp.wait_ge(y_stored[j],16*NC//2+16)
        @block.gpsimd
        def _(pool):
            pool.memset(Cst[:],0.0).then_inc(init,1)
            pool.memset(va[:,:,:,DV:DVA],1.0).then_inc(init,1)
            pool.memset(eps[:],EPS).then_inc(init,1)
        order=[(h,kind) for h in range(NH) for kind in range(3)]
        done_of=(intra_copied,inter_used,state_used)
        @block.tensor
        def _(pe):
            pe.sem_inc(out_ready,1)
            pe.sem_inc(scores,1)
            pe.wait_ge(init,3)
            with pe.Fori(0,NC//2) as g:
                for j in range(2):
                    pe.wait_ge(z_loaded[j],g*48+48)
                    pe.wait_ge(k_ready,g*2+j+1); pe.wait_ge(q_ready,g*2+j+1)
                    for h in range(NH):
                        nc.tensor.transpose(ps[:,TQ,h*128:h*128+128],zq[:,j,h*128:h*128+128],ident[:])
                        t=nc.tensor.transpose(ps[:,TK,h*128:h*128+128],zq[:,j,NH*DK+h*128:NH*DK+h*128+128],ident[:])
                    t.then_inc(qk_turned,1)
                    pe.wait_ge(D_ready,g*2+j+1)
                    for h in range(NH):
                        t=nc.tensor.matmul(ps[:,AB,h*128:h*128+128],sel[:,h],A[:,bass.ds(g*(2*C)+j*C,C)],start=True,stop=True)
                    t.then_inc(a_wide,1)
                    pe.wait_ge(k_ready,g*2+j+1+1); pe.wait_ge(q_ready,g*2+j+1+1); pe.wait_ge(W_ready,g*2+j+1)
                    for h in range(NH):
                        t=nc.tensor.matmul(ps[:,SC,h*128:h*128+128],kT[:,h],qT[:,h],start=True,stop=True)
                    t.then_inc(scores,1)
                    pe.wait_ge(state_used,g*8+j*4+4); pe.wait_ge(W_ready,g*2+j+1+1); pe.wait_ge(kw_ready,g*2+j+1)
                    for n,(h,kind) in enumerate(order):
                        ph,pk=order[(n-4)%12]
                        pe.wait_ge(done_of[pk],g*8+(j*4+ph+1+(4 if n>=4 else 0)))
                        lhs,rhs=((W[:,h],va[:,j,h]),(qT[:,h],Cst[:,h]),(kw[:,h],va[:,j,h]))[kind]
                        nc.tensor.matmul(ps[:,OUT+n%4,0:DVA],lhs,rhs,start=True,stop=True).then_inc(out_ready,1)
        @block.scalar
        def _(act):
            act.sem_inc(E_ready,1)
            act.sem_inc(q_ready,1)
            act.wait_ge(init,3)
            act.sem_inc(intra_copied,4)
            with act.Fori(0,NC//2) as g:
                for j in range(2):
                    col=lambda q,h: gcols[:,q,bass.ds(g*2+j,1),h]
                    act.wait_ge(qk_turned,g*2+j+1)
                    act.wait_ge(out_ready,g*24+12*j+1)
                    nc.scalar.activation(qT[:].rearrange("p h c -> p (h c)"),ps[:,TQ],ACT.Copy,scale=float(DK)**-0.5).then_inc(q_ready,1)
                    act.wait_ge(z_loaded[j],g*48+48)
                    for h in range(NH):
                        t=nc.scalar.activation(kw[:,h],zq[:,j,NH*DK+h*128:NH*DK+h*128+128],ACT.Copy,scale=col(3,h))
                    t.then_inc(kw_ready,1)
                    act.wait_ge(D_ready,g*2+j+1+1); act.wait_ge(W_ready,g*2+j+1)
                    for h in range(NH):
                        t=nc.scalar.activation(Ex[:,h],Dm[:,h],ACT.Exp,scale=-1.0,bias=col(0,h))
                    t.then_inc(E_ready,1)
                    act.wait_ge(y_ready,g*2+j+1)
                    nc.scalar.activation(sg[:],zo[:,j],ACT.Exp,scale=-1.0).then_inc(sg_exp,1)
                    for h in range(NH):
                        act.wait_ge(out_ready,g*24+(12*j+3*h+1)+1); act.wait_ge(inter_used,g*8+(j*4+h+1))
                        nc.scalar.copy(intra[:,h],ps[:,OUT+(3*h)%4,0:DVA]).then_inc(intra_copied,1)
                    act.wait_ge(inter_used,g*8+(j*4+8)); act.wait_ge(f_ready,g*4+j*2+1)
                    nc.scalar.activation(den[:],num[:,:,DV],ACT.Abs).then_inc(den_abs,1)
                    act.wait_ge(r_ready,g*2+j+1)
                    for h in range(NH):
                        t=nc.scalar.activation(hn[:,h],num[:,h,0:DV],ACT.Square,scale=den[:,h:h+1],accum_out=ss[:,h:h+1])
                        t.then_inc(ss_ready,1)
                    act.wait_ge(ss_ready,g*8+j*4+4)
                    nc.scalar.activation(ss[:],ss[:],ACT.Ln,scale=1.0/DV,bias=eps[:]).then_inc(rs_ready,1)
                    act.wait_ge(rs_ready,g*4+j*2+1)
                    nc.scalar.activation(ss[:],ss[:],ACT.Exp,scale=-0.5).then_inc(rs_ready,1)
        @block.vector
        def _(dve):
            dve.sem_inc(D_ready,1)
            dve.sem_inc(W_ready,1)
            dve.sem_inc(f_ready,1)
            dve.sem_inc(k_ready,1)
            dve.sem_inc(y_ready,1)
            dve.wait_ge(init,3)
            dve.sem_inc(inter_used,4); dve.sem_inc(state_used,4)
            with dve.Fori(0,NC//2) as g:
                for j in range(2):
                    col=lambda q,h: gcols[:,q,bass.ds(g*2+j,1),h]
                    dve.wait_ge(qk_turned,g*2+j+1)
                    dve.wait_ge(scores,g*2+j+1)
                    nc.vector.tensor_copy(kT[:].rearrange("p h c -> p (h c)"),ps[:,TK]).then_inc(k_ready,1)
                    dve.wait_ge(a_wide,g*2+j+1); dve.wait_ge(E_ready,g*2+j+1)
                    nc.vector.tensor_tensor(Dm[:],ps[:,AB].rearrange("p (h c) -> p h c",h=NH),mask[:].rearrange("p (o c) -> p o c",o=1).to_broadcast([128,NH,C]),ALU.add).then_inc(D_ready,1)
                    dve.wait_ge(scores,g*2+j+1+1); dve.wait_ge(E_ready,g*2+j+1+1)
                    dve.wait_ge(out_ready,g*24+12*j+1)
                    nc.vector.tensor_tensor(W[:].rearrange("p h c -> p (h c)"),ps[:,SC],Ex[:].rearrange("p h c -> p (h c)"),ALU.mult).then_inc(W_ready,1)
                    dve.wait_ge(sg_exp,g*2+j+1)
                    nc.vector.tensor_scalar(sg[:],sg[:],1.0,None,ALU.add).then_inc(dchain,1)
                    dve.wait_ge(dchain,g*6+j*3+1)
                    nc.vector.reciprocal(sg[:],sg[:]).then_inc(dchain,1)
                    dve.wait_ge(dchain,g*6+j*3+2)
                    nc.vector.tensor_tensor(sg[:],sg[:],gbc[:],ALU.mult).then_inc(dchain,1)
                    for h in range(NH):
                        n=3*h+1
                        dve.wait_ge(out_ready,g*24+(12*j+n+1)+1); dve.wait_ge(intra_copied,g*8+(j*4+h+1+4))
                        nc.vector.scalar_tensor_tensor(out=num[:,h],in0=ps[:,OUT+n%4,0:DVA],scalar=col(1,h),in1=intra[:,h],op0=ALU.mult,op1=ALU.add).then_inc(inter_used,1)
                        dve.wait_ge(out_ready,g*24+(12*j+n+2)+1)
                        nc.vector.scalar_tensor_tensor(out=Cst[:,h],in0=Cst[:,h],scalar=wold[:,h,bass.ds(g*2+j,1)],in1=ps[:,OUT+(n+1)%4,0:DVA],op0=ALU.mult,op1=ALU.add).then_inc(state_used,1)
                    dve.wait_ge(den_abs,g*2+j+1)
                    nc.vector.tensor_tensor(den[:],den[:],gcols[:,2,bass.ds(g*2+j,1),:].rearrange("p o h -> p (o h)"),ALU.max).then_inc(f_ready,1)
                    dve.wait_ge(f_ready,g*4+j*2+1+1)
                    nc.vector.reciprocal(den[:],den[:]).then_inc(r_ready,1)
                    dve.wait_ge(rs_ready,g*4+j*2+2); dve.wait_ge(r_ready,g*2+j+1)
                    nc.vector.tensor_tensor(f[:],den[:],ss[:],ALU.mult).then_inc(f_ready,1)
                    dve.wait_ge(f_ready,g*4+j*2+2+1); dve.wait_ge(y_stored[j],g*16+16)
                    for h in range(NH):
                        t=nc.vector.scalar_tensor_tensor(out=yo[:,j,h*DV:(h+1)*DV],in0=num[:,h,0:DV],scalar=f[:,h:h+1],in1=sg[:,h*DV:(h+1)*DV],op0=ALU.mult,op1=ALU.mult)
                    t.then_inc(y_ready,1)

QR=512; KR=256; NIH=8; ID=64; TOPK=256; NAH=8; HD=128
BF=mybir.dt.bfloat16
QK_=QR//128; KK=KR//128
WIDTH=[(b+1)*128 for b in range(TT)]
MOFF=[sum(WIDTH[:b]) for b in range(TT)]; MTOT=sum(WIDTH)
TAKEN=-3e38; UNSEEN=-1e30

def dsa(nc, z, cq_g, ckv_g, w_uq, w_uk, w_uv, w_qidx, y):
    zt=z.rearrange("(t p) n -> t p n",p=128)
    yt=y.rearrange("(t p) n -> t p n",p=128)
    with ExitStack() as ctx:
        sb=lambda n,s,d=F32: ctx.enter_context(nc.sbuf_tensor("dsa_"+n,s,d))
        cqT=sb("cqT",[128,QK_,S]); ckvT=sb("ckvT",[128,KK,S]); bias=sb("select_bias",[128,MTOT],BF); ident=sb("ident",[128,128])
        with ExitStack() as ictx:
            kiT=ictx.enter_context(nc.sbuf_tensor("kiT",[128,S],F32)); wi=ictx.enter_context(nc.sbuf_tensor("w_idx",[128,TT,NIH],F32))
            latents(nc,zt,z,cq_g,ckv_g,cqT,ckvT,kiT,wi,ident)
            indexer(nc,w_qidx,cqT,kiT,wi,bias)
        attention(nc,w_uq,w_uk,w_uv,cqT,ckvT,bias,ident,yt)

def latents(nc,zt,z,cq_g,ckv_g,cqT,ckvT,kiT,wi,ident):
    NL=QR+KR; NT=QK_+KK+1
    with ExitStack() as ctx:
        sb=lambda n,s,d=F32: ctx.enter_context(nc.sbuf_tensor("lat_"+n,s,d))
        sem=semaphores(nc,ctx,"lat")
        zl=sb("z_latents",[128,2,NL+2*ID]); xn=sb("latents_normed",[128,2,NL]); junk=sb("squares",[128,2,NL]); ss=sb("ss",[128,2,2]); rs=sb("rs",[128,2,2]); eps=sb("eps",[128,1])
        grow=sb("gain_rows",[QK_+KK,128]); gcol=sb("gain_cols",[128,QK_+KK])
        ps=ctx.enter_context(nc.psum_tensor("lat_ps",[128,8,512],F32))
        loaded=[sem(f"loaded{j}") for j in range(2)]; const_loaded=sem("const_loaded"); made=sem("made"); gturned=sem("gains_turned"); gready=sem("gains_ready"); wi_ready=sem("wi_ready")
        ss_ready=sem("ss_ready"); ln_ready=sem("ln_ready"); rs_ready=sem("rs_ready"); xn_ready=sem("xn_ready"); turned=sem("turned"); act_ev=sem("act_evacuated"); dve_ev=sem("dve_evacuated")
        block=ctx.enter_context(nc.Block())
        @block.gpsimd
        def _(pool):
            identity_tile(nc,pool,ident,made)
            pool.memset(eps[:],EPS).then_inc(made,1)
        @block.sync
        def _(sp):
            sp.dma_start(grow[0:QK_],cq_g.rearrange("l (k p) -> (l k) p",p=128)).then_inc(const_loaded,16)
            sp.dma_start(grow[QK_:],ckv_g.rearrange("l (k p) -> (l k) p",p=128)).then_inc(const_loaded,16)
            with nc.allow_non_contiguous_dma(reason="short rows"):
                sp.dma_start(wi[:],z.rearrange("(t p) n -> p t n",p=128)[:,:,Z_WI:Z_WI+NIH]).then_inc(const_loaded,16)
            with sp.Fori(0,TT//2) as g:
                for j in range(2):
                    sp.wait_ge(turned,g*2+j+1)
                    sp.dma_start(zl[:,j,0:NL+ID],zt[g*2+j,:,0:NL+ID]).then_inc(loaded[j],16)
                    sp.dma_start(zl[:,j,NL+ID:],zt[g*2+j,:,Z_KI:Z_KI+ID]).then_inc(loaded[j],16)
        @block.tensor
        def _(pe):
            pe.sem_inc(turned,1)
            pe.wait_ge(made,3); pe.wait_ge(const_loaded,48)
            nc.tensor.transpose(ps[:,0,0:QK_+KK],grow[:],ident[0:QK_+KK,0:QK_+KK]).then_inc(gturned,1)
            pe.wait_ge(gready,1)
            with pe.Fori(0,TT//2) as g:
                for j in range(2):
                    pe.wait_ge(xn_ready,g*2+j+1+1); pe.wait_ge(act_ev,g*2+1); pe.wait_ge(dve_ev,g*2+1)
                    for k in range(NT):
                        src=xn[:,j,k*128:(k+1)*128] if k<NT-1 else zl[:,j,NL:]
                        t=nc.tensor.transpose(ps[:,4*j+k//4,(k%4)*128:(k%4)*128+128],src,ident[:])
                    t.then_inc(turned,1)
        @block.scalar
        def _(act):
            act.sem_inc(act_ev,1)
            act.sem_inc(rs_ready,1)
            act.wait_ge(made,3); act.wait_ge(gready,1)
            with act.Fori(0,TT//2) as g:
                for j in range(2):
                    act.wait_ge(loaded[j],g*32+32); act.wait_ge(rs_ready,g*2+1)
                    nc.scalar.activation(junk[:,j,0:QR],zl[:,j,0:QR],ACT.Square,scale=float(QR)**-0.5,accum_out=ss[:,j,0:1]).then_inc(ss_ready,1)
                    nc.scalar.activation(junk[:,j,QR:],zl[:,j,QR:NL],ACT.Square,scale=float(KR)**-0.5,accum_out=ss[:,j,1:2]).then_inc(ss_ready,1)
                    act.wait_ge(ss_ready,g*4+j*2+2)
                    nc.scalar.activation(ss[:,j],ss[:,j],ACT.Ln,bias=eps[:]).then_inc(ln_ready,1)
                    act.wait_ge(ln_ready,g*2+j+1); act.wait_ge(xn_ready,g*2+1)
                    nc.scalar.activation(rs[:,j],ss[:,j],ACT.Exp,scale=-0.5).then_inc(rs_ready,1)
                    act.wait_ge(turned,g*2+j+1+1)
                    for k in range(QK_):
                        t=nc.scalar.activation(cqT[:,k,bass.ds(g*256+j*128,128)],ps[:,4*j,k*128:k*128+128],ACT.Copy,scale=gcol[:,k:k+1])
                    t.then_inc(act_ev,1)
        @block.vector
        def _(dve):
            dve.sem_inc(dve_ev,1)
            dve.sem_inc(xn_ready,1)
            dve.wait_ge(gturned,1)
            nc.vector.tensor_copy(gcol[:],ps[:,0,0:QK_+KK]).then_inc(gready,1)
            dve.wait_ge(const_loaded,48)
            nc.vector.tensor_scalar(wi[:],wi[:],float(NIH)**-0.5*float(ID)**-0.5,None,ALU.mult).then_inc(wi_ready,1)
            dve.wait_ge(gready,1)
            with dve.Fori(0,TT//2) as g:
                for j in range(2):
                    dve.wait_ge(rs_ready,g*2+j+1+1); dve.wait_ge(turned,g*2+1); dve.wait_ge(loaded[j],g*32+32)
                    nc.vector.tensor_scalar(xn[:,j,0:QR],zl[:,j,0:QR],rs[:,j,0:1],None,ALU.mult)
                    nc.vector.tensor_scalar(xn[:,j,QR:],zl[:,j,QR:NL],rs[:,j,1:2],None,ALU.mult).then_inc(xn_ready,1)
                    dve.wait_ge(turned,g*2+j+1+1)
                    for k in range(KK):
                        nc.vector.tensor_scalar(ckvT[:,k,bass.ds(g*256+j*128,128)],ps[:,4*j+1,k*128:k*128+128],gcol[:,QK_+k:QK_+k+1],None,ALU.mult)
                    nc.vector.tensor_copy(kiT[:,bass.ds(g*256+j*128,128)],ps[:,4*j+1,KK*128:KK*128+128]).then_inc(dve_ev,1)
            dve.wait_ge(wi_ready,1)

def indexer(nc,w_qidx,cqT,kiT,wi,bias):
    RR=4
    CH=[[(c,min(512,WIDTH[b]-c)) for c in range(0,WIDTH[b],512)] for b in range(TT)]
    FB=TOPK//128
    BLOCKS=list(range(FB,TT))
    with ExitStack() as ctx:
        sb=lambda n,s,d=F32: ctx.enter_context(nc.sbuf_tensor("idx_"+n,s,d))
        sem=semaphores(nc,ctx,"idx")
        w=sb("w_qidx_sb",[128,QK_,NIH*ID]); qi=sb("q_idxT",[128,NIH//2,S]); relu=sb("relu",[128,RR,512]); isc=sb("isc",[128,S]); m8=sb("max8",[128,8]); cmask=sb("causal",[128,128])
        ps=ctx.enter_context(nc.psum_tensor("idx_ps",[128,8,512],F32))
        w_loaded=sem("w_loaded"); made=sem("made"); proj=sem("proj"); proj_copied=sem("proj_copied"); scored=sem("scored"); relu_ready=sem("relu_ready"); summed=sem("summed")
        seen=sem("causal_done"); found=sem("max8_found"); waited=sem("waited"); taken=sem("taken"); biased=sem("bias_written")
        NP_=NIH//2*(S//512)
        block=ctx.enter_context(nc.Block())
        @block.sync
        def _(sp):
            sp.dma_start(w[:],w_qidx.rearrange("l (k p) n -> p (l k) n",p=128)).then_inc(w_loaded,16)
            sp.wait_ge(w_loaded,16)
        @block.gpsimd
        def _(pool):
            pool.memset(cmask[:],0.0).then_inc(made,1)
            pool.wait_ge(made,1)
            pool.affine_select(out=cmask[:],in_=cmask[:],compare_op=ALU.is_ge,fill=UNSEEN,base=0,pattern=[[-1,128]],channel_multiplier=1).then_inc(made,1)
        @block.tensor
        def _(pe):
            pe.wait_ge(w_loaded,16)
            n=0
            for p in range(NIH//2):
                for c in range(S//512):
                    if n>=8: pe.wait_ge(proj_copied,n-7)
                    for k in range(QK_):
                        t=nc.tensor.matmul(ps[:,n%8],w[:,k,p*128:(p+1)*128],cqT[:,k,c*512:(c+1)*512],start=(k==0),stop=(k==QK_-1))
                    t.then_inc(proj,1); n+=1
            pe.wait_ge(proj_copied,NP_)
            n=0
            for b in BLOCKS:
                for c,wd in CH[b]:
                    for h in range(NIH):
                        if n>=8: pe.wait_ge(relu_ready,n-7)
                        r=(h%2)*ID
                        nc.tensor.matmul(ps[:,n%8,0:wd],qi[r:r+ID,h//2,b*128:(b+1)*128],kiT[r:r+ID,c:c+wd],start=True,stop=True).then_inc(scored,1)
                        n+=1
        @block.scalar
        def _(act):
            for n in range(NP_):
                act.wait_ge(proj,n+1)
                nc.scalar.copy(qi[:,n//(S//512),(n%(S//512))*512:(n%(S//512))*512+512],ps[:,n%8]).then_inc(proj_copied,1)
            n=0
            for b in BLOCKS:
                for c,wd in CH[b]:
                    for h in range(NIH):
                        act.wait_ge(scored,n+1)
                        if n>=RR: act.wait_ge(summed,n-RR+1)
                        nc.scalar.activation(relu[:,n%RR,0:wd],ps[:,n%8,0:wd],ACT.Relu).then_inc(relu_ready,1)
                        n+=1
        @block.vector
        def _(dve):
            dve.sem_inc(taken,1)
            dve.wait_ge(made,2)
            for b in range(FB):
                if b: nc.vector.memset(bias[:,MOFF[b]:MOFF[b]+b*128],0.0)
                nc.vector.tensor_copy(bias[:,MOFF[b]+b*128:MOFF[b]+WIDTH[b]],cmask[:]).then_inc(biased,1)
            n=0
            for i,b in enumerate(BLOCKS):
                if i: dve.wait_ge(biased,FB+i)
                for c,wd in CH[b]:
                    for h in range(NIH):
                        dve.wait_ge(relu_ready,n+1)
                        o=isc[:,c:c+wd]
                        if h==0: nc.vector.tensor_scalar(o,relu[:,n%RR,0:wd],wi[:,b,h:h+1],None,ALU.mult).then_inc(summed,1)
                        else:
                            dve.wait_ge(summed,n)
                            nc.vector.scalar_tensor_tensor(out=o,in0=relu[:,n%RR,0:wd],scalar=wi[:,b,h:h+1],in1=o,op0=ALU.mult,op1=ALU.add).then_inc(summed,1)
                        n+=1
                dve.wait_ge(summed,n)
                nc.vector.tensor_tensor(isc[:,b*128:WIDTH[b]],isc[:,b*128:WIDTH[b]],cmask[:],ALU.add).then_inc(seen,1)
                dve.wait_ge(seen,i+1)
                v=isc[:,0:WIDTH[b]]
                base=i*(TOPK//8)
                with dve.Fori(0,TOPK//8) as r:
                    dve.wait_ge(taken,r+(base+1)); dve.sem_inc(waited,1)
                    nc.vector.max(m8[:],v).then_inc(found,1)
                    dve.wait_ge(found,r+(base+1)); dve.sem_inc(waited,1)
                    nc.vector.match_replace(v,m8[:],v,TAKEN).then_inc(taken,1)
                dve.wait_ge(taken,base+TOPK//8+1)
                nc.vector.tensor_scalar(bias[:,MOFF[b]:MOFF[b]+WIDTH[b]],v,-2e38,UNSEEN,ALU.is_gt,ALU.mult).then_inc(biased,1)

def attention(nc,w_uq,w_uk,w_uv,cqT,ckvT,bias,ident,yt):
    SCALE=float(HD)**-0.5; HG=4; SR=3; TR=2
    CH=[[(c,min(512,WIDTH[b]-c)) for c in range(0,WIDTH[b],512)] for b in range(TT)]
    NCH=sum(len(c) for c in CH)
    C0=[sum(len(c) for c in CH[:b]) for b in range(TT)]
    TQ4=S//512
    with ExitStack() as ctx:
        sb=lambda n,s,d=F32: ctx.enter_context(nc.sbuf_tensor("att_"+n,s,d))
        sem=semaphores(nc,ctx,"att")
        wq=sb("w_uq_h",[128,2,QK_,HD]); wk=sb("w_uk_h",[128,2,KK,HD]); wv=sb("w_uv_g",[128,KK,HG*HD])
        qT=sb("qT",[128,S]); kT=sb("kT",[128,S]); V=sb("V",[128,TT,HG*HD]); Sc=sb("scores",[128,2,S]); PT=sb("probsT",[128,2,TT,128])
        cm=sb("chunk_max",[128,2,4]); nm=sb("neg_max",[128,2]); rsum=sb("row_sum",[128,2]); rinv=sb("row_inv",[128,2]); o=sb("o",[128,4,HD])
        ps=ctx.enter_context(nc.psum_tensor("att_ps",[128,8,512],F32)); PJ,OB=6,7
        wq_l=[sem(f"wqk_loaded{j}") for j in range(2)]; wv_l=sem("wv_loaded"); proj=sem("projected"); pcopy=sem("proj_copied"); v_ps=sem("v_in_psum"); v_copy=sem("v_copied")
        scored=sem("scored"); masked=sem("masked"); waited=sem("waited"); maxed=sem("maxed"); mx=sem("mx"); expd=sem("exp_done"); pturned=sem("probs_turned"); pt_act=sem("probsT_act"); pt_dve=sem("probsT_dve"); pv=sem("pv_done"); inv=sem("row_inv_ready"); o_ready=sem("o_ready"); stored=[sem(f"o_stored{j}") for j in range(4)]
        block=ctx.enter_context(nc.Block())
        wqv=w_uq.rearrange("l (k p) n -> p (l k) n",p=128); wkv=w_uk.rearrange("l (k p) h d -> p (l k) (h d)",p=128); wvv=w_uv.rearrange("l (k p) h d -> p (l k) (h d)",p=128)
        PC=2*TQ4
        G=[(b,t0,min(4,b+1-t0)) for b in range(TT) for t0 in range(0,b+1,4)]
        NG=len(G); G0=[sum(1 for g in G if g[0]<b) for b in range(TT)]
        def loops(eng,body):
            with eng.Fori(0,NAH//HG) as gg:
                for hh in range(HG): body(gg,hh)
        @block.sync
        def _(sp):
            for s in stored: sp.sem_inc(s,16)
            def body(gg,hh):
                j=hh%2
                if hh==0:
                    sp.wait_ge(v_ps,gg*TT+1)
                    sp.dma_start(wv[:],wvv[:,:,bass.ds(gg*(HG*HD),HG*HD)]).then_inc(wv_l,16)
                sp.wait_ge(proj,(gg*HG+hh)*PC+1)
                sp.dma_start(wq[:,j],wqv[:,:,bass.ds((gg*HG+hh)*HD,HD)]).then_inc(wq_l[j],16)
                sp.dma_start(wk[:,j],wkv[:,:,bass.ds((gg*HG+hh)*HD,HD)]).then_inc(wq_l[j],16)
                for b in range(TT):
                    sp.wait_ge(o_ready,(gg*HG+hh)*TT+(b+1)+1)
                    sp.dma_start(yt[b,:,bass.ds((gg*HG+hh)*HD,HD)],o[:,b%4]).then_inc(stored[b%4],16)
            loops(sp,body)
            for j in range(4): sp.wait_ge(stored[j],16*NAH*TT//4+16)
        @block.tensor
        def _(pe):
            pe.sem_inc(pturned,1)
            pe.sem_inc(proj,1)
            pe.sem_inc(scored,1)
            pe.sem_inc(v_ps,1)
            def body(gg,hh):
                H=gg*HG+hh; j=hh%2
                if hh==0:
                    pe.wait_ge(wv_l,gg*16+16)
                    pe.wait_ge(pv,gg*(HG*TT)+2)
                    for t in range(TT):
                        pe.wait_ge(v_copy,gg*TT+t+1)
                        pe.wait_ge(pcopy,gg*(HG*PC)+1)
                        for k in range(KK):
                            m=nc.tensor.matmul(ps[:,PJ],ckvT[:,k,t*128:(t+1)*128],wv[:,k],start=(k==0),stop=(k==KK-1))
                        m.then_inc(v_ps,1)
                    pe.wait_ge(v_copy,gg*TT+TT+1)
                pe.wait_ge(wq_l[j],(gg*(HG//2)+hh//2)*32+32)
                for n in range(PC):
                    pe.wait_ge(pcopy,H*PC+n+1)
                    s,c=(wq,n) if n<TQ4 else (wk,n-TQ4)
                    K_=QK_ if n<TQ4 else KK; src=cqT if n<TQ4 else ckvT
                    for k in range(K_):
                        m=nc.tensor.matmul(ps[:,PJ],s[:,j,k],src[:,k,c*512:(c+1)*512],start=(k==0),stop=(k==K_-1))
                    m.then_inc(proj,1)
                pe.wait_ge(pcopy,H*PC+PC+1)
                def scores(b):
                    for i,(c,wd) in enumerate(CH[b]):
                        pe.wait_ge(masked,H*NCH+(C0[b]+i+1))
                        nc.tensor.matmul(ps[:,(C0[b]+i)%4,0:wd],qT[:,b*128:(b+1)*128],kT[:,c:c+wd],start=True,stop=True).then_inc(scored,1)
                def out(b):
                    pe.wait_ge(expd,H*TT+b+1+1)
                    for gi in range(G0[b],G0[b]+len([1 for g in G if g[0]==b])):
                        _,t0,nt=G[gi]
                        pe.wait_ge((pt_act,pt_dve)[gi%2],H*(NG//2)+(gi//2+1))
                        for t in range(nt):
                            m=nc.tensor.transpose(ps[:,4+gi%2,t*128:(t+1)*128],Sc[:,b%2,(t0+t)*128:(t0+t+1)*128],ident[:])
                        m.then_inc(pturned,1)
                    pe.wait_ge(o_ready,H*TT+b+1)
                    for gi in range(G0[b],G0[b]+len([1 for g in G if g[0]==b])):
                        _,t0,nt=G[gi]
                        pe.wait_ge((pt_act,pt_dve)[gi%2],H*(NG//2)+(gi//2+2))
                        for t in range(nt):
                            m=nc.tensor.matmul(ps[:,OB,0:HD],PT[:,b%2,t0+t],V[:,t0+t,hh*HD:(hh+1)*HD],start=(t0+t==0),stop=(t0+t==b))
                    m.then_inc(pv,1)
                scores(0)
                for b in range(TT):
                    if b+1<TT: scores(b+1)
                    out(b)
            loops(pe,body)
        @block.scalar
        def _(act):
            act.sem_inc(expd,1)
            act.sem_inc(pt_act,1)
            def body(gg,hh):
                H=gg*HG+hh
                if hh==0:
                    for t in range(0,TT,2):
                        act.wait_ge(v_ps,gg*TT+t+1+1)
                        nc.scalar.copy(V[:,t],ps[:,PJ]).then_inc(v_copy,1)
                        act.wait_ge(v_copy,gg*TT+t+2+1)
                act.wait_ge(scored,H*NCH+1)
                for n in range(0,PC,2):
                    act.wait_ge(proj,H*PC+n+1+1)
                    dst=(qT,kT)[n//TQ4]
                    nc.scalar.copy(dst[:,(n%TQ4)*512:(n%TQ4)*512+512],ps[:,PJ]).then_inc(pcopy,1)
                    act.wait_ge(pcopy,H*PC+n+2+1)
                for b in range(TT):
                    act.wait_ge(maxed,(H*TT+b)+1); act.wait_ge(masked,H*NCH+(C0[b]+len(CH[b])+4)); act.wait_ge(inv,H*TT+(b+1))
                    nc.scalar.activation(Sc[:,b%2,0:WIDTH[b]],Sc[:,b%2,0:WIDTH[b]],ACT.Exp,bias=nm[:,b%2:b%2+1],scale=SCALE,accum_out=rsum[:,b%2:b%2+1]).then_inc(expd,1)
                    for gi,(bb,t0,nt) in enumerate(G):
                        if bb!=b or gi%2: continue
                        act.wait_ge(pturned,H*NG+gi+1+1); act.wait_ge(pv,H*TT+(b+1))
                        nc.scalar.copy(PT[:,b%2,t0:t0+nt].rearrange("p t n -> p (t n)"),ps[:,4,0:nt*128]).then_inc(pt_act,1)
            act.sem_inc(inv,2)
            act.sem_inc(pv,2)
            loops(act,body)
        @block.vector
        def _(dve):
            dve.sem_inc(o_ready,1)
            dve.sem_inc(pcopy,1)
            dve.sem_inc(v_copy,1)
            dve.sem_inc(pt_dve,1); dve.sem_inc(masked,4)
            def body(gg,hh):
                H=gg*HG+hh
                if hh==0:
                    for t in range(1,TT,2):
                        dve.wait_ge(v_ps,gg*TT+t+1+1)
                        nc.vector.tensor_copy(V[:,t],ps[:,PJ]).then_inc(v_copy,1)
                dve.wait_ge(scored,H*NCH+1)
                for n in range(1,PC,2):
                    dve.wait_ge(proj,H*PC+n+1+1)
                    dst=(qT,kT)[n//TQ4]
                    nc.vector.tensor_copy(dst[:,(n%TQ4)*512:(n%TQ4)*512+512],ps[:,PJ]).then_inc(pcopy,1)
                def mask(b):
                    dve.wait_ge(pturned,H*NG+(G0[b-1] if b else 0)+1); dve.wait_ge(expd,H*TT+b+1)
                    for i,(c,wd) in enumerate(CH[b]):
                        dve.wait_ge(scored,H*NCH+(C0[b]+i+1)+1); dve.sem_inc(waited,1)
                        nc.vector.tensor_tensor_reduce(Sc[:,b%2,c:c+wd],ps[:,(C0[b]+i)%4,0:wd],bias[:,MOFF[b]+c:MOFF[b]+c+wd],1.0,-3e38,ALU.add,ALU.max,cm[:,b%2,i:i+1]).then_inc(masked,1)
                    dve.wait_ge(masked,H*NCH+(C0[b]+len(CH[b])+4))
                    nc.vector.tensor_reduce(nm[:,b%2:b%2+1],cm[:,b%2,0:len(CH[b])],AX.X,ALU.max).then_inc(mx,1)
                    dve.wait_ge(mx,H*TT+b+1)
                    nc.vector.tensor_scalar(nm[:,b%2:b%2+1],nm[:,b%2:b%2+1],-SCALE,None,ALU.mult).then_inc(maxed,1)
                def rest(b):
                    for gi,(bb,t0,nt) in enumerate(G):
                        if bb!=b or gi%2==0: continue
                        dve.wait_ge(pturned,H*NG+gi+1+1); dve.wait_ge(pv,H*TT+(b+1))
                        nc.vector.tensor_copy(PT[:,b%2,t0:t0+nt].rearrange("p t n -> p (t n)"),ps[:,5,0:nt*128]).then_inc(pt_dve,1)
                    dve.wait_ge(expd,H*TT+b+1+1); dve.wait_ge(o_ready,H*TT+b+1)
                    nc.vector.reciprocal(rinv[:,b%2:b%2+1],rsum[:,b%2:b%2+1]).then_inc(inv,1)
                    dve.wait_ge(pv,H*TT+(b+3)); dve.wait_ge(inv,H*TT+(b+3)); dve.wait_ge(stored[b%4],(H*(TT//4)+b//4)*16+16)
                    nc.vector.tensor_scalar(o[:,b%4],ps[:,OB,0:HD],rinv[:,b%2:b%2+1],None,ALU.mult).then_inc(o_ready,1)
                mask(0)
                for b in range(TT):
                    if b+1<TT: mask(b+1)
                    rest(b)
            loops(dve,body)

NE=32; GRP=4; EPG=8; FF=512; MT=63; SLOTS_=(MT+1)*128
U32=mybir.dt.uint32; I32=mybir.dt.int32

def out_projection(nc, y, x, mod, w_out, norm_g, router_w, x1, h2, logits):
    yt=y.rearrange("(t p) d -> t p d",p=128); xt=x.rearrange("b (t p) d -> (b t) p d",p=128)
    x1t=x1.rearrange("(t p) d -> t p d",p=128); h2t=h2.rearrange("(t p) d -> t p d",p=128)
    row=lambda s: mod[:,s*D:(s+1)*D].to_broadcast([128,D])
    with ExitStack() as ctx:
        sb=lambda n,s,d=F32: ctx.enter_context(nc.sbuf_tensor("op_"+n,s,d))
        sem=semaphores(nc,ctx,"op")
        w=sb("w_out",[128,KD,D]); yb=sb("y",[128,2,D]); xb=sb("x",[128,2,D]); g1=sb("gate1",[128,D]); A2=sb("scale2",[128,D]); sh2=sb("shift2",[128,D])
        yT=sb("yT",[128,KD,128]); hT=sb("h2T",[128,KD,128]); rw=sb("router_w",[128,KD,NE]); ident=sb("ident",[128,128]); ss=sb("ss",[128,2]); eps=sb("eps",[128,1])
        ps=ctx.enter_context(nc.psum_tensor("op_ps",[128,8,512],F32)); YB,HB,LB=4,6,7
        w_loaded=sem("w_loaded"); rows_loaded=sem("rows_loaded"); made=sem("made"); in_loaded=[sem(f"in_loaded{j}") for j in range(2)]; A_ready=sem("A_ready")
        y_turned=sem("y_turned"); yT_ev=sem("yT_copied"); acc_ready=sem("acc_ready"); acc_used=sem("acc_used"); x1_ready=sem("x1_ready"); ss_ready=sem("ss_ready"); rs_ready=sem("rstd_ready"); hmul=sem("h2_scaled"); h2_ready=sem("h2_ready")
        h_turned=sem("h_turned"); hT_ev=sem("hT_copied"); lg_ready=sem("logits_ready"); lg_copied=sem("logits_copied"); x1_st=[sem(f"x1_stored{j}") for j in range(2)]; h2_st=[sem(f"h2_stored{j}") for j in range(2)]
        block=ctx.enter_context(nc.Block())
        def paired(eng,step):
            step(0,0,first=True)
            with eng.Fori(0,TT//2-1) as g:
                step(g*2+1,1); step(g*2+2,0)
            step(TT-1,1)
        half=lambda t,j: (t-j)//2 if isinstance(t,int) else None
        @block.gpsimd
        def _(pool):
            identity_tile(nc,pool,ident,made)
            pool.memset(eps[:],EPS).then_inc(made,1)
        @block.sync
        def _(sp):
            def load(t,j):
                sp.dma_start(yb[:,j],yt[t]).then_inc(in_loaded[j],16)
                sp.dma_start(xb[:,j],xt[t]).then_inc(in_loaded[j],16)
            load(0,0)
            wv=w_out.rearrange("l (k p) n -> p (l k) n",p=128)
            for n in range(4): sp.dma_start(w[:,:,n*512:(n+1)*512],wv[:,:,n*512:(n+1)*512]).then_inc(w_loaded,16)
            load(1,1)
            sp.dma_start(g1[:],row(2)).then_inc(rows_loaded,16); sp.dma_start(A2[:],row(4)).then_inc(rows_loaded,16); sp.dma_start(sh2[:],row(3)).then_inc(rows_loaded,16)
            sp.dma_start(hT[:].rearrange("p k n -> p (k n)"),norm_g.to_broadcast([128,D])).then_inc(rows_loaded,16)
            sp.dma_start(rw[:],router_w.rearrange("(k p) n -> p k n",p=128)).then_inc(rows_loaded,16)
            def store(t,j,u):
                sp.wait_ge(x1_ready,t*4+4)
                sp.dma_start(x1t[t],xb[:,j]).then_inc(x1_st[j],16)
                sp.wait_ge(h2_ready,t+1)
                sp.dma_start(h2t[t],yb[:,j]).then_inc(h2_st[j],16)
                sp.wait_ge(h_turned,t*4+4)
                sp.wait_ge(x1_st[j],u*16+16); sp.wait_ge(h2_st[j],u*16+16)
            with sp.Fori(0,TT//2-1) as g:
                for j in range(2):
                    store(g*2+j,j,g)
                    load(g*2+(j+2),j)
            for j in range(2): store(TT-2+j,j,TT//2-1)
        @block.tensor
        def _(pe):
            pe.sem_inc(lg_ready,1)
            pe.wait_ge(made,2)
            def y_turn(t,j):
                pe.wait_ge(in_loaded[j],(t-j)*16+32)
                for i in range(4):
                    pe.wait_ge(yT_ev,t*4+i)
                    for q in range(4):
                        m=nc.tensor.transpose(ps[:,YB+i%2,q*128:q*128+128],yb[:,j,(4*i+q)*128:(4*i+q+1)*128],ident[:])
                    m.then_inc(y_turned,1)
            def main(t,j):
                pe.wait_ge(yT_ev,t*4+5)
                for n in range(4):
                    if isinstance(t,int) and t==0: pe.wait_ge(w_loaded,64)
                    pe.wait_ge(acc_used,t*4+(n+1))
                    for k in range(KD):
                        m=nc.tensor.matmul(ps[:,n],yT[:,k],w[:,k,n*512:(n+1)*512],start=(k==0),stop=(k==KD-1))
                    m.then_inc(acc_ready,1)
            def router(t,j):
                pe.wait_ge(h2_ready,t+1)
                for i in range(4):
                    pe.wait_ge(hT_ev,t*4+i+1)
                    for q in range(4):
                        m=nc.tensor.transpose(ps[:,HB,q*128:q*128+128],yb[:,j,(4*i+q)*128:(4*i+q+1)*128],ident[:])
                    m.then_inc(h_turned,1)
                pe.wait_ge(hT_ev,t*4+4+1); pe.wait_ge(lg_copied,t+1); pe.wait_ge(rows_loaded,80)
                for k in range(KD):
                    m=nc.tensor.matmul(ps[:,LB,0:NE],hT[:,k],rw[:,k],start=(k==0),stop=(k==KD-1))
                m.then_inc(lg_ready,1)
            def step(t,j,first=False):
                y_turn(t,j)
                main(t,j)
                if not first: router(t-1,1-j)
            paired(pe,step)
            router(TT-1,1)
        @block.scalar
        def _(act):
            act.sem_inc(hT_ev,1)
            act.sem_inc(lg_copied,1)
            act.wait_ge(made,3)
            act.sem_inc(yT_ev,1)
            def y_copy(t,j):
                act.wait_ge(acc_ready,t*4)
                for i in range(4):
                    act.wait_ge(y_turned,t*4+(i+1))
                    nc.scalar.copy(yT[:,4*i:4*i+4].rearrange("p k n -> p (k n)"),ps[:,YB+i%2]).then_inc(yT_ev,1)
            def norm(t,j):
                act.wait_ge(x1_ready,t*4+4); act.wait_ge(hmul,t)
                nc.scalar.activation(yb[:,j],xb[:,j],ACT.Square,scale=float(D)**-0.5,accum_out=ss[:,j:j+1]).then_inc(ss_ready,1)
                act.wait_ge(ss_ready,t*2+1)
                nc.scalar.activation(ss[:,j:j+1],ss[:,j:j+1],ACT.Ln,bias=eps[:]).then_inc(ss_ready,1)
                act.wait_ge(ss_ready,t*2+2)
                nc.scalar.activation(ss[:,j:j+1],ss[:,j:j+1],ACT.Exp,scale=-0.5).then_inc(rs_ready,1)
            def h_copy(t,j):
                act.wait_ge(A_ready,1)
                act.wait_ge(lg_ready,t+1)
                for i in range(4):
                    act.wait_ge(h_turned,t*4+(i+1))
                    nc.scalar.copy(hT[:,4*i:4*i+4].rearrange("p k n -> p (k n)"),ps[:,HB]).then_inc(hT_ev,1)
                act.wait_ge(lg_ready,t+1+1)
                nc.scalar.copy(logits[:,bass.ds(t,1),:].rearrange("p o e -> p (o e)"),ps[:,LB,0:NE]).then_inc(lg_copied,1)
            def step(t,j,first=False):
                y_copy(t,j)
                if not first: h_copy(t-1,1-j)
                norm(t,j)
            paired(act,step)
            h_copy(TT-1,1)
        @block.vector
        def _(dve):
            dve.sem_inc(acc_used,4)
            dve.wait_ge(rows_loaded,80)
            nc.vector.scalar_tensor_tensor(out=A2[:],in0=A2[:],scalar=1.0,in1=hT[:].rearrange("p k n -> p (k n)"),op0=ALU.add,op1=ALU.mult).then_inc(A_ready,1)
            dve.wait_ge(A_ready,1)
            def step(t,j,first=False):
                dve.wait_ge(in_loaded[j],(t-j)*16+32); dve.wait_ge(y_turned,t*4+4)
                for n in range(4):
                    c=slice(n*512,(n+1)*512)
                    dve.wait_ge(acc_ready,t*4+(n+1))
                    nc.vector.tensor_tensor(yb[:,j,c],ps[:,n],g1[:,c],ALU.mult).then_inc(acc_used,1)
                    dve.wait_ge(acc_used,t*4+(n+5))
                    nc.vector.tensor_tensor(xb[:,j,c],xb[:,j,c],yb[:,j,c],ALU.add).then_inc(x1_ready,1)
                dve.wait_ge(rs_ready,t+1)
                nc.vector.scalar_tensor_tensor(out=yb[:,j],in0=xb[:,j],scalar=ss[:,j:j+1],in1=A2[:],op0=ALU.mult,op1=ALU.mult).then_inc(hmul,1)
                dve.wait_ge(hmul,t+1)
                nc.vector.tensor_tensor(yb[:,j],yb[:,j],sh2[:],ALU.add).then_inc(h2_ready,1)
            paired(dve,step)
            dve.wait_ge(lg_copied,TT+1)

MT_ALL=MT+1

def routing(nc, logits, router_b, token_of_slot, slots, gates, tile_expert, tiles_used):
    with ExitStack() as ctx:
        sb=lambda n,s,d=F32: ctx.enter_context(nc.sbuf_tensor("rt_"+n,s,d))
        sem=semaphores(nc,ctx,"rt")
        NG_=TT*GRP; E_=TT*NE
        rb=sb("router_b",[128,NE]); aff=sb("affinity",[128,TT,NE]); sel=sb("selection",[128,TT,NE])
        ie=sb("expert_iota_m8",[128,EPG]); ig=sb("group_iota_m4",[128,GRP]); tok=sb("token_ids",[128,TT],I32); tri=sb("before",[128,128]); ones=sb("ones",[128,128]); zeros=sb("zero_slots",[128,MT_ALL],I32)
        m=sb("best",[128,2,NG_]); i8=sb("first_index",[128,2,NG_]); t8=sb("tmp",[128,TT,NE]); oh=sb("onehot",[128,2,TT,NE]); M=sb("chosen",[128,TT,NE])
        gs=sb("group_score",[128,TT,GRP]); gb=sb("group_best",[128,TT]); gi=sb("group_index",[128,TT]); goh=sb("group_onehot",[128,TT,GRP])
        carry=sb("carry",[128,TT+1,NE]); mi=sb("multiples_of_128",[128,S//128]); cmp=sb("compare",[128,NE,S//128]); nt=sb("tiles_of_expert",[128,NE]); end=sb("end_tile",[128,NE]); one=sb("one_row",[128,NE]); base=sb("first_slot",[128,NE])
        ti=sb("tile_iota",[1,MT_ALL]); tc=sb("tile_compare",[1,MT_ALL,NE]); te=sb("tile_expert_f",[1,MT_ALL]); sf=sb("slots_f",[128,2,TT]); a12=sb("gates_raw",[128,2,TT]); asum=sb("gate_sum",[128,TT])
        ps=ctx.enter_context(nc.psum_tensor("rt_ps",[128,2,512],F32))
        made=sem("made"); rb_loaded=sem("rb_loaded"); zeroed=sem("zeroed"); ex=sem("exp_ready"); v=sem("vector_done"); ranked=sem("ranked"); chosen=sem("chosen"); slotted=sem("slotted"); scattered=sem("scattered")
        block=ctx.enter_context(nc.Block())
        v8=lambda t: t.rearrange("p t (g e) -> p (t g) e",g=GRP)
        up=lambda ap,n: ap.rearrange("p (n o) -> p n o",o=1).to_broadcast([128,ap.shape[1],n])
        lead=lambda ap,n: ap.rearrange("p (o n) -> p o n",o=1).to_broadcast([ap.shape[0],n,ap.shape[1]])
        @block.sync
        def _(sp):
            sp.dma_start(rb[:],router_b.rearrange("(o e) -> o e",o=1).to_broadcast([128,NE])).then_inc(rb_loaded,16)
            sp.wait_ge(made,9)
            sp.dma_start(token_of_slot.rearrange("(p t) o -> p (t o)",p=128),zeros[:]).then_inc(zeroed,16)
            sp.wait_ge(rb_loaded,16)
        @block.gpsimd
        def _(pool):
            ap=dict(allow_small_or_imprecise_dtypes=True)
            pool.iota(ie[:],pattern=[[1,EPG]],base=-EPG,channel_multiplier=0,**ap).then_inc(made,1)
            pool.iota(ig[:],pattern=[[1,GRP]],base=-GRP,channel_multiplier=0,**ap).then_inc(made,1)
            pool.iota(tok[:],pattern=[[128,TT]],base=0,channel_multiplier=1).then_inc(made,1)
            pool.iota(mi[:],pattern=[[128,S//128]],base=0,channel_multiplier=0,**ap).then_inc(made,1)
            pool.iota(ti[:],pattern=[[1,MT_ALL]],base=0,channel_multiplier=0,**ap).then_inc(made,1)
            pool.memset(ones[:],1.0).then_inc(made,1)
            pool.memset(tri[:],1.0).then_inc(made,1)
            pool.memset(one[:],1.0).then_inc(made,1)
            pool.memset(zeros[:],0).then_inc(made,1)
            pool.wait_ge(made,9)
            pool.affine_select(out=tri[:],in_=tri[:],compare_op=ALU.is_gt,fill=0.0,base=0,pattern=[[1,128]],channel_multiplier=-1).then_inc(made,1)
            pool.wait_ge(zeroed,16); pool.wait_ge(slotted,1)
            for q in range(2):
                for t in range(TT):
                    pool.indirect_dma_start(out=token_of_slot,out_offset=bass.IndirectOffsetOnAxis(ap=slots[:,q,t:t+1],axis=0),in_=tok[:,t:t+1],in_offset=None).then_inc(scattered,16)
            pool.wait_ge(scattered,32*TT)
        @block.scalar
        def _(act):
            nc.scalar.activation(aff[:].rearrange("p t e -> p (t e)"),logits[:].rearrange("p t e -> p (t e)"),ACT.Exp,scale=-1.0).then_inc(ex,1)
        @block.tensor
        def _(pe):
            pe.wait_ge(made,10); pe.wait_ge(chosen,1)
            r=M[:].rearrange("p t e -> p (t e)")
            nc.tensor.matmul(ps[:,0],tri[:],r,start=True,stop=True)
            nc.tensor.matmul(ps[:,1],ones[:],r,start=True,stop=True).then_inc(ranked,1)
        @block.vector
        def _(dve):
            n=[0]
            def then(ins):
                n[0]+=1
                ins.then_inc(v,1); dve.wait_ge(v,n[0])
            V=nc.vector
            dve.wait_ge(ex,1); dve.wait_ge(rb_loaded,16); dve.wait_ge(made,10)
            then(V.tensor_scalar(aff[:],aff[:],1.0,None,ALU.add))
            then(V.reciprocal(aff[:],aff[:]))
            then(V.tensor_tensor(sel[:],aff[:],lead(rb[:],TT),ALU.add))
            for q in range(2):
                then(V.tensor_reduce(m[:,q],v8(sel[:]),AX.X,ALU.max))
                then(V.tensor_tensor(v8(t8[:]),v8(sel[:]),up(m[:,q],EPG),ALU.is_equal))
                then(V.tensor_tensor(v8(t8[:]),v8(t8[:]),lead(ie[:],NG_),ALU.mult))
                then(V.tensor_reduce(i8[:,q],v8(t8[:]),AX.X,ALU.min))
                then(V.tensor_tensor(v8(oh[:,q]),lead(ie[:],NG_),up(i8[:,q],EPG),ALU.is_equal))
                if q==0: then(V.scalar_tensor_tensor(out=sel[:],in0=oh[:,0],scalar=-BIG,in1=sel[:],op0=ALU.mult,op1=ALU.add))
            then(V.tensor_tensor(gs[:].rearrange("p t g -> p (t g)"),m[:,0],m[:,1],ALU.add))
            then(V.tensor_reduce(gb[:],gs[:],AX.X,ALU.max))
            then(V.tensor_tensor(gs[:],gs[:],up(gb[:],GRP),ALU.is_equal))
            then(V.tensor_tensor(gs[:],gs[:],lead(ig[:],TT),ALU.mult))
            then(V.tensor_reduce(gi[:],gs[:],AX.X,ALU.min))
            then(V.tensor_tensor(goh[:],lead(ig[:],TT),up(gi[:],GRP),ALU.is_equal))
            gflat=goh[:].rearrange("p t g -> p (t g)")
            for q in range(2):
                then(V.tensor_tensor(v8(oh[:,q]),v8(oh[:,q]),up(gflat,EPG),ALU.mult))
                then(V.tensor_tensor(t8[:],oh[:,q],aff[:],ALU.mult))
                then(V.tensor_reduce(a12[:,q],t8[:],AX.X,ALU.add))
            then(V.tensor_tensor(asum[:],a12[:,0],a12[:,1],ALU.add))
            then(V.reciprocal(asum[:],asum[:]))
            for q in range(2): then(V.tensor_tensor(gates[:,q],a12[:,q],asum[:],ALU.mult))
            V.tensor_tensor(M[:],oh[:,0],oh[:,1],ALU.add).then_inc(chosen,1)
            dve.wait_ge(ranked,1)
            then(V.memset(carry[:,0],0.0))
            for t in range(TT):
                then(V.tensor_tensor(carry[:,t+1],carry[:,t],ps[:,1,t*NE:(t+1)*NE],ALU.add))
            then(V.tensor_tensor(cmp[:],up(carry[:,TT],S//128),lead(mi[:],NE),ALU.is_gt))
            then(V.tensor_reduce(nt[:],cmp[:],AX.X,ALU.add))
            then(V.tensor_tensor_scan(end[:],one[:],nt[:],0.0,ALU.mult,ALU.add))
            then(V.tensor_tensor(base[:],end[:],nt[:],ALU.subtract))
            then(V.tensor_scalar(base[:],base[:],128.0,None,ALU.mult))
            then(V.tensor_tensor(M[:],carry[:,0:TT],lead(base[:],TT),ALU.add))
            then(V.tensor_tensor(M[:].rearrange("p t e -> p (t e)"),M[:].rearrange("p t e -> p (t e)"),ps[:,0],ALU.add))
            for q in range(2):
                then(V.tensor_tensor(t8[:],oh[:,q],M[:],ALU.mult))
                then(V.tensor_reduce(sf[:,q],t8[:],AX.X,ALU.add))
            V.tensor_copy(slots[:],sf[:]).then_inc(slotted,1)
            ebc=end[0:1].rearrange("p (o e) -> p o e",o=1).to_broadcast([1,MT_ALL,NE]); tbc=ti[:].rearrange("p (t o) -> p t o",o=1).to_broadcast([1,MT_ALL,NE])
            then(V.tensor_tensor(tc[:],ebc,tbc,ALU.is_le))
            then(V.tensor_reduce(te[:],tc[:],AX.X,ALU.add))
            then(V.tensor_scalar(te[:],te[:],float(NE-1),None,ALU.min))
            then(V.tensor_copy(tile_expert[:],te[:]))
            then(V.tensor_copy(tiles_used[:,0:1],end[0:1,NE-1:NE]))
            then(V.tensor_scalar(tiles_used[:,1:2],end[0:1,NE-1:NE],-1.0,None,ALU.add))
            then(V.tensor_scalar(tiles_used[:,2:3],end[0:1,NE-1:NE],-1.0,float(MT_ALL),ALU.mult,ALU.add))

def experts(nc, h2, mod, w_gate_up, w_down, token_of_slot, tile_expert, tiles_used, ys):
    KF=FF//128; GC=8
    yst=ys.rearrange("(t p) d -> t p d",p=128)
    wgv=w_gate_up.rearrange("l e (k p) n -> p (l e k) n",p=128); wdv=w_down.rearrange("l e (k p) n -> p (l e k) n",p=128)
    with ExitStack() as ctx:
        sb=lambda n,s,d=F32: ctx.enter_context(nc.sbuf_tensor("ex_"+n,s,d))
        sem=semaphores(nc,ctx,"ex")
        wg=sb("w_gate_up",[128,KD,2*FF]); wd=sb("w_down",[128,KF,D]); xg=sb("x",[128,2,D]); xT=sb("xT",[128,2,KD,128]); g2=sb("gate2",[128,D]); idx=sb("token_idx",[128,MT_ALL],I32); ic=sb("tile_idx",[128,2],I32)
        sg=sb("sigmoid",[128,FF]); gu=sb("gate_sig",[128,FF]); a=sb("act",[128,FF]); aT=sb("actT",[128,KF,128]); yo=sb("y",[128,D]); zero=sb("zero",[128,512]); ident=sb("ident",[128,128])
        ps=ctx.enter_context(nc.psum_tensor("ex_ps",[128,8,512],F32)); GU,TR,DN=0,2,4
        made=sem("made"); rows=sem("rows_loaded"); wg_l=[sem(f"wg_loaded{i}") for i in range(GC)]; wd_l=[sem(f"wd_loaded{i}") for i in range(KF)]; wg_used=sem("wg_used"); wd_used=sem("wd_used")
        idx_ready=sem("idx_ready"); pool_waited=sem("pool_waited"); act_waited=sem("act_waited"); x_l=[sem(f"x_loaded{j}") for j in range(2)]; x_turned=sem("x_turned"); x_part=sem("x_part_turned"); xT_act=sem("xT_act"); xT_dve=sem("xT_dve"); gu_ready=sem("gu_ready"); sig=sem("sig_ready"); gated=sem("gated"); a_ready=sem("act_ready")
        a_turned=sem("act_turned"); aT_ready=sem("actT_ready"); dn_ready=sem("down_ready"); y_ready=sem("y_ready"); y_st=sem("y_stored"); zero_st=sem("zeros_stored")
        block=ctx.enter_context(nc.Block())
        def tiles(eng,step,last,reg):
            step(0,0,True)
            used=eng.value_load(tiles_used[0:1,0:1],min_val=1,max_val=MT)
            with eng.Fori(0,(MT-1)//2) as g:
                for j,d in ((1,1),(0,2)):
                    t=g*2+d
                    with eng.If(t<used): step(t,j,False)
            last(used,eng.value_load(tiles_used[0:1,1:2],min_val=0,max_val=MT-1))
        @block.sync
        def _(sp):
            sp.dma_start(idx[:],token_of_slot.rearrange("(t p) o -> p (t o)",p=128)).then_inc(rows,16) if False else None
            with nc.allow_non_contiguous_dma(reason="a slot's token is one word"):
                sp.dma_start(idx[:],token_of_slot.rearrange("(t p) o -> p (t o)",p=128)).then_inc(rows,16)
            sp.dma_start(g2[:],mod[:,5*D:6*D].to_broadcast([128,D])).then_inc(rows,16)
            def step(t,j,first):
                e=sp.value_load(tile_expert[0:1,bass.ds(t,1)],min_val=0,max_val=NE-1)
                def wdown():
                    for i in range(KF):
                        sp.wait_ge(wd_used,t*KF+(i+1))
                        sp.dma_start(wd[:,i],wdv[:,bass.ds(e*KF+i,1)].rearrange("p o n -> p (o n)")).then_inc(wd_l[i],16)
                for i in range(GC):
                    sp.wait_ge(wg_used,t*GC+(i+1))
                    sp.dma_start(wg[:,2*i:2*i+2],wgv[:,bass.ds(e*KD+2*i,2)]).then_inc(wg_l[i],16)
                wdown()
            tiles(sp,step,lambda used,final: None,None)
        @block.gpsimd
        def _(pool):
            identity_tile(nc,pool,ident,made)
            pool.wait_ge(rows,32)
            def gather(t,j,n):
                pool.tensor_copy(ic[:,j:j+1],idx[:,bass.ds(t,1)]).then_inc(idx_ready,1)
                pool.wait_ge(idx_ready,t+1); pool.sem_inc(pool_waited,1)
                pool.indirect_dma_start(out=xg[:,j],out_offset=None,in_=h2,in_offset=bass.IndirectOffsetOnAxis(ap=ic[:,j:j+1],axis=0)).then_inc(x_l[j],16)
            gather(0,0,0)
            pool.memset(zero[:],0.0).then_inc(made,1)
            pool.wait_ge(made,3)
            unused=pool.value_load(tiles_used[0:1,2:3],min_val=1,max_val=MT_ALL-1)
            with pool.Fori(0,MT_ALL-1) as u:
                with pool.If(u<unused):
                    pool.dma_start(yst[(MT_ALL-1)-u].rearrange("p (r n) -> p r n",n=512),zero[:].rearrange("p (o n) -> p o n",o=1).to_broadcast([128,4,512])).then_inc(zero_st,16)
            def step(t,j,first):
                pool.wait_ge(x_turned,t)
                gather(t+1,1-j,0)
            def last(used,_):
                pool.wait_ge(x_turned,used+1)
                pool.wait_ge(zero_st,unused*16); pool.sem_inc(pool_waited,1)
            tiles(pool,step,last,None)
        @block.tensor
        def _(pe):
            pe.wait_ge(made,2)
            pe.sem_inc(wg_used,GC); pe.sem_inc(wd_used,KF)
            def turn_x(t,j,n2):
                pe.wait_ge(x_l[j],n2)
                if not (isinstance(t,int) and t==0): pe.wait_ge(aT_ready,t-1)
                for i in range(4):
                    pe.wait_ge((xT_act,xT_dve)[i%2],t*2+(i//2+1))
                    for q in range(4):
                        m=nc.tensor.transpose(ps[:,TR+i%2,q*128:q*128+128],xg[:,j,(4*i+q)*128:(4*i+q+1)*128],ident[:])
                    if i<3: m.then_inc(x_part,1)
                    else: m.then_inc(x_turned,1)
            def gate_up(t,j):
                pe.wait_ge(xT_act,t*2+3); pe.wait_ge(xT_dve,t*2+3)
                pe.wait_ge(gated,t)
                pe.wait_ge(a_ready,t)
                for i in range(GC):
                    pe.wait_ge(wg_l[i],t*16+16)
                    for k in (2*i,2*i+1):
                        for n in range(2):
                            m=nc.tensor.matmul(ps[:,GU+n],xT[:,j,k],wg[:,k,n*512:(n+1)*512],start=(k==0),stop=(k==KD-1))
                    m.then_inc(wg_used,1)
            def turn_a(t):
                pe.wait_ge(a_ready,t+1)
                pe.wait_ge(xT_act,t*2+5)
                for k in range(KF):
                    m=nc.tensor.transpose(ps[:,TR,k*128:(k+1)*128],a[:,k*128:(k+1)*128],ident[:])
                m.then_inc(a_turned,1)
            def down(t):
                pe.wait_ge(aT_ready,t+1); pe.wait_ge(y_ready,t*4+4 if False else t*4+1)
                for k in range(KF):
                    pe.wait_ge(wd_l[k],t*16+16)
                    for n in range(4):
                        m=nc.tensor.matmul(ps[:,DN+n],aT[:,k],wd[:,k,n*512:(n+1)*512],start=(k==0),stop=(k==KF-1))
                        if n==3: m.then_inc(wd_used,1)
            def step(t,j,first):
                if first: turn_x(0,0,16)
                gate_up(t,j)
                n2=16 if first else (t+1-(1-j))*8+16
                turn_x(t+1,1-j,n2)
                if not first: down(t-1)
                turn_a(t)
            tiles(pe,step,lambda used,final: down(final),None)
        @block.scalar
        def _(act):
            act.sem_inc(y_st,16)
            act.sem_inc(xT_act,1)
            def copy_x(t,j,part):
                for i in (0,2):
                    if i==0: act.wait_ge(wg_used,t*GC); act.wait_ge(x_part,t*3+1)
                    else: act.wait_ge(x_part,t*3+3)
                    nc.scalar.copy(xT[:,j,4*i:4*i+4].rearrange("p k n -> p (k n)"),ps[:,TR]).then_inc(xT_act,1)
            def store(t):
                act.wait_ge(y_ready,t*4+4+1)
                act.dma_start(yst[t],yo[:]).then_inc(y_st,16)
            def step(t,j,first):
                if first: copy_x(0,0,0)
                act.wait_ge(wg_used,t*GC+2*GC); act.wait_ge(gated,t)
                nc.scalar.activation(sg[:],ps[:,GU],ACT.Sigmoid).then_inc(sig,1)
                copy_x(t+1,1-j,0)
                act.wait_ge(a_turned,t+1); act.wait_ge(wd_used,t*KF+KF)
                nc.scalar.copy(aT[:].rearrange("p k n -> p (k n)"),ps[:,TR]).then_inc(aT_ready,1)
                if not first: store(t-1)
            def last(used,final):
                store(final)
                act.wait_ge(y_st,used*16+16); act.sem_inc(act_waited,1)
            tiles(act,step,last,None)
        @block.vector
        def _(dve):
            dve.sem_inc(y_ready,1)
            dve.sem_inc(xT_dve,1)
            dve.wait_ge(rows,32)
            def copy_x(t,j):
                for i in (1,3):
                    if i==1: dve.wait_ge(x_part,t*3+2); dve.wait_ge(wg_used,t*GC)
                    else: dve.wait_ge(x_turned,t+1)
                    nc.vector.tensor_copy(xT[:,j,4*i:4*i+4].rearrange("p k n -> p (k n)"),ps[:,TR+1]).then_inc(xT_dve,1)
            def y_out(t):
                dve.wait_ge(wd_used,t*KF+2*KF); dve.wait_ge(y_st,t*16+16)
                for n in range(4):
                    nc.vector.tensor_tensor(yo[:,n*512:(n+1)*512],ps[:,DN+n],g2[:,n*512:(n+1)*512],ALU.mult).then_inc(y_ready,1)
            def step(t,j,first):
                if first: copy_x(0,0)
                dve.wait_ge(sig,t+1)
                nc.vector.tensor_tensor(gu[:],ps[:,GU],sg[:],ALU.mult).then_inc(gated,1)
                dve.wait_ge(gated,t+1); dve.wait_ge(a_turned,t)
                nc.vector.tensor_tensor(a[:],ps[:,GU+1],gu[:],ALU.mult).then_inc(a_ready,1)
                copy_x(t+1,1-j)
                if not first: y_out(t-1)
            tiles(dve,step,lambda used,final: y_out(final),None)
    
def combine(nc, x1, ys, slots, gates, final_g, out):
    x1t=x1.rearrange("(t p) d -> t p d",p=128); ot=out.rearrange("b (t p) d -> (b t) p d",p=128)
    NB=2
    with ExitStack() as ctx:
        sb=lambda n,s,d=F32: ctx.enter_context(nc.sbuf_tensor("co_"+n,s,d))
        sem=semaphores(nc,ctx,"co")
        xb=sb("x",[128,NB,D]); y1=sb("y1",[128,NB,D]); y2=sb("y2",[128,NB,D]); g=sb("final_g",[128,D]); ic=sb("slot_idx",[128,2,NB],I32); ss=sb("ss",[128,NB]); eps=sb("eps",[128,1])
        g_l=sem("g_loaded"); made=sem("made"); x_l=[sem(f"x_loaded{j}") for j in range(NB)]; y_l=[sem(f"y_loaded{j}") for j in range(NB)]
        y1s=sem("y1_scaled"); ysum=sem("y_sum"); xs=sem("x_sum"); sse=sem("ss_steps"); done=sem("out_ready"); st=[sem(f"stored{j}") for j in range(NB)]
        block=ctx.enter_context(nc.Block())
        def loop(eng,f):
            with eng.Fori(0,TT//NB) as q:
                for j in range(NB): f(q,q*NB+j,j)
        @block.sync
        def _(sp):
            sp.dma_start(g[:],final_g.rearrange("(o d) -> o d",o=1).to_broadcast([128,D])).then_inc(g_l,16)
            for j in range(NB): sp.dma_start(xb[:,j],x1t[j]).then_inc(x_l[j],16)
            def store(t,j):
                sp.wait_ge(done,t+1)
                sp.dma_start(ot[t],y1[:,j]).then_inc(st[j],16)
            with sp.Fori(0,TT//NB-1) as q:
                for j in range(NB):
                    store(q*NB+j,j)
                    sp.dma_start(xb[:,j],x1t[q*NB+(j+NB)]).then_inc(x_l[j],16)
            for j in range(NB): store(TT-NB+j,j)
            for j in range(NB): sp.wait_ge(st[j],16*TT//NB)
        @block.gpsimd
        def _(pool):
            pool.memset(eps[:],EPS).then_inc(made,1)
            def f(q,t,j):
                pool.wait_ge(st[j],q*16); 
                pool.indirect_dma_start(out=y1[:,j],out_offset=None,in_=ys,in_offset=bass.IndirectOffsetOnAxis(ap=slots[:,0,t:t+1],axis=0)).then_inc(y_l[j],16)
                pool.indirect_dma_start(out=y2[:,j],out_offset=None,in_=ys,in_offset=bass.IndirectOffsetOnAxis(ap=slots[:,1,t:t+1],axis=0)).then_inc(y_l[j],16)
            for t in range(TT): f(t//NB,t,t%NB)
        @block.scalar
        def _(act):
            act.wait_ge(made,1)
            def f(q,t,j):
                act.wait_ge(y_l[j],q*32+32)
                nc.scalar.activation(y1[:,j],y1[:,j],ACT.Copy,scale=gates[:,0,bass.ds(t,1)]).then_inc(y1s,1)
                act.wait_ge(xs,t+1)
                nc.scalar.activation(y2[:,j],xb[:,j],ACT.Square,scale=float(D)**-0.5,accum_out=ss[:,j:j+1]).then_inc(sse,1)
                act.wait_ge(sse,t*3+1)
                nc.scalar.activation(ss[:,j:j+1],ss[:,j:j+1],ACT.Ln,bias=eps[:]).then_inc(sse,1)
                act.wait_ge(sse,t*3+2)
                nc.scalar.activation(ss[:,j:j+1],ss[:,j:j+1],ACT.Exp,scale=-0.5).then_inc(sse,1)
            loop(act,f)
        @block.vector
        def _(dve):
            dve.wait_ge(g_l,16)
            def f(q,t,j):
                dve.wait_ge(y1s,t+1)
                nc.vector.scalar_tensor_tensor(out=y1[:,j],in0=y2[:,j],scalar=gates[:,1,bass.ds(t,1)],in1=y1[:,j],op0=ALU.mult,op1=ALU.add).then_inc(ysum,1)
                dve.wait_ge(ysum,t+1); dve.wait_ge(x_l[j],q*16+16)
                nc.vector.tensor_tensor(xb[:,j],xb[:,j],y1[:,j],ALU.add).then_inc(xs,1)
                dve.wait_ge(sse,t*3+3)
                nc.vector.scalar_tensor_tensor(out=y1[:,j],in0=xb[:,j],scalar=ss[:,j:j+1],in1=g[:],op0=ALU.mult,op1=ALU.mult).then_inc(done,1)
            loop(dve,f)

def hybrid_layer(nc, x, c, ada_w, ada_b, mix_norm_g, w_in, cq_norm_g, ckv_norm_g, w_uq, w_uk, w_uv, w_qidx,
                 mlstm_i_b, mlstm_f_b, mlstm_norm_g, w_out, ffn_norm_g, router_w, router_b, w_gate_up, w_down,
                 final_norm_g, out):
    scratch = lambda name, shape, dtype=F32: nc.dram_tensor(name, shape, dtype).ap()
    mod = scratch("mod", [1, 6 * D])
    z = scratch("z", [S, D_IN])
    y = scratch("y", [S, D])
    x1 = scratch("x1", [S, D])
    h2 = scratch("h2", [S, D])
    token_of_slot = scratch("token_of_slot", [SLOTS_, 1], I32)
    ys = scratch("ys", [SLOTS_, D])
    modulation(nc, c, ada_w, ada_b, mod)
    in_projection(nc, x, mod, mix_norm_g, w_in, z)
    mlstm(nc, z, mlstm_i_b, mlstm_f_b, mlstm_norm_g, y)
    dsa(nc, z, cq_norm_g, ckv_norm_g, w_uq, w_uk, w_uv, w_qidx, y)
    with ExitStack() as ctx:
        sb = lambda n, s, d=F32: ctx.enter_context(nc.sbuf_tensor(n, s, d))
        logits = sb("logits", [128, TT, NE])
        slots = sb("slots", [128, 2, TT], I32)
        gates = sb("gates", [128, 2, TT])
        tile_expert = sb("tile_expert", [1, MT_ALL], I32)
        tiles_used = sb("tiles_used", [1, 3], I32)
        out_projection(nc, y, x, mod, w_out, ffn_norm_g, router_w, x1, h2, logits)
        routing(nc, logits, router_b, token_of_slot, slots, gates, tile_expert, tiles_used)
        experts(nc, h2, mod, w_gate_up, w_down, token_of_slot, tile_expert, tiles_used, ys)
        combine(nc, x1, ys, slots, gates, final_norm_g, out)


_INS = ["x", "c", "ada_w", "ada_b", "mix_norm_g", "w_in", "cq_norm_g", "ckv_norm_g", "w_uq", "w_uk", "w_uv", "w_qidx",
        "mlstm_i_b", "mlstm_f_b", "mlstm_norm_g", "w_out", "ffn_norm_g", "router_w", "router_b", "w_gate_up", "w_down",
        "final_norm_g"]
_OUTS = [((1, S, D), "float32")]


def kernel(**inputs):
    import numpy as _np
    import concourse.bacc as _bacc
    from concourse import mybir as _mybir
    from concourse.bass_utils import run_bass_kernel_spmd as _run

    nc = _bacc.Bacc("TRN2", target_bir_lowering=False, num_devices=1)
    arrays, args = {}, []
    for name in _INS:
        a = _np.ascontiguousarray(inputs[name])
        arrays[f"in_{name}_dram"] = a
        args.append(nc.dram_tensor(f"in_{name}_dram", a.shape, _mybir.dt.from_np(a.dtype), kind="ExternalInput").ap())
    for i, (shape, dtype) in enumerate(_OUTS):
        dt = _mybir.dt.from_np(_np.dtype(dtype))
        args.append(nc.dram_tensor(f"out_{i}_dram", shape, dt, kind="ExternalOutput").ap())
    hybrid_layer(nc, *args)
    r = _run(nc, [arrays], core_ids=[0])
    got = tuple(r.results[0][f"out_{i}_dram"] for i in range(len(_OUTS)))
    return got[0]
```

```python
from contextlib import ExitStack

import concourse.bass as bass
from concourse import mybir
F32=mybir.dt.float32
ALU=mybir.AluOpType; ACT=mybir.ActivationFunctionType; AX=mybir.AxisListType
D=2048; KD=16

def semaphores(nc, ctx, stage):
    held = []

    def close():
        nc.clear_and_free_semaphores(held)
        nc.all_engine_barrier()

    def sem(name):
        held.append(nc.alloc_semaphore(f"{stage}_{name}"))
        return held[-1]

    ctx.callback(close)
    return sem

def modulation(nc, c, ada_w, ada_b, mod):
    N=512; NB=6*D//N; SLOTS=3
    w_view=ada_w.rearrange("l (p k) n -> p (l k) n",k=KD)
    with ExitStack() as ctx:
        sb=lambda n,s,d=F32: ctx.enter_context(nc.sbuf_tensor("mod_"+n,s,d))
        sem=semaphores(nc,ctx,"mod")
        c_col=sb("c_col",[128,KD]); e_col=sb("e_col",[128,KD]); s_col=sb("s_col",[128,KD])
        w=sb("ada_w_ring",[128,SLOTS,KD,N]); row=sb("mod_row",[1,6*D])
        acc=ctx.enter_context(nc.psum_tensor("mod_mod_acc",[128,SLOTS,512],F32))
        c_loaded=sem("c_loaded"); b_loaded=sem("b_loaded"); w_loaded=[sem(f"w_loaded{i}") for i in range(SLOTS)]
        w_used=sem("w_used"); acc_free=sem("acc_free"); c_exp=sem("c_exp"); c_step=sem("c_step"); mod_stored=sem("mod_stored")
        block=ctx.enter_context(nc.Block())
        @block.sync
        def _(sp):
            sp.dma_start(c_col[:],c.rearrange("b (p k) -> p (b k)",k=KD)).then_inc(c_loaded,16)
            sp.dma_start(row[:],ada_b).then_inc(b_loaded,16)
            for j in range(SLOTS):
                sp.dma_start(w[:,j],w_view[:,:,j*N:(j+1)*N]).then_inc(w_loaded[j],16)
            with sp.Fori(1,NB//SLOTS) as g:
                for j in range(SLOTS):
                    sp.wait_ge(w_used,g*SLOTS+(j-SLOTS+1))
                    sp.dma_start(w[:,j],w_view[:,:,bass.ds(g*(SLOTS*N)+j*N,N)]).then_inc(w_loaded[j],16)
            sp.wait_ge(acc_free,NB+SLOTS)
            sp.dma_start(mod,row[:]).then_inc(mod_stored,16)
            sp.wait_ge(mod_stored,16)
        @block.scalar
        def _(act):
            act.wait_ge(c_loaded,16)
            nc.scalar.activation(e_col[:],c_col[:],ACT.Exp,scale=-1.0).then_inc(c_exp,1)
        @block.vector
        def _(dve):
            dve.wait_ge(c_exp,1)
            nc.vector.tensor_scalar_add(e_col[:],e_col[:],1.0).then_inc(c_step,1)
            dve.wait_ge(c_step,1)
            nc.vector.reciprocal(e_col[:],e_col[:]).then_inc(c_step,1)
            dve.wait_ge(c_step,2)
            nc.vector.tensor_tensor(s_col[:],e_col[:],c_col[:],ALU.mult).then_inc(c_step,1)
            dve.wait_ge(b_loaded,16)
            dve.sem_inc(acc_free,SLOTS)
            with dve.Fori(0,NB//SLOTS) as g:
                for j in range(SLOTS):
                    dve.wait_ge(w_used,g*SLOTS+(j+1))
                    nc.vector.tensor_tensor(row[:,bass.ds(g*(SLOTS*N)+j*N,N)],acc[0:1,j],row[:,bass.ds(g*(SLOTS*N)+j*N,N)],ALU.add).then_inc(acc_free,1)
        @block.tensor
        def _(pe):
            pe.wait_ge(c_step,3)
            with pe.Fori(0,NB//SLOTS) as g:
                for j in range(SLOTS):
                    pe.wait_ge(w_loaded[j],g*16+16)
                    pe.wait_ge(acc_free,g*SLOTS+(j+1))
                    for k in range(KD):
                        mm=nc.tensor.matmul(acc[0:1,j],s_col[:,k:k+1],w[:,j,k],start=(k==0),stop=(k==KD-1))
                    mm.then_inc(w_used,1)

S=2048; TT=S//128
D_IN=3920; ZN=420; ZB=2; ZA=ZN*ZB
ZN2=440; ZB2=(D_IN-ZA)//ZN2
EPS=1e-6

def identity_tile(nc, pool, ident, made):
    pool.memset(ident[:],0.0).then_inc(made,1)
    pool.wait_ge(made,1)
    pool.affine_select(out=ident[:],in_=ident[:],compare_op=ALU.not_equal,fill=1.0,base=0,pattern=[[-1,128]],channel_multiplier=1).then_inc(made,1)

def in_projection(nc, x, mod, norm_g, w_in, z, h_tiles):
    xt=x.rearrange("b (t p) d -> (b t) p d",p=128)
    zt=z.rearrange("(t p) n -> t p n",p=128)
    wv=w_in.rearrange("l (k p) n -> p (l k) n",p=128)
    modv=mod.rearrange("l (s k p) -> s (l k) p",s=6,p=128)
    with ExitStack() as ctx:
        sb=lambda n,s,d=F32: ctx.enter_context(nc.sbuf_tensor("in_"+n,s,d))
        sem=semaphores(nc,ctx,"in")
        hT=sb("hT",[128,KD,S]); w=sb("w_in_ring",[128,2,KD,ZN])
        ident=sb("ident",[128,128]); rows=sb("param_rows",[3*KD,128]); cols=sb("param_cols",[128,3*KD])
        xb=w[:,1].rearrange("p k n -> p (k n)")[:,0:2*D].rearrange("p (s d) -> p s d",s=2)
        stage=sb("z_stage",[128,4,ZN]); ss=sb("sum_squares",[128,2]); rstd=sb("rstd",[128,2]); eps=sb("eps",[128,1])
        squares_out=stage[:].rearrange("p s n -> p (s n)")[:,0:D//2].bitcast(mybir.dt.bfloat16)
        FREE=4
        acc=ctx.enter_context(nc.psum_tensor("in_acc",[128,8,512],F32))
        xn=xb
        params_loaded=sem("params_loaded"); ident_made=sem("ident_made"); params_turned=sem("params_turned"); params_ready=sem("params_ready")
        x_loaded=[sem(f"x_loaded{i}") for i in range(2)]; ss_ready=sem("ss_ready"); rms_ready=sem("rms_ready"); rstd_ready=sem("rstd_ready")
        xn_ready=sem("xn_ready"); turned=sem("turned"); hT_act=sem("hT_act"); hT_dve=sem("hT_dve")
        w_loaded=[sem(f"w_loaded{i}") for i in range(2)]; z_acc=sem("z_acc"); h_stored=sem("h_stored")
        z_act=sem("z_act"); z_dve=sem("z_dve"); stored=[sem(f"z_stored{i}") for i in range(4)]
        block=ctx.enter_context(nc.Block())
        HK=KD//2
        @block.gpsimd
        def _(pool):
            identity_tile(nc,pool,ident,ident_made)
            pool.memset(eps[:],EPS).then_inc(ident_made,1)
        @block.sync
        def _(sp):
            for s in stored: sp.sem_inc(s,16)
            sp.dma_start(rows[0:KD],norm_g.rearrange("l (k p) -> (l k) p",p=128)).then_inc(params_loaded,16)
            sp.dma_start(rows[KD:2*KD],modv[1]).then_inc(params_loaded,16)
            sp.dma_start(rows[2*KD:3*KD],modv[0]).then_inc(params_loaded,16)
            with sp.Fori(0,TT//2) as g:
                for j in range(2):
                    sp.wait_ge(turned,g*2+(j)+1)
                    sp.dma_start(xb[:,j],xt[g*2+j]).then_inc(x_loaded[j],16)
            for n in range(ZB):
                for m in range(TT):
                    sp.wait_ge((z_act,z_dve)[m%2],n*(TT//2)+(m//2+1+FREE))
                    sp.dma_start(zt[m,:,n*ZN:(n+1)*ZN],stage[:,m%4]).then_inc(stored[m%4],16)
                    if n==0: sp.dma_start(h_tiles[m],hT[:,:,m*128:(m+1)*128]).then_inc(h_stored,16)
            sp.wait_ge(h_stored,16*TT)
            for s in range(4): sp.wait_ge(stored[s],16*ZB*TT//4+16)
        @block.scalar
        def _(act):
            act.sem_inc(hT_act,1)
            act.dma_start(w[:,0],wv[:,:,0:ZN]).then_inc(w_loaded[0],16)
            act.wait_ge(ident_made,3)
            def squares(t,j):
                act.wait_ge(x_loaded[j],t*16+16)
                nc.scalar.activation(squares_out,xb[:,j],ACT.Square,accum_out=ss[:,j:j+1]).then_inc(ss_ready,1)
            def root(t2,j):
                act.wait_ge(ss_ready,t2*2+j+1)
                nc.scalar.activation(rstd[:,j:j+1],ss[:,j:j+1],ACT.Sqrt,bias=eps[:],scale=1.0/D).then_inc(rms_ready,1)
            def evac(t2,j):
                act.wait_ge(turned,t2*2+j+1+1)
                for k in range(HK):
                    i=nc.scalar.activation(hT[:,k,bass.ds(t2*256+j*128,128)],acc[:,4*j+k//4,(k%4)*128:(k%4)*128+128],ACT.Identity,scale=cols[:,k:k+1],bias=cols[:,2*KD+k:2*KD+k+1])
                i.then_inc(hT_act,1)
            act.wait_ge(params_ready,2)
            with act.Fori(0,TT//2) as g:
                for j in range(2):
                    squares(g,j); root(g,j); evac(g,j)
            act.wait_ge(turned,TT+1)
            act.dma_start(w[:,1],wv[:,:,ZN:2*ZN]).then_inc(w_loaded[1],16)
            act.sem_inc(z_act,FREE)
            def z_evac(n2,j):
                for m in range(0,TT,2):
                    act.wait_ge(z_acc,n2*(2*TT)+j*TT+m+1)
                    act.wait_ge(stored[m%4],n2*(16*TT//2)+16*(j*TT//4+m//4)+16)
                    nc.scalar.copy(stage[:,m%4],acc[:,m%8,0:ZN]).then_inc(z_act,1)
            for j in range(2): z_evac(0,j)
        @block.vector
        def _(dve):
            dve.sem_inc(hT_dve,1)
            dve.wait_ge(params_turned,1)
            nc.vector.tensor_copy(cols[:],acc[:,0,0:3*KD]).then_inc(params_ready,1)
            dve.wait_ge(params_ready,1)
            nc.vector.scalar_tensor_tensor(out=cols[:,0:KD],in0=cols[:,KD:2*KD],scalar=1.0,in1=cols[:,0:KD],op0=ALU.add,op1=ALU.mult).then_inc(params_ready,1)
            dve.wait_ge(params_ready,2)
            with dve.Fori(0,TT//2) as g:
                for j in range(2):
                    dve.wait_ge(rms_ready,g*2+j+1)
                    nc.vector.reciprocal(rstd[:,j:j+1],rstd[:,j:j+1]).then_inc(rstd_ready,1)
                    dve.wait_ge(rstd_ready,g*2+j+1)
                    nc.vector.tensor_scalar(xn[:,j],xb[:,j],rstd[:,j:j+1],None,ALU.mult).then_inc(xn_ready,1)
                    dve.wait_ge(turned,g*2+j+1+1)
                    for k in range(HK,KD):
                        i=nc.vector.tensor_scalar(hT[:,k,bass.ds(g*256+j*128,128)],acc[:,4*j+k//4,(k%4)*128:(k%4)*128+128],cols[:,k:k+1],cols[:,2*KD+k:2*KD+k+1],ALU.mult,ALU.add)
                    i.then_inc(hT_dve,1)
            dve.sem_inc(z_dve,FREE)
            with dve.Fori(0,ZB) as n:
                for m in range(1,TT,2):
                    dve.wait_ge(z_acc,n*TT+m+1)
                    dve.wait_ge(stored[m%4],n*(16*TT//4)+16*(m//4)+16)
                    nc.vector.tensor_copy(stage[:,m%4],acc[:,m%8,0:ZN]).then_inc(z_dve,1)
        @block.tensor
        def _(pe):
            pe.sem_inc(turned,1)
            pe.wait_ge(ident_made,2); pe.wait_ge(params_loaded,48)
            nc.tensor.transpose(acc[:,0,0:3*KD],rows[:],ident[0:3*KD,0:3*KD]).then_inc(params_turned,1)
            pe.wait_ge(params_ready,1)
            with pe.Fori(0,TT//2) as g:
                for j in range(2):
                    pe.wait_ge(xn_ready,g*2+j+1)
                    pe.wait_ge(hT_act,g*2+1); pe.wait_ge(hT_dve,g*2+1)
                    for k in range(KD):
                        t=nc.tensor.transpose(acc[:,4*j+k//4,(k%4)*128:(k%4)*128+128],xn[:,j,k*128:(k+1)*128],ident[:])
                    t.then_inc(turned,1)
            pe.wait_ge(hT_act,TT+1); pe.wait_ge(hT_dve,TT+1)
            for j in range(ZB):
                pe.wait_ge(w_loaded[j],16)
                for m in range(TT):
                    pe.wait_ge((z_act,z_dve)[m%2],j*(TT//2)+m//2+1)
                    for k in range(KD):
                        mm=nc.tensor.matmul(acc[:,m%8,0:ZN],hT[:,k,m*128:(m+1)*128],w[:,j,k],start=(k==0),stop=(k==KD-1))
                    mm.then_inc(z_acc,1)

NH=4; DK=128; DV=256; DVA=DV+1; C=128; NC=S//C
Z_CQ,Z_CKV,Z_KI,Z_WI,Z_MQ,Z_MK,Z_MV,Z_MO,Z_MI,Z_MF=0,512,768,832,840,1352,1864,2888,3912,3916
BIG=1e30

def mlstm(nc, z, i_b, f_b, norm_g, y):
    zt=z.rearrange("(t p) n -> p t n",p=128)
    zc=z.rearrange("(t p) n -> t p n",p=128)
    yc=y.rearrange("(t p) n -> t p n",p=128)
    with ExitStack() as ctx:
        sb=lambda n,s,d=F32: ctx.enter_context(nc.sbuf_tensor("ml_"+n,s,d))
        sem=semaphores(nc,ctx,"ml")
        ident=sb("ident",[128,128]); sel=sb("head_rows",[NH,NH,128]); mask=sb("future_mask",[128,128])
        A=sb("A",[NH,S]); gcols=sb("gate_cols",[128,4,NC,NH]); wold=sb("wold",[128,NH,NC])
        gbc=sb("norm_g_rows",[128,NH*DV])
        with ExitStack() as gctx:
            gsb=lambda n,s,d=F32: gctx.enter_context(nc.sbuf_tensor("mlg_"+n,s,d))
            gsem=semaphores(nc,gctx,"mlg")
            zg=gsb("gates_in",[128,NC,8]); bias=gsb("gate_bias",[NH,2]); I=gsb("I",[NH,S]); Fg=gsb("F",[NH,S]); E=gsb("E",[NH,S]); L=gsb("L",[NH,S])
            b=gsb("b",[NH,S]); reset=gsb("reset",[NH,S]); step=gsb("step",[NH,S]); a=gsb("a",[NH,S]); Mp=gsb("m_prev",[NH,NC]); Wo=gsb("w_old",[NH,NC])
            win=gsb("w_inter",[NH,S]); en=gsb("exp_neg_m",[NH,S]); ws=gsb("w_s",[NH,S])
            ps=gctx.enter_context(nc.psum_tensor("ml_gates_ps",[128,8,512],F32))
            loaded=gsem("gates_loaded"); made=gsem("consts_made"); turned=gsem("gates_turned"); biased=gsem("gates_biased"); absd=gsem("abs_ready"); ln1p=gsem("ln_ready")
            v=gsem("vector_done"); expd=gsem("exp_ready"); cols_ps=gsem("cols_in_psum"); cdone=gsem("cols_copied")
            block=gctx.enter_context(nc.Block())
            ch=lambda t: t[:].rearrange("h (c j) -> h c j",j=C)
            @block.sync
            def _(sp):
                with nc.allow_non_contiguous_dma(reason="short rows of gates"):
                    sp.dma_start(zg[:],zt[:,:,Z_MI:Z_MI+8]).then_inc(loaded,16)
                    sp.dma_start(bias[:,0:1],i_b.rearrange("l h -> h l")).then_inc(loaded,16)
                    sp.dma_start(bias[:,1:2],f_b.rearrange("l h -> h l")).then_inc(loaded,16)
                sp.dma_start(gbc[:],norm_g.rearrange("l h v -> l (h v)").to_broadcast([128,NH*DV])).then_inc(loaded,16)
                sp.wait_ge(loaded,64)
            @block.gpsimd
            def _(pool):
                identity_tile(nc,pool,ident,made)
                pool.memset(mask[:],0.0).then_inc(made,1)
                pool.memset(sel[:],1.0).then_inc(made,1)
                pool.wait_ge(made,4)
                pool.affine_select(out=mask[:],in_=mask[:],compare_op=ALU.is_ge,fill=BIG,base=0,pattern=[[1,128]],channel_multiplier=-1).then_inc(made,1)
                pool.affine_select(out=sel[:],in_=sel[:],compare_op=ALU.is_equal,fill=0.0,base=0,pattern=[[-1,NH],[0,128]],channel_multiplier=1).then_inc(made,1)
                pool.memset(reset[:],1.0).then_inc(made,1)
                pool.memset(step[:],0.0).then_inc(made,1)
                pool.memset(Mp[:],0.0).then_inc(made,1)
                pool.wait_ge(made,7)
                pool.memset(ch(reset)[:,:,0:1],0.0).then_inc(made,1)
            @block.tensor
            def _(pe):
                pe.wait_ge(loaded,64); pe.wait_ge(made,10)
                for c in range(NC):
                    nc.tensor.transpose(ps[0:NH,c//4,(c%4)*128:(c%4)*128+128],zg[:,c,0:4],ident[:])
                    t=nc.tensor.transpose(ps[0:NH,4+c//4,(c%4)*128:(c%4)*128+128],zg[:,c,4:8],ident[:])
                t.then_inc(turned,1)
                pe.wait_ge(expd,4); 
                for q,r in enumerate((a,win,en,ws)):
                    for c in range(NC):
                        nc.tensor.transpose(ps[:,0,(q*NC+c)*NH:(q*NC+c+1)*NH],r[:,c*C:(c+1)*C],ident[0:NH,0:NH])
                for h in range(NH):
                    t=nc.tensor.matmul(ps[:,1,h*NC:(h+1)*NC],sel[:,h],Wo[:],start=True,stop=True)
                t.then_inc(cols_ps,1)
            @block.scalar
            def _(act):
                act.wait_ge(loaded,64); act.wait_ge(turned,1)
                nc.scalar.activation(I[:],ps[0:NH,0:4].rearrange("h b n -> h (b n)"),ACT.Identity,bias=bias[:,0:1]).then_inc(biased,1)
                nc.scalar.activation(Fg[:],ps[0:NH,4:8].rearrange("h b n -> h (b n)"),ACT.Identity,bias=bias[:,1:2]).then_inc(biased,1)
                act.wait_ge(biased,2)
                nc.scalar.activation(E[:],Fg[:],ACT.Abs).then_inc(absd,1)
                act.wait_ge(absd,1)
                nc.scalar.activation(E[:],E[:],ACT.Exp,scale=-1.0).then_inc(ln1p,1)
                act.wait_ge(ln1p,1)
                nc.scalar.activation(L[:],E[:],ACT.Ln,bias=1.0).then_inc(ln1p,1)
                act.wait_ge(v,9)
                nc.scalar.activation(win[:],win[:],ACT.Exp).then_inc(expd,1)
                act.wait_ge(v,10)
                nc.scalar.activation(en[:],en[:],ACT.Exp,scale=-1.0).then_inc(expd,1)
                act.wait_ge(v,11)
                nc.scalar.activation(ws[:],ws[:],ACT.Exp).then_inc(expd,1)
                act.wait_ge(v,12)
                nc.scalar.activation(Wo[:],Wo[:],ACT.Exp).then_inc(expd,1)
            @block.vector
            def _(dve):
                dve.wait_ge(ln1p,2); dve.wait_ge(made,10)
                nc.vector.scalar_tensor_tensor(out=L[:],in0=Fg[:],scalar=0.0,in1=L[:],op0=ALU.min,op1=ALU.subtract).then_inc(v,1)
                dve.wait_ge(v,1)
                nc.vector.tensor_tensor_scan(b[:],reset[:],L[:],0.0,ALU.mult,ALU.add).then_inc(v,1)
                dve.wait_ge(v,2)
                nc.vector.tensor_tensor(a[:],I[:],b[:],ALU.subtract).then_inc(v,1)
                nc.vector.tensor_copy(ch(step)[:,1:NC,0:1],ch(b)[:,0:NC-1,C-1:C]).then_inc(v,1)
                dve.wait_ge(v,4)
                nc.vector.tensor_tensor_scan(A[:],step[:],a[:],0.0,ALU.add,ALU.max).then_inc(v,1)
                dve.wait_ge(v,5)
                nc.vector.tensor_tensor(Mp[:,1:NC],ch(b)[:,0:NC-1,C-1],ch(A)[:,0:NC-1,C-1],ALU.add).then_inc(v,1)
                nc.vector.tensor_copy(Wo[:],ch(A)[:,:,C-1]).then_inc(v,1)
                dve.wait_ge(v,7)
                nc.vector.tensor_copy(reset[:,0:1],b[:,0:1]).then_inc(v,1)
                nc.vector.tensor_tensor(ch(win),Mp[:].broadcast(2,C) if False else Mp[:].rearrange("h (c o) -> h c o",o=1).to_broadcast([NH,NC,C]),ch(A),ALU.subtract).then_inc(v,1)
                nc.vector.tensor_tensor(en[:],b[:],A[:],ALU.add).then_inc(v,1)
                nc.vector.tensor_tensor(ch(ws),ch(a),Wo[:].rearrange("h (c o) -> h c o",o=1).to_broadcast([NH,NC,C]),ALU.subtract).then_inc(v,1)
                dve.wait_ge(v,11)
                nc.vector.tensor_tensor(Wo[:],Mp[:],Wo[:],ALU.subtract).then_inc(v,1)
                dve.wait_ge(cols_ps,1)
                nc.vector.tensor_copy(gcols[:].rearrange("p q c h -> p (q c h)"),ps[:,0,0:4*NC*NH]).then_inc(cdone,1)
                nc.vector.tensor_copy(wold[:].rearrange("p h c -> p (h c)"),ps[:,1,0:NH*NC]).then_inc(cdone,1)
                dve.wait_ge(cdone,2)
        zq=sb("zq",[128,2,2*NH*DK]); va=sb("va",[128,2,NH,DVA]); zo=sb("zo",[128,2,NH*DV])
        qT=sb("qT",[128,NH,C]); kT=sb("kT",[128,NH,C]); kw=sb("kw",[128,NH,DK]); Dm=sb("Dm",[128,NH,C]); Ex=sb("Ex",[128,NH,C]); W=sb("W",[128,NH,C])
        Cst=sb("C_state",[128,NH,DVA]); intra=sb("intra",[128,NH,DVA]); num=sb("num",[128,NH,DVA]); hn=sb("hn",[128,NH,DV])
        den=sb("den",[128,NH]); ss=sb("ss",[128,NH]); f=sb("f",[128,NH]); sg=sb("sg",[128,NH*DV]); yo=sb("yo",[128,2,NH*DV]); eps=sb("eps",[128,1])
        ps=ctx.enter_context(nc.psum_tensor("ml_ps",[128,8,512],F32)); TQ,TK,AB,SC,OUT=0,1,2,3,4
        z_loaded=[sem(f"z_loaded{j}") for j in range(2)]; init=sem("state_zeroed"); sp_waited=sem("sp_waited")
        qk_turned=sem("qk_turned"); a_wide=sem("a_wide"); q_ready=sem("q_ready"); k_ready=sem("k_ready"); scores=sem("scores"); D_ready=sem("D_ready"); E_ready=sem("E_ready")
        W_ready=sem("W_ready"); kw_ready=sem("kw_ready"); out_ready=sem("out_ready"); intra_copied=sem("intra_copied"); inter_used=sem("inter_used"); state_used=sem("state_used")
        sg_exp=sem("sg_exp"); r_ready=sem("r_ready"); ss_ready=sem("ss_ready"); rs_ready=sem("rs_ready"); dchain=sem("dchain"); f_ready=sem("f_ready"); den_abs=sem("den_abs"); y_ready=sem("y_ready"); y_stored=[sem(f"y_stored{j}") for j in range(2)]
        block=ctx.enter_context(nc.Block())
        @block.sync
        def _(sp):
            for s in y_stored: sp.sem_inc(s,16)
            def load(c,j):
                sp.dma_start(zq[:,j],zc[c,:,Z_MQ:Z_MV]).then_inc(z_loaded[j],16)
                sp.dma_start(va[:,j,:,0:DV],zc[c,:,Z_MV:Z_MO].rearrange("p (h v) -> p h v",h=NH)).then_inc(z_loaded[j],16)
                sp.dma_start(zo[:,j],zc[c,:,Z_MO:Z_MI]).then_inc(z_loaded[j],16)
            for j in range(2): load(j,j)
            with sp.Fori(0,NC//2-1) as g:
                for j in range(2):
                    sp.wait_ge(y_ready,g*2+j+1+1)
                    sp.sem_inc(sp_waited,1)
                    load(g*2+j+2,j)
                    sp.dma_start(yc[g*2+j,:,1024:2048],yo[:,j]).then_inc(y_stored[j],16)
            for j in range(2):
                sp.wait_ge(y_ready,NC-1+j+1)
                sp.dma_start(yc[NC-2+j,:,1024:2048],yo[:,j]).then_inc(y_stored[j],16)
            for j in range(2): sp.wait_ge(y_stored[j],16*NC//2+16)
        @block.gpsimd
        def _(pool):
            pool.memset(Cst[:],0.0).then_inc(init,1)
            pool.memset(va[:,:,:,DV:DVA],1.0).then_inc(init,1)
            pool.memset(eps[:],EPS).then_inc(init,1)
        order=[(h,kind) for h in range(NH) for kind in range(3)]
        done_of=(intra_copied,inter_used,state_used)
        @block.tensor
        def _(pe):
            pe.sem_inc(out_ready,1)
            pe.sem_inc(scores,1)
            pe.wait_ge(init,3)
            with pe.Fori(0,NC//2) as g:
                for j in range(2):
                    pe.wait_ge(z_loaded[j],g*48+48)
                    pe.wait_ge(k_ready,g*2+j+1); pe.wait_ge(q_ready,g*2+j+1)
                    for h in range(NH):
                        nc.tensor.transpose(ps[:,TQ,h*128:h*128+128],zq[:,j,h*128:h*128+128],ident[:])
                        t=nc.tensor.transpose(ps[:,TK,h*128:h*128+128],zq[:,j,NH*DK+h*128:NH*DK+h*128+128],ident[:])
                    t.then_inc(qk_turned,1)
                    pe.wait_ge(D_ready,g*2+j+1)
                    for h in range(NH):
                        t=nc.tensor.matmul(ps[:,AB,h*128:h*128+128],sel[:,h],A[:,bass.ds(g*(2*C)+j*C,C)],start=True,stop=True)
                    t.then_inc(a_wide,1)
                    pe.wait_ge(k_ready,g*2+j+1+1); pe.wait_ge(q_ready,g*2+j+1+1); pe.wait_ge(W_ready,g*2+j+1)
                    for h in range(NH):
                        t=nc.tensor.matmul(ps[:,SC,h*128:h*128+128],kT[:,h],qT[:,h],start=True,stop=True)
                    t.then_inc(scores,1)
                    pe.wait_ge(state_used,g*8+j*4+4); pe.wait_ge(W_ready,g*2+j+1+1); pe.wait_ge(kw_ready,g*2+j+1)
                    for n,(h,kind) in enumerate(order):
                        ph,pk=order[(n-4)%12]
                        pe.wait_ge(done_of[pk],g*8+(j*4+ph+1+(4 if n>=4 else 0)))
                        lhs,rhs=((W[:,h],va[:,j,h]),(qT[:,h],Cst[:,h]),(kw[:,h],va[:,j,h]))[kind]
                        nc.tensor.matmul(ps[:,OUT+n%4,0:DVA],lhs,rhs,start=True,stop=True).then_inc(out_ready,1)
        @block.scalar
        def _(act):
            act.sem_inc(E_ready,1)
            act.sem_inc(q_ready,1)
            act.wait_ge(init,3)
            act.sem_inc(intra_copied,4)
            with act.Fori(0,NC//2) as g:
                for j in range(2):
                    col=lambda q,h: gcols[:,q,bass.ds(g*2+j,1),h]
                    act.wait_ge(qk_turned,g*2+j+1)
                    act.wait_ge(out_ready,g*24+12*j+1)
                    nc.scalar.activation(qT[:].rearrange("p h c -> p (h c)"),ps[:,TQ],ACT.Copy,scale=float(DK)**-0.5).then_inc(q_ready,1)
                    act.wait_ge(z_loaded[j],g*48+48)
                    for h in range(NH):
                        t=nc.scalar.activation(kw[:,h],zq[:,j,NH*DK+h*128:NH*DK+h*128+128],ACT.Copy,scale=col(3,h))
                    t.then_inc(kw_ready,1)
                    act.wait_ge(D_ready,g*2+j+1+1); act.wait_ge(W_ready,g*2+j+1)
                    for h in range(NH):
                        t=nc.scalar.activation(Ex[:,h],Dm[:,h],ACT.Exp,scale=-1.0,bias=col(0,h))
                    t.then_inc(E_ready,1)
                    act.wait_ge(y_ready,g*2+j+1)
                    nc.scalar.activation(sg[:],zo[:,j],ACT.Exp,scale=-1.0).then_inc(sg_exp,1)
                    for h in range(NH):
                        act.wait_ge(out_ready,g*24+(12*j+3*h+1)+1); act.wait_ge(inter_used,g*8+(j*4+h+1))
                        nc.scalar.copy(intra[:,h],ps[:,OUT+(3*h)%4,0:DVA]).then_inc(intra_copied,1)
                    act.wait_ge(inter_used,g*8+(j*4+8)); act.wait_ge(f_ready,g*4+j*2+1)
                    nc.scalar.activation(den[:],num[:,:,DV],ACT.Abs).then_inc(den_abs,1)
                    act.wait_ge(r_ready,g*2+j+1)
                    for h in range(NH):
                        t=nc.scalar.activation(hn[:,h],num[:,h,0:DV],ACT.Square,scale=den[:,h:h+1],accum_out=ss[:,h:h+1])
                        t.then_inc(ss_ready,1)
                    act.wait_ge(ss_ready,g*8+j*4+4)
                    nc.scalar.activation(ss[:],ss[:],ACT.Ln,scale=1.0/DV,bias=eps[:]).then_inc(rs_ready,1)
                    act.wait_ge(rs_ready,g*4+j*2+1)
                    nc.scalar.activation(ss[:],ss[:],ACT.Exp,scale=-0.5).then_inc(rs_ready,1)
        @block.vector
        def _(dve):
            dve.sem_inc(D_ready,1)
            dve.sem_inc(W_ready,1)
            dve.sem_inc(f_ready,1)
            dve.sem_inc(k_ready,1)
            dve.sem_inc(y_ready,1)
            dve.wait_ge(init,3)
            dve.sem_inc(inter_used,4); dve.sem_inc(state_used,4)
            with dve.Fori(0,NC//2) as g:
                for j in range(2):
                    col=lambda q,h: gcols[:,q,bass.ds(g*2+j,1),h]
                    dve.wait_ge(qk_turned,g*2+j+1)
                    dve.wait_ge(scores,g*2+j+1)
                    nc.vector.tensor_copy(kT[:].rearrange("p h c -> p (h c)"),ps[:,TK]).then_inc(k_ready,1)
                    dve.wait_ge(a_wide,g*2+j+1); dve.wait_ge(E_ready,g*2+j+1)
                    nc.vector.tensor_tensor(Dm[:],ps[:,AB].rearrange("p (h c) -> p h c",h=NH),mask[:].rearrange("p (o c) -> p o c",o=1).to_broadcast([128,NH,C]),ALU.add).then_inc(D_ready,1)
                    dve.wait_ge(scores,g*2+j+1+1); dve.wait_ge(E_ready,g*2+j+1+1)
                    dve.wait_ge(out_ready,g*24+12*j+1)
                    nc.vector.tensor_tensor(W[:].rearrange("p h c -> p (h c)"),ps[:,SC],Ex[:].rearrange("p h c -> p (h c)"),ALU.mult).then_inc(W_ready,1)
                    dve.wait_ge(sg_exp,g*2+j+1)
                    nc.vector.tensor_scalar(sg[:],sg[:],1.0,None,ALU.add).then_inc(dchain,1)
                    dve.wait_ge(dchain,g*6+j*3+1)
                    nc.vector.reciprocal(sg[:],sg[:]).then_inc(dchain,1)
                    dve.wait_ge(dchain,g*6+j*3+2)
                    nc.vector.tensor_tensor(sg[:],sg[:],gbc[:],ALU.mult).then_inc(dchain,1)
                    for h in range(NH):
                        n=3*h+1
                        dve.wait_ge(out_ready,g*24+(12*j+n+1)+1); dve.wait_ge(intra_copied,g*8+(j*4+h+1+4))
                        nc.vector.scalar_tensor_tensor(out=num[:,h],in0=ps[:,OUT+n%4,0:DVA],scalar=col(1,h),in1=intra[:,h],op0=ALU.mult,op1=ALU.add).then_inc(inter_used,1)
                        dve.wait_ge(out_ready,g*24+(12*j+n+2)+1)
                        nc.vector.scalar_tensor_tensor(out=Cst[:,h],in0=Cst[:,h],scalar=wold[:,h,bass.ds(g*2+j,1)],in1=ps[:,OUT+(n+1)%4,0:DVA],op0=ALU.mult,op1=ALU.add).then_inc(state_used,1)
                    dve.wait_ge(den_abs,g*2+j+1)
                    nc.vector.tensor_tensor(den[:],den[:],gcols[:,2,bass.ds(g*2+j,1),:].rearrange("p o h -> p (o h)"),ALU.max).then_inc(f_ready,1)
                    dve.wait_ge(f_ready,g*4+j*2+1+1)
                    nc.vector.reciprocal(den[:],den[:]).then_inc(r_ready,1)
                    dve.wait_ge(rs_ready,g*4+j*2+2); dve.wait_ge(r_ready,g*2+j+1)
                    nc.vector.tensor_tensor(f[:],den[:],ss[:],ALU.mult).then_inc(f_ready,1)
                    dve.wait_ge(f_ready,g*4+j*2+2+1); dve.wait_ge(y_stored[j],g*16+16)
                    for h in range(NH):
                        t=nc.vector.scalar_tensor_tensor(out=yo[:,j,h*DV:(h+1)*DV],in0=num[:,h,0:DV],scalar=f[:,h:h+1],in1=sg[:,h*DV:(h+1)*DV],op0=ALU.mult,op1=ALU.mult)
                    t.then_inc(y_ready,1)

QR=512; KR=256; NIH=8; ID=64; TOPK=256; NAH=8; HD=128
BF=mybir.dt.bfloat16
QK_=QR//128; KK=KR//128
WIDTH=[(b+1)*128 for b in range(TT)]
MOFF=[sum(WIDTH[:b]) for b in range(TT)]; MTOT=sum(WIDTH)
TAKEN=-3e38; UNSEEN=-1e30

def dsa(nc, z, h_tiles, w_in, cq_g, ckv_g, w_uq, w_uk, w_uv, w_qidx, y):
    zt=z.rearrange("(t p) n -> t p n",p=128)
    yt=y.rearrange("(t p) n -> t p n",p=128)
    with ExitStack() as ctx:
        sb=lambda n,s,d=F32: ctx.enter_context(nc.sbuf_tensor("dsa_"+n,s,d))
        cqT=sb("cqT",[128,QK_,S]); ckvT=sb("ckvT",[128,KK,S]); bias=sb("select_bias",[128,MTOT],BF); ident=sb("ident",[128,128])
        with ExitStack() as ictx:
            kiT=ictx.enter_context(nc.sbuf_tensor("kiT",[128,S],F32)); wi=ictx.enter_context(nc.sbuf_tensor("w_idx",[128,TT,NIH],F32))
            latents(nc,zt,z,cq_g,ckv_g,cqT,ckvT,kiT,wi,ident)
            indexer(nc,w_qidx,cqT,kiT,wi,bias,h_tiles,w_in,zt)
        attention(nc,w_uq,w_uk,w_uv,cqT,ckvT,bias,ident,yt)

def latents(nc,zt,z,cq_g,ckv_g,cqT,ckvT,kiT,wi,ident):
    NL=QR+KR; NT=QK_+KK+1
    with ExitStack() as ctx:
        sb=lambda n,s,d=F32: ctx.enter_context(nc.sbuf_tensor("lat_"+n,s,d))
        sem=semaphores(nc,ctx,"lat")
        zl=sb("z_latents",[128,2,NL+2*ID]); xn=sb("latents_normed",[128,2,NL]); junk=sb("squares",[128,2,NL]); ss=sb("ss",[128,2,2]); rs=sb("rs",[128,2,2]); eps=sb("eps",[128,1])
        grow=sb("gain_rows",[QK_+KK,128]); gcol=sb("gain_cols",[128,QK_+KK])
        ps=ctx.enter_context(nc.psum_tensor("lat_ps",[128,8,512],F32))
        loaded=[sem(f"loaded{j}") for j in range(2)]; const_loaded=sem("const_loaded"); made=sem("made"); gturned=sem("gains_turned"); gready=sem("gains_ready"); wi_ready=sem("wi_ready")
        ss_ready=sem("ss_ready"); ln_ready=sem("ln_ready"); rs_ready=sem("rs_ready"); xn_ready=sem("xn_ready"); turned=sem("turned"); act_ev=sem("act_evacuated"); dve_ev=sem("dve_evacuated")
        block=ctx.enter_context(nc.Block())
        @block.gpsimd
        def _(pool):
            identity_tile(nc,pool,ident,made)
            pool.memset(eps[:],EPS).then_inc(made,1)
        @block.sync
        def _(sp):
            sp.dma_start(grow[0:QK_],cq_g.rearrange("l (k p) -> (l k) p",p=128)).then_inc(const_loaded,16)
            sp.dma_start(grow[QK_:],ckv_g.rearrange("l (k p) -> (l k) p",p=128)).then_inc(const_loaded,16)
            with nc.allow_non_contiguous_dma(reason="short rows"):
                sp.dma_start(wi[:],z.rearrange("(t p) n -> p t n",p=128)[:,:,Z_WI:Z_WI+NIH]).then_inc(const_loaded,16)
            with sp.Fori(0,TT//2) as g:
                for j in range(2):
                    sp.wait_ge(turned,g*2+j+1)
                    sp.dma_start(zl[:,j,0:NL+ID],zt[g*2+j,:,0:NL+ID]).then_inc(loaded[j],16)
                    sp.dma_start(zl[:,j,NL+ID:],zt[g*2+j,:,Z_KI:Z_KI+ID]).then_inc(loaded[j],16)
        @block.tensor
        def _(pe):
            pe.sem_inc(turned,1)
            pe.wait_ge(made,3); pe.wait_ge(const_loaded,48)
            nc.tensor.transpose(ps[:,0,0:QK_+KK],grow[:],ident[0:QK_+KK,0:QK_+KK]).then_inc(gturned,1)
            pe.wait_ge(gready,1)
            with pe.Fori(0,TT//2) as g:
                for j in range(2):
                    pe.wait_ge(xn_ready,g*2+j+1+1); pe.wait_ge(act_ev,g*2+1); pe.wait_ge(dve_ev,g*2+1)
                    for k in range(NT):
                        src=xn[:,j,k*128:(k+1)*128] if k<NT-1 else zl[:,j,NL:]
                        t=nc.tensor.transpose(ps[:,4*j+k//4,(k%4)*128:(k%4)*128+128],src,ident[:])
                    t.then_inc(turned,1)
        @block.scalar
        def _(act):
            act.sem_inc(act_ev,1)
            act.sem_inc(rs_ready,1)
            act.wait_ge(made,3); act.wait_ge(gready,1)
            with act.Fori(0,TT//2) as g:
                for j in range(2):
                    act.wait_ge(loaded[j],g*32+32); act.wait_ge(rs_ready,g*2+1)
                    nc.scalar.activation(junk[:,j,0:QR],zl[:,j,0:QR],ACT.Square,scale=float(QR)**-0.5,accum_out=ss[:,j,0:1]).then_inc(ss_ready,1)
                    nc.scalar.activation(junk[:,j,QR:],zl[:,j,QR:NL],ACT.Square,scale=float(KR)**-0.5,accum_out=ss[:,j,1:2]).then_inc(ss_ready,1)
                    act.wait_ge(ss_ready,g*4+j*2+2)
                    nc.scalar.activation(ss[:,j],ss[:,j],ACT.Ln,bias=eps[:]).then_inc(ln_ready,1)
                    act.wait_ge(ln_ready,g*2+j+1); act.wait_ge(xn_ready,g*2+1)
                    nc.scalar.activation(rs[:,j],ss[:,j],ACT.Exp,scale=-0.5).then_inc(rs_ready,1)
                    act.wait_ge(turned,g*2+j+1+1)
                    for k in range(QK_):
                        t=nc.scalar.activation(cqT[:,k,bass.ds(g*256+j*128,128)],ps[:,4*j,k*128:k*128+128],ACT.Copy,scale=gcol[:,k:k+1])
                    t.then_inc(act_ev,1)
        @block.vector
        def _(dve):
            dve.sem_inc(dve_ev,1)
            dve.sem_inc(xn_ready,1)
            dve.wait_ge(gturned,1)
            nc.vector.tensor_copy(gcol[:],ps[:,0,0:QK_+KK]).then_inc(gready,1)
            dve.wait_ge(const_loaded,48)
            nc.vector.tensor_scalar(wi[:],wi[:],float(NIH)**-0.5*float(ID)**-0.5,None,ALU.mult).then_inc(wi_ready,1)
            dve.wait_ge(gready,1)
            with dve.Fori(0,TT//2) as g:
                for j in range(2):
                    dve.wait_ge(rs_ready,g*2+j+1+1); dve.wait_ge(turned,g*2+1); dve.wait_ge(loaded[j],g*32+32)
                    nc.vector.tensor_scalar(xn[:,j,0:QR],zl[:,j,0:QR],rs[:,j,0:1],None,ALU.mult)
                    nc.vector.tensor_scalar(xn[:,j,QR:],zl[:,j,QR:NL],rs[:,j,1:2],None,ALU.mult).then_inc(xn_ready,1)
                    dve.wait_ge(turned,g*2+j+1+1)
                    for k in range(KK):
                        nc.vector.tensor_scalar(ckvT[:,k,bass.ds(g*256+j*128,128)],ps[:,4*j+1,k*128:k*128+128],gcol[:,QK_+k:QK_+k+1],None,ALU.mult)
                    nc.vector.tensor_copy(kiT[:,bass.ds(g*256+j*128,128)],ps[:,4*j+1,KK*128:KK*128+128]).then_inc(dve_ev,1)
            dve.wait_ge(wi_ready,1)

def indexer(nc,w_qidx,cqT,kiT,wi,bias,h_tiles,w_in,zt):
    RR=4
    CH=[[(c,min(512,WIDTH[b]-c)) for c in range(0,WIDTH[b],512)] for b in range(TT)]
    FB=TOPK//128
    BLOCKS=list(range(FB,TT))
    with ExitStack() as ctx:
        sb=lambda n,s,d=F32: ctx.enter_context(nc.sbuf_tensor("idx_"+n,s,d))
        sem=semaphores(nc,ctx,"idx")
        w=sb("w_qidx_sb",[128,QK_,NIH*ID]); qi=sb("q_idxT",[128,2,NIH//2*128]); relu=sb("relu",[128,RR,512]); isc=sb("isc",[128,S]); m8=sb("max8",[128,8]); cmask=sb("causal",[128,128])
        hT=sb("hT_tiles",[128,2,KD,128]); wz=sb("w_in_ring",[128,2,KD,ZN2]); stage=sb("z_stage",[128,2,ZN2])
        ps=ctx.enter_context(nc.psum_tensor("idx_ps",[128,8,512],F32)); SB_,ZB_,PB=4,4,7
        w_loaded=sem("w_loaded"); made=sem("made"); proj=sem("proj"); proj_copied=sem("proj_copied"); scored=sem("scored"); relu_ready=sem("relu_ready"); summed=sem("summed")
        seen=sem("causal_done"); found=sem("max8_found"); waited=sem("waited"); taken=sem("taken"); biased=sem("bias_written")
        hT_l=[sem(f"hT_loaded{j}") for j in range(2)]; wz_l=[sem(f"w_in_loaded{j}") for j in range(2)]; z_acc=sem("z_acc"); z_copied=sem("z_copied"); z_st=[sem(f"z_stored{j}") for j in range(2)]
        block=ctx.enter_context(nc.Block())
        PAIRS=ZB2*TT//2; done=[round(PAIRS*sum(WIDTH[FB:b])/sum(WIDTH[FB:])) for b in range(FB,TT+1)]
        def z_pairs(eng,b,each,first=lambda cb: None):
            p,end=done[b-FB],done[b-FB+1]
            while p<end:
                cb=p//(TT//2); p0=cb*(TT//2); stop=min(end,p0+TT//2)
                if p==p0: first(cb)
                loop_end=stop-1 if stop==p0+TT//2 else stop
                if loop_end-p==1: each(cb,p-p0)
                elif loop_end>p:
                    with eng.Fori(p-p0,loop_end-p0) as r: each(cb,r)
                if loop_end<stop: each(cb,loop_end-p0)
                p=stop
        wv=w_in.rearrange("l (k p) n -> p (l k) n",p=128)
        @block.sync
        def _(sp):
            sp.dma_start(w[:],w_qidx.rearrange("l (k p) n -> p (l k) n",p=128)).then_inc(w_loaded,16)
            for j in range(2): sp.sem_inc(z_st[j],16)
            def load_w(cb): sp.dma_start(wz[:,cb%2],wv[:,:,ZA+cb*ZN2:ZA+(cb+1)*ZN2]).then_inc(wz_l[cb%2],16)
            load_w(0)
            for j in range(2): sp.dma_start(hT[:,j],h_tiles[j]).then_inc(hT_l[j],16)
            load_w(1)
            def first(cb):
                if cb>=1 and cb+1<ZB2:
                    sp.wait_ge(z_acc,cb*TT+2)
                    load_w(cb+1)
            def each(cb,p):
                for j in range(2):
                    u=cb*TT+j
                    sp.wait_ge(z_acc,p*2+(u+1+2))
                    wrap=isinstance(p,int) and p==TT//2-1
                    sp.dma_start(hT[:,j],h_tiles[j] if wrap else h_tiles[p*2+(j+2)]).then_inc(hT_l[j],16)
                    sp.wait_ge(z_copied,p*2+(u+1+2))
                    sp.dma_start(zt[p*2+j,:,ZA+cb*ZN2:ZA+(cb+1)*ZN2],stage[:,j]).then_inc(z_st[j],16)
            for b in BLOCKS: z_pairs(sp,b,each,first)
            for j in range(2): sp.wait_ge(z_st[j],16*PAIRS+16); sp.wait_ge(hT_l[j],16*PAIRS+16)
        @block.gpsimd
        def _(pool):
            pool.memset(cmask[:],0.0).then_inc(made,1)
            pool.wait_ge(made,1)
            pool.affine_select(out=cmask[:],in_=cmask[:],compare_op=ALU.is_ge,fill=UNSEEN,base=0,pattern=[[-1,128]],channel_multiplier=1).then_inc(made,1)
        @block.tensor
        def _(pe):
            pe.wait_ge(w_loaded,16)
            pe.sem_inc(z_acc,2)
            def project(i,b):
                if i: pe.wait_ge(proj_copied,i)
                for p in range(NIH//2):
                    for k in range(QK_):
                        t=nc.tensor.matmul(ps[:,PB,p*128:(p+1)*128],w[:,k,p*128:(p+1)*128],cqT[:,k,b*128:(b+1)*128],start=(k==0),stop=(k==QK_-1))
                t.then_inc(proj,1)
            def each(cb,p):
                for j in range(2):
                    u=cb*TT+j
                    pe.wait_ge(hT_l[j],p*16+(u//2*16+16))
                    pe.wait_ge(z_copied,p*2+(u+1))
                    for k in range(KD):
                        t=nc.tensor.matmul(ps[:,ZB_+j,0:ZN2],hT[:,j,k],wz[:,cb%2,k],start=(k==0),stop=(k==KD-1))
                    t.then_inc(z_acc,1)
            project(0,FB)
            n=0
            for i,b in enumerate(BLOCKS):
                pe.wait_ge(proj_copied,i+1)
                for c,wd in CH[b]:
                    for h in range(NIH):
                        if n>=SB_: pe.wait_ge(relu_ready,n-SB_+1)
                        r=(h%2)*ID; q=h//2*128
                        nc.tensor.matmul(ps[:,n%SB_,0:wd],qi[r:r+ID,b%2,q:q+128],kiT[r:r+ID,c:c+wd],start=True,stop=True).then_inc(scored,1)
                        n+=1
                if b+1<TT: project(i+1,b+1)
                z_pairs(pe,b,each,lambda cb: pe.wait_ge(wz_l[cb%2],cb//2*16+16))
        @block.scalar
        def _(act):
            act.sem_inc(z_copied,2)
            def copy_q(i,b):
                act.wait_ge(proj,i+1)
                nc.scalar.copy(qi[:,b%2],ps[:,PB]).then_inc(proj_copied,1)
            def each(cb,p):
                for j in range(2):
                    u=cb*TT+j
                    act.wait_ge(z_acc,p*2+(u+1+2))
                    act.wait_ge(z_st[j],p*16+(u//2*16+16))
                    nc.scalar.copy(stage[:,j],ps[:,ZB_+j,0:ZN2]).then_inc(z_copied,1)
            copy_q(0,FB)
            n=0
            for i,b in enumerate(BLOCKS):
                for c,wd in CH[b]:
                    for h in range(NIH):
                        act.wait_ge(scored,n+1)
                        if n>=RR: act.wait_ge(summed,n-RR+1)
                        nc.scalar.activation(relu[:,n%RR,0:wd],ps[:,n%SB_,0:wd],ACT.Relu).then_inc(relu_ready,1)
                        n+=1
                if b+1<TT: copy_q(i+1,b+1)
                z_pairs(act,b,each)
        @block.vector
        def _(dve):
            dve.sem_inc(taken,1)
            dve.wait_ge(made,2)
            for b in range(FB):
                if b: nc.vector.memset(bias[:,MOFF[b]:MOFF[b]+b*128],0.0)
                nc.vector.tensor_copy(bias[:,MOFF[b]+b*128:MOFF[b]+WIDTH[b]],cmask[:]).then_inc(biased,1)
            n=0
            for i,b in enumerate(BLOCKS):
                if i: dve.wait_ge(biased,FB+i)
                for c,wd in CH[b]:
                    for h in range(NIH):
                        dve.wait_ge(relu_ready,n+1)
                        o=isc[:,c:c+wd]
                        if h==0: nc.vector.tensor_scalar(o,relu[:,n%RR,0:wd],wi[:,b,h:h+1],None,ALU.mult).then_inc(summed,1)
                        else:
                            dve.wait_ge(summed,n)
                            nc.vector.scalar_tensor_tensor(out=o,in0=relu[:,n%RR,0:wd],scalar=wi[:,b,h:h+1],in1=o,op0=ALU.mult,op1=ALU.add).then_inc(summed,1)
                        n+=1
                dve.wait_ge(summed,n)
                nc.vector.tensor_tensor(isc[:,b*128:WIDTH[b]],isc[:,b*128:WIDTH[b]],cmask[:],ALU.add).then_inc(seen,1)
                dve.wait_ge(seen,i+1)
                v=isc[:,0:WIDTH[b]]
                base=i*(TOPK//8)
                with dve.Fori(0,TOPK//8) as r:
                    dve.wait_ge(taken,r+(base+1)); dve.sem_inc(waited,1)
                    nc.vector.max(m8[:],v).then_inc(found,1)
                    dve.wait_ge(found,r+(base+1)); dve.sem_inc(waited,1)
                    nc.vector.match_replace(v,m8[:],v,TAKEN).then_inc(taken,1)
                dve.wait_ge(taken,base+TOPK//8+1)
                nc.vector.tensor_scalar(bias[:,MOFF[b]:MOFF[b]+WIDTH[b]],v,-2e38,UNSEEN,ALU.is_gt,ALU.mult).then_inc(biased,1)

def attention(nc,w_uq,w_uk,w_uv,cqT,ckvT,bias,ident,yt):
    SCALE=float(HD)**-0.5; HG=4; SR=3; TR=2
    CH=[[(c,min(512,WIDTH[b]-c)) for c in range(0,WIDTH[b],512)] for b in range(TT)]
    NCH=sum(len(c) for c in CH)
    C0=[sum(len(c) for c in CH[:b]) for b in range(TT)]
    TQ4=S//512
    with ExitStack() as ctx:
        sb=lambda n,s,d=F32: ctx.enter_context(nc.sbuf_tensor("att_"+n,s,d))
        sem=semaphores(nc,ctx,"att")
        wq=sb("w_uq_h",[128,2,QK_,HD]); wk=sb("w_uk_h",[128,2,KK,HD]); wv=sb("w_uv_g",[128,KK,HG*HD])
        qT=sb("qT",[128,S]); kT=sb("kT",[128,S]); V=sb("V",[128,TT,HG*HD]); Sc=sb("scores",[128,2,S]); PT=sb("probsT",[128,2,TT,128])
        cm=sb("chunk_max",[128,2,4]); nm=sb("neg_max",[128,2]); rsum=sb("row_sum",[128,2]); rinv=sb("row_inv",[128,2]); o=sb("o",[128,4,HD])
        ps=ctx.enter_context(nc.psum_tensor("att_ps",[128,8,512],F32)); PJ,OB=6,7
        wq_l=[sem(f"wqk_loaded{j}") for j in range(2)]; wv_l=sem("wv_loaded"); proj=sem("projected"); pcopy=sem("proj_copied"); v_ps=sem("v_in_psum"); v_copy=sem("v_copied")
        scored=sem("scored"); masked=sem("masked"); waited=sem("waited"); maxed=sem("maxed"); mx=sem("mx"); expd=sem("exp_done"); pturned=sem("probs_turned"); pt_act=sem("probsT_act"); pt_dve=sem("probsT_dve"); pv=sem("pv_done"); inv=sem("row_inv_ready"); o_ready=sem("o_ready"); stored=[sem(f"o_stored{j}") for j in range(4)]
        block=ctx.enter_context(nc.Block())
        wqv=w_uq.rearrange("l (k p) n -> p (l k) n",p=128); wkv=w_uk.rearrange("l (k p) h d -> p (l k) (h d)",p=128); wvv=w_uv.rearrange("l (k p) h d -> p (l k) (h d)",p=128)
        PC=2*TQ4
        G=[(b,t0,min(4,b+1-t0)) for b in range(TT) for t0 in range(0,b+1,4)]
        NG=len(G); G0=[sum(1 for g in G if g[0]<b) for b in range(TT)]
        def loops(eng,body):
            with eng.Fori(0,NAH//HG) as gg:
                for hh in range(HG): body(gg,hh)
        @block.sync
        def _(sp):
            for s in stored: sp.sem_inc(s,16)
            def body(gg,hh):
                j=hh%2
                if hh==0:
                    sp.wait_ge(v_ps,gg*TT+1)
                    sp.dma_start(wv[:],wvv[:,:,bass.ds(gg*(HG*HD),HG*HD)]).then_inc(wv_l,16)
                sp.wait_ge(proj,(gg*HG+hh)*PC+1)
                sp.dma_start(wq[:,j],wqv[:,:,bass.ds((gg*HG+hh)*HD,HD)]).then_inc(wq_l[j],16)
                sp.dma_start(wk[:,j],wkv[:,:,bass.ds((gg*HG+hh)*HD,HD)]).then_inc(wq_l[j],16)
                for b in range(TT):
                    sp.wait_ge(o_ready,(gg*HG+hh)*TT+(b+1)+1)
                    sp.dma_start(yt[b,:,bass.ds((gg*HG+hh)*HD,HD)],o[:,b%4]).then_inc(stored[b%4],16)
            loops(sp,body)
            for j in range(4): sp.wait_ge(stored[j],16*NAH*TT//4+16)
        @block.tensor
        def _(pe):
            pe.sem_inc(pturned,1)
            pe.sem_inc(proj,1)
            pe.sem_inc(scored,1)
            pe.sem_inc(v_ps,1)
            def body(gg,hh):
                H=gg*HG+hh; j=hh%2
                if hh==0:
                    pe.wait_ge(wv_l,gg*16+16)
                    pe.wait_ge(pv,gg*(HG*TT)+2)
                    for t in range(TT):
                        pe.wait_ge(v_copy,gg*TT+t+1)
                        pe.wait_ge(pcopy,gg*(HG*PC)+1)
                        for k in range(KK):
                            m=nc.tensor.matmul(ps[:,PJ],ckvT[:,k,t*128:(t+1)*128],wv[:,k],start=(k==0),stop=(k==KK-1))
                        m.then_inc(v_ps,1)
                    pe.wait_ge(v_copy,gg*TT+TT+1)
                pe.wait_ge(wq_l[j],(gg*(HG//2)+hh//2)*32+32)
                for n in range(PC):
                    pe.wait_ge(pcopy,H*PC+n+1)
                    s,c=(wq,n) if n<TQ4 else (wk,n-TQ4)
                    K_=QK_ if n<TQ4 else KK; src=cqT if n<TQ4 else ckvT
                    for k in range(K_):
                        m=nc.tensor.matmul(ps[:,PJ],s[:,j,k],src[:,k,c*512:(c+1)*512],start=(k==0),stop=(k==K_-1))
                    m.then_inc(proj,1)
                pe.wait_ge(pcopy,H*PC+PC+1)
                def scores(b):
                    for i,(c,wd) in enumerate(CH[b]):
                        pe.wait_ge(masked,H*NCH+(C0[b]+i+1))
                        nc.tensor.matmul(ps[:,(C0[b]+i)%4,0:wd],qT[:,b*128:(b+1)*128],kT[:,c:c+wd],start=True,stop=True).then_inc(scored,1)
                def out(b):
                    pe.wait_ge(expd,H*TT+b+1+1)
                    for gi in range(G0[b],G0[b]+len([1 for g in G if g[0]==b])):
                        _,t0,nt=G[gi]
                        pe.wait_ge((pt_act,pt_dve)[gi%2],H*(NG//2)+(gi//2+1))
                        for t in range(nt):
                            m=nc.tensor.transpose(ps[:,4+gi%2,t*128:(t+1)*128],Sc[:,b%2,(t0+t)*128:(t0+t+1)*128],ident[:])
                        m.then_inc(pturned,1)
                    pe.wait_ge(o_ready,H*TT+b+1)
                    for gi in range(G0[b],G0[b]+len([1 for g in G if g[0]==b])):
                        _,t0,nt=G[gi]
                        pe.wait_ge((pt_act,pt_dve)[gi%2],H*(NG//2)+(gi//2+2))
                        for t in range(nt):
                            m=nc.tensor.matmul(ps[:,OB,0:HD],PT[:,b%2,t0+t],V[:,t0+t,hh*HD:(hh+1)*HD],start=(t0+t==0),stop=(t0+t==b))
                    m.then_inc(pv,1)
                scores(0)
                for b in range(TT):
                    if b+1<TT: scores(b+1)
                    out(b)
            loops(pe,body)
        @block.scalar
        def _(act):
            act.sem_inc(expd,1)
            act.sem_inc(pt_act,1)
            def body(gg,hh):
                H=gg*HG+hh
                if hh==0:
                    for t in range(0,TT,2):
                        act.wait_ge(v_ps,gg*TT+t+1+1)
                        nc.scalar.copy(V[:,t],ps[:,PJ]).then_inc(v_copy,1)
                        act.wait_ge(v_copy,gg*TT+t+2+1)
                act.wait_ge(scored,H*NCH+1)
                for n in range(0,PC,2):
                    act.wait_ge(proj,H*PC+n+1+1)
                    dst=(qT,kT)[n//TQ4]
                    nc.scalar.copy(dst[:,(n%TQ4)*512:(n%TQ4)*512+512],ps[:,PJ]).then_inc(pcopy,1)
                    act.wait_ge(pcopy,H*PC+n+2+1)
                for b in range(TT):
                    act.wait_ge(maxed,(H*TT+b)+1); act.wait_ge(masked,H*NCH+(C0[b]+len(CH[b])+4)); act.wait_ge(inv,H*TT+(b+1))
                    nc.scalar.activation(Sc[:,b%2,0:WIDTH[b]],Sc[:,b%2,0:WIDTH[b]],ACT.Exp,bias=nm[:,b%2:b%2+1],scale=SCALE,accum_out=rsum[:,b%2:b%2+1]).then_inc(expd,1)
                    for gi,(bb,t0,nt) in enumerate(G):
                        if bb!=b or gi%2: continue
                        act.wait_ge(pturned,H*NG+gi+1+1); act.wait_ge(pv,H*TT+(b+1))
                        nc.scalar.copy(PT[:,b%2,t0:t0+nt].rearrange("p t n -> p (t n)"),ps[:,4,0:nt*128]).then_inc(pt_act,1)
            act.sem_inc(inv,2)
            act.sem_inc(pv,2)
            loops(act,body)
        @block.vector
        def _(dve):
            dve.sem_inc(o_ready,1)
            dve.sem_inc(pcopy,1)
            dve.sem_inc(v_copy,1)
            dve.sem_inc(pt_dve,1); dve.sem_inc(masked,4)
            def body(gg,hh):
                H=gg*HG+hh
                if hh==0:
                    for t in range(1,TT,2):
                        dve.wait_ge(v_ps,gg*TT+t+1+1)
                        nc.vector.tensor_copy(V[:,t],ps[:,PJ]).then_inc(v_copy,1)
                dve.wait_ge(scored,H*NCH+1)
                for n in range(1,PC,2):
                    dve.wait_ge(proj,H*PC+n+1+1)
                    dst=(qT,kT)[n//TQ4]
                    nc.vector.tensor_copy(dst[:,(n%TQ4)*512:(n%TQ4)*512+512],ps[:,PJ]).then_inc(pcopy,1)
                def mask(b):
                    dve.wait_ge(pturned,H*NG+(G0[b-1] if b else 0)+1); dve.wait_ge(expd,H*TT+b+1)
                    for i,(c,wd) in enumerate(CH[b]):
                        dve.wait_ge(scored,H*NCH+(C0[b]+i+1)+1); dve.sem_inc(waited,1)
                        nc.vector.tensor_tensor_reduce(Sc[:,b%2,c:c+wd],ps[:,(C0[b]+i)%4,0:wd],bias[:,MOFF[b]+c:MOFF[b]+c+wd],1.0,-3e38,ALU.add,ALU.max,cm[:,b%2,i:i+1]).then_inc(masked,1)
                    dve.wait_ge(masked,H*NCH+(C0[b]+len(CH[b])+4))
                    nc.vector.tensor_reduce(nm[:,b%2:b%2+1],cm[:,b%2,0:len(CH[b])],AX.X,ALU.max).then_inc(mx,1)
                    dve.wait_ge(mx,H*TT+b+1)
                    nc.vector.tensor_scalar(nm[:,b%2:b%2+1],nm[:,b%2:b%2+1],-SCALE,None,ALU.mult).then_inc(maxed,1)
                def rest(b):
                    for gi,(bb,t0,nt) in enumerate(G):
                        if bb!=b or gi%2==0: continue
                        dve.wait_ge(pturned,H*NG+gi+1+1); dve.wait_ge(pv,H*TT+(b+1))
                        nc.vector.tensor_copy(PT[:,b%2,t0:t0+nt].rearrange("p t n -> p (t n)"),ps[:,5,0:nt*128]).then_inc(pt_dve,1)
                    dve.wait_ge(expd,H*TT+b+1+1); dve.wait_ge(o_ready,H*TT+b+1)
                    nc.vector.reciprocal(rinv[:,b%2:b%2+1],rsum[:,b%2:b%2+1]).then_inc(inv,1)
                    dve.wait_ge(pv,H*TT+(b+3)); dve.wait_ge(inv,H*TT+(b+3)); dve.wait_ge(stored[b%4],(H*(TT//4)+b//4)*16+16)
                    nc.vector.tensor_scalar(o[:,b%4],ps[:,OB,0:HD],rinv[:,b%2:b%2+1],None,ALU.mult).then_inc(o_ready,1)
                mask(0)
                for b in range(TT):
                    if b+1<TT: mask(b+1)
                    rest(b)
            loops(dve,body)

NE=32; GRP=4; EPG=8; FF=512; MT=63; SLOTS_=(MT+1)*128
U32=mybir.dt.uint32; I32=mybir.dt.int32

def out_projection(nc, y, x, mod, w_out, norm_g, router_w, x1, xn, ffn_cols, logits):
    yt=y.rearrange("(t p) d -> t p d",p=128); xt=x.rearrange("b (t p) d -> (b t) p d",p=128)
    x1t=x1.rearrange("(t p) d -> t p d",p=128); xnt=xn.rearrange("(t p) d -> t p d",p=128)
    modv=mod.rearrange("l (s k p) -> s (l k) p",s=6,p=128)
    row=lambda s: mod[:,s*D:(s+1)*D].to_broadcast([128,D])
    with ExitStack() as ctx:
        sb=lambda n,s,d=F32: ctx.enter_context(nc.sbuf_tensor("op_"+n,s,d))
        sem=semaphores(nc,ctx,"op")
        w=sb("w_out",[128,KD,D]); yb=sb("y",[128,2,D]); xb=sb("x",[128,2,D]); g1=sb("gate1",[128,D]); junk=sb("squares",[128,D],mybir.dt.bfloat16); gated=sb("gated",[128,2,512]); rows=sb("param_rows",[3*KD,128])
        yT=sb("yT",[128,2,KD,128]); hT=sb("h2T",[128,KD,128]); rw=sb("router_w",[128,KD,NE]); ident=sb("ident",[128,128]); ss=sb("ss",[128,2]); eps=sb("eps",[128,1])
        ps=ctx.enter_context(nc.psum_tensor("op_ps",[128,8,512],F32)); YB,HB,LB=4,6,7
        w_loaded=[sem(f"w_loaded{n}") for n in range(4)]; rows_loaded=sem("rows_loaded"); gate_loaded=sem("gate_loaded"); rw_loaded=sem("router_w_loaded"); made=sem("made"); y_loaded=[sem(f"y_loaded{j}") for j in range(2)]; x_loaded=[sem(f"x_loaded{j}") for j in range(2)]; cols_turned=sem("cols_turned"); cols_ready=sem("cols_ready")
        y_turned=sem("y_turned"); yT_ev=sem("yT_copied"); acc_ready=sem("acc_ready"); acc_used=sem("acc_used"); x1_ready=sem("x1_ready"); ss_ready=sem("ss_ready"); rs_ready=sem("rstd_ready"); xn_ready=sem("xn_ready"); xn_st=sem("xn_stored")
        h_turned=sem("h_turned"); hT_ev=sem("hT_copied"); lg_ready=sem("logits_ready"); lg_copied=sem("logits_copied"); x1_st=sem("x1_stored"); sp_waited=sem("sp_waited")
        block=ctx.enter_context(nc.Block())
        def paired(eng,step):
            step(0,0,first=True)
            with eng.Fori(0,TT//2-1) as g:
                step(g*2+1,1); step(g*2+2,0)
            step(TT-1,1,last=True)
        @block.gpsimd
        def _(pool):
            identity_tile(nc,pool,ident,made)
            pool.memset(eps[:],EPS).then_inc(made,1)
        @block.sync
        def _(sp):
            def load(t,j):
                sp.dma_start(yb[:,j],yt[t]).then_inc(y_loaded[j],16)
                sp.dma_start(xb[:,j],xt[t]).then_inc(x_loaded[j],16)
            sp.dma_start(rows[0:KD],norm_g.rearrange("l (k p) -> (l k) p",p=128)).then_inc(rows_loaded,16)
            sp.dma_start(rows[KD:2*KD],modv[4]).then_inc(rows_loaded,16)
            sp.dma_start(rows[2*KD:3*KD],modv[3]).then_inc(rows_loaded,16)
            load(0,0)
            wv=w_out.rearrange("l (k p) n -> p (l k) n",p=128)
            sp.dma_start(w[:,:,0:512],wv[:,:,0:512]).then_inc(w_loaded[0],16)
            sp.dma_start(g1[:],row(2)).then_inc(gate_loaded,16)
            for n in range(1,4): sp.dma_start(w[:,:,n*512:(n+1)*512],wv[:,:,n*512:(n+1)*512]).then_inc(w_loaded[n],16)
            load(1,1)
            sp.dma_start(rw[:],router_w.rearrange("(k p) n -> p k n",p=128)).then_inc(rw_loaded,16)
            def step(t,j,more):
                if more:
                    sp.wait_ge(y_turned,t*4+8)
                    sp.dma_start(yb[:,j],yt[t+2]).then_inc(y_loaded[j],16)
                sp.wait_ge(x1_ready,t*4+4)
                sp.dma_start(x1t[t],xb[:,j]).then_inc(x1_st,16)
                sp.wait_ge(xn_ready,t+1)
                sp.dma_start(xnt[t],xb[:,j]).then_inc(xn_st,16)
                if more:
                    sp.wait_ge(h_turned,t*4+4); sp.sem_inc(sp_waited,1)
                    sp.wait_ge(xn_st,t*16+16)
                    sp.dma_start(xb[:,j],xt[t+2]).then_inc(x_loaded[j],16)
            with sp.Fori(0,TT//2-1) as g:
                for j in range(2): step(g*2+j,j,True)
            for j in range(2): step(TT-2+j,j,False)
            sp.wait_ge(xn_st,16*TT); sp.wait_ge(x1_st,16*TT)
        @block.tensor
        def _(pe):
            pe.sem_inc(lg_ready,1)
            pe.wait_ge(made,2); pe.wait_ge(rows_loaded,48)
            nc.tensor.transpose(ps[:,LB,0:3*KD],rows[:],ident[0:3*KD,0:3*KD]).then_inc(cols_turned,1)
            def y_turn(t,j,i):
                if i==0: pe.wait_ge(y_loaded[j],(t-j)*8+16)
                pe.wait_ge(yT_ev,t*4+i)
                for q in range(4):
                    m=nc.tensor.transpose(ps[:,YB+i%2,q*128:q*128+128],yb[:,j,(4*i+q)*128:(4*i+q+1)*128],ident[:])
                m.then_inc(y_turned,1)
            def h_turn(t,j,i):
                if i==0: pe.wait_ge(xn_ready,t+1)
                pe.wait_ge(hT_ev,t*4+i+1)
                for q in range(4):
                    m=nc.tensor.transpose(ps[:,HB,q*128:q*128+128],xb[:,j,(4*i+q)*128:(4*i+q+1)*128],ident[:])
                m.then_inc(h_turned,1)
            def router(t):
                pe.wait_ge(hT_ev,t*4+4+1); pe.wait_ge(lg_copied,t+1)
                for k in range(KD):
                    m=nc.tensor.matmul(ps[:,LB,0:NE],hT[:,k],rw[:,k],start=(k==0),stop=(k==KD-1))
                m.then_inc(lg_ready,1)
            def step(t,j,first=False,last=False):
                y=lambda i: None if last else y_turn(t+1,1-j,i)
                h=lambda i: None if first else h_turn(t-1,1-j,i)
                pe.wait_ge(yT_ev,t*4+5)
                for e in range(8):
                    n=e//2
                    if e%2==0:
                        if first: pe.wait_ge(w_loaded[n],16)
                        pe.wait_ge(acc_used,t*4+(n+1))
                    for k in range(e%2*8,e%2*8+8):
                        m=nc.tensor.matmul(ps[:,n],yT[:,j,k],w[:,k,n*512:(n+1)*512],start=(k==0),stop=(k==KD-1))
                    if e%2: m.then_inc(acc_ready,1)
                    if e==1: y(0)
                    if e==2: y(1); h(0)
                    if e==3: y(2); h(1)
                    if e==4: y(3); h(2)
                    if e==5: h(3)
                    if e==6 and first: pe.wait_ge(rw_loaded,16)
                    if e==6 and not first: router(t-1)
            for i in range(4): y_turn(0,0,i)
            paired(pe,step)
            for i in range(4): h_turn(TT-1,1,i)
            router(TT-1)
        @block.scalar
        def _(act):
            act.sem_inc(hT_ev,1)
            act.sem_inc(lg_copied,1)
            act.wait_ge(made,3)
            act.sem_inc(yT_ev,1)
            def y_copy(t,j,i):
                act.wait_ge(y_turned,t*4+(i+1))
                nc.scalar.copy(yT[:,j,4*i:4*i+4].rearrange("p k n -> p (k n)"),ps[:,YB+i%2]).then_inc(yT_ev,1)
            def norm(t,j):
                act.wait_ge(x1_ready,t*4+4)
                nc.scalar.activation(junk[:],xb[:,j],ACT.Square,scale=float(D)**-0.5,accum_out=ss[:,j:j+1]).then_inc(ss_ready,1)
                act.wait_ge(ss_ready,t*2+1)
                nc.scalar.activation(ss[:,j:j+1],ss[:,j:j+1],ACT.Ln,bias=eps[:]).then_inc(ss_ready,1)
                act.wait_ge(ss_ready,t*2+2)
                nc.scalar.activation(ss[:,j:j+1],ss[:,j:j+1],ACT.Exp,scale=-0.5).then_inc(rs_ready,1)
            def h_copy(t,j,i):
                if i==0: act.wait_ge(lg_ready,t+1)
                act.wait_ge(h_turned,t*4+(i+1))
                for k in range(4*i,4*i+4):
                    m=nc.scalar.activation(hT[:,k],ps[:,HB,(k-4*i)*128:(k-4*i)*128+128],ACT.Identity,scale=ffn_cols[:,k:k+1],bias=ffn_cols[:,KD+k:KD+k+1])
                m.then_inc(hT_ev,1)
            def logits_copy(t):
                act.wait_ge(lg_ready,t+2)
                nc.scalar.copy(logits[:,bass.ds(t,1),:].rearrange("p o e -> p (o e)"),ps[:,LB,0:NE]).then_inc(lg_copied,1)
            def step(t,j,first=False,last=False):
                y=lambda i: None if last else y_copy(t+1,1-j,i)
                h=lambda i: None if first else h_copy(t-1,1-j,i)
                if not first:
                    norm(t-1,1-j)
                    act.wait_ge(acc_ready,t*4)
                y(0); y(1); h(0); y(2); h(1); y(3); h(2); h(3)
                if not first: logits_copy(t-1)
            for i in range(4): y_copy(0,0,i)
            act.wait_ge(cols_ready,2)
            paired(act,step)
            norm(TT-1,1)
            for i in range(4): h_copy(TT-1,1,i)
            logits_copy(TT-1)
        @block.vector
        def _(dve):
            dve.sem_inc(acc_used,4)
            dve.wait_ge(cols_turned,1)
            nc.vector.tensor_copy(ffn_cols[:],ps[:,LB,KD:3*KD]).then_inc(cols_ready,1)
            dve.wait_ge(cols_ready,1)
            nc.vector.scalar_tensor_tensor(out=ffn_cols[:,0:KD],in0=ffn_cols[:,0:KD],scalar=1.0,in1=ps[:,LB,0:KD],op0=ALU.add,op1=ALU.mult).then_inc(cols_ready,1)
            dve.wait_ge(gate_loaded,16)
            def step(t,j):
                dve.wait_ge(x_loaded[j],(t-j)*8+16)
                for n in range(4):
                    c=slice(n*512,(n+1)*512)
                    dve.wait_ge(acc_ready,t*4+(n+1))
                    nc.vector.tensor_tensor(gated[:,n%2],ps[:,n],g1[:,c],ALU.mult).then_inc(acc_used,1)
                    dve.wait_ge(acc_used,t*4+(n+5))
                    nc.vector.tensor_tensor(xb[:,j,c],xb[:,j,c],gated[:,n%2],ALU.add).then_inc(x1_ready,1)
                dve.wait_ge(rs_ready,t+1); dve.wait_ge(x1_st,t*16+16)
                nc.vector.tensor_scalar(xb[:,j],xb[:,j],ss[:,j:j+1],None,ALU.mult).then_inc(xn_ready,1)
            with dve.Fori(0,TT//2) as g:
                for j in range(2): step(g*2+j,j)
            dve.wait_ge(lg_copied,TT+1)

MT_ALL=MT+1

def routing(nc, logits, router_b, token_of_slot, slots, gates, tile_expert, new_expert, tiles_used):
    with ExitStack() as ctx:
        sb=lambda n,s,d=F32: ctx.enter_context(nc.sbuf_tensor("rt_"+n,s,d))
        sem=semaphores(nc,ctx,"rt")
        NG_=TT*GRP; E_=TT*NE
        rb=sb("router_b",[128,NE]); aff=sb("affinity",[128,TT,NE]); sel=sb("selection",[128,TT,NE])
        ie=sb("expert_iota_m8",[128,EPG]); ig=sb("group_iota_m4",[128,GRP]); tok=sb("token_ids",[128,TT],I32); tri=sb("before",[128,128]); ones=sb("ones",[128,128]); zeros=sb("zero_slots",[128,MT_ALL],I32)
        m=sb("best",[128,2,NG_]); i8=sb("first_index",[128,2,NG_]); t8=sb("tmp",[128,TT,NE]); oh=sb("onehot",[128,2,TT,NE]); M=sb("chosen",[128,TT,NE])
        gs=sb("group_score",[128,TT,GRP]); gb=sb("group_best",[128,TT]); gi=sb("group_index",[128,TT]); goh=sb("group_onehot",[128,TT,GRP])
        carry=sb("carry",[128,TT+1,NE]); mi=sb("multiples_of_128",[128,S//128]); cmp=sb("compare",[128,NE,S//128]); nt=sb("tiles_of_expert",[128,NE]); end=sb("end_tile",[128,NE]); one=sb("one_row",[128,NE]); base=sb("first_slot",[128,NE])
        ti=sb("tile_iota",[1,MT_ALL]); tc=sb("tile_compare",[1,MT_ALL,NE]); te=sb("tile_expert_f",[1,MT_ALL]); tf=sb("tile_fresh",[1,MT_ALL]); sf=sb("slots_f",[128,2,TT]); a12=sb("gates_raw",[128,2,TT]); asum=sb("gate_sum",[128,TT])
        ps=ctx.enter_context(nc.psum_tensor("rt_ps",[128,2,512],F32))
        made=sem("made"); rb_loaded=sem("rb_loaded"); zeroed=sem("zeroed"); ex=sem("exp_ready"); v=sem("vector_done"); ranked=sem("ranked"); chosen=sem("chosen"); slotted=sem("slotted"); scattered=sem("scattered")
        block=ctx.enter_context(nc.Block())
        v8=lambda t: t.rearrange("p t (g e) -> p (t g) e",g=GRP)
        up=lambda ap,n: ap.rearrange("p (n o) -> p n o",o=1).to_broadcast([128,ap.shape[1],n])
        lead=lambda ap,n: ap.rearrange("p (o n) -> p o n",o=1).to_broadcast([ap.shape[0],n,ap.shape[1]])
        @block.sync
        def _(sp):
            sp.dma_start(rb[:],router_b.rearrange("(o e) -> o e",o=1).to_broadcast([128,NE])).then_inc(rb_loaded,16)
            sp.wait_ge(made,9)
            sp.dma_start(token_of_slot.rearrange("(p t) o -> p (t o)",p=128),zeros[:]).then_inc(zeroed,16)
            sp.wait_ge(rb_loaded,16)
        @block.gpsimd
        def _(pool):
            ap=dict(allow_small_or_imprecise_dtypes=True)
            pool.iota(ie[:],pattern=[[1,EPG]],base=-EPG,channel_multiplier=0,**ap).then_inc(made,1)
            pool.iota(ig[:],pattern=[[1,GRP]],base=-GRP,channel_multiplier=0,**ap).then_inc(made,1)
            pool.iota(tok[:],pattern=[[128,TT]],base=0,channel_multiplier=1).then_inc(made,1)
            pool.iota(mi[:],pattern=[[128,S//128]],base=0,channel_multiplier=0,**ap).then_inc(made,1)
            pool.iota(ti[:],pattern=[[1,MT_ALL]],base=0,channel_multiplier=0,**ap).then_inc(made,1)
            pool.memset(ones[:],1.0).then_inc(made,1)
            pool.memset(tri[:],1.0).then_inc(made,1)
            pool.memset(one[:],1.0).then_inc(made,1)
            pool.memset(zeros[:],0).then_inc(made,1)
            pool.wait_ge(made,9)
            pool.affine_select(out=tri[:],in_=tri[:],compare_op=ALU.is_gt,fill=0.0,base=0,pattern=[[1,128]],channel_multiplier=-1).then_inc(made,1)
            pool.wait_ge(zeroed,16); pool.wait_ge(slotted,1)
            for q in range(2):
                for t in range(TT):
                    pool.indirect_dma_start(out=token_of_slot,out_offset=bass.IndirectOffsetOnAxis(ap=slots[:,q,t:t+1],axis=0),in_=tok[:,t:t+1],in_offset=None).then_inc(scattered,16)
            pool.wait_ge(scattered,32*TT)
        @block.scalar
        def _(act):
            nc.scalar.activation(aff[:].rearrange("p t e -> p (t e)"),logits[:].rearrange("p t e -> p (t e)"),ACT.Exp,scale=-1.0).then_inc(ex,1)
        @block.tensor
        def _(pe):
            pe.wait_ge(made,10); pe.wait_ge(chosen,1)
            r=M[:].rearrange("p t e -> p (t e)")
            nc.tensor.matmul(ps[:,0],tri[:],r,start=True,stop=True)
            nc.tensor.matmul(ps[:,1],ones[:],r,start=True,stop=True).then_inc(ranked,1)
        @block.vector
        def _(dve):
            n=[0]
            def then(ins):
                n[0]+=1
                ins.then_inc(v,1); dve.wait_ge(v,n[0])
            V=nc.vector
            dve.wait_ge(ex,1); dve.wait_ge(rb_loaded,16); dve.wait_ge(made,10)
            then(V.tensor_scalar(aff[:],aff[:],1.0,None,ALU.add))
            then(V.reciprocal(aff[:],aff[:]))
            then(V.tensor_tensor(sel[:],aff[:],lead(rb[:],TT),ALU.add))
            for q in range(2):
                then(V.tensor_reduce(m[:,q],v8(sel[:]),AX.X,ALU.max))
                then(V.tensor_tensor(v8(t8[:]),v8(sel[:]),up(m[:,q],EPG),ALU.is_equal))
                then(V.tensor_tensor(v8(t8[:]),v8(t8[:]),lead(ie[:],NG_),ALU.mult))
                then(V.tensor_reduce(i8[:,q],v8(t8[:]),AX.X,ALU.min))
                then(V.tensor_tensor(v8(oh[:,q]),lead(ie[:],NG_),up(i8[:,q],EPG),ALU.is_equal))
                if q==0: then(V.scalar_tensor_tensor(out=sel[:],in0=oh[:,0],scalar=-BIG,in1=sel[:],op0=ALU.mult,op1=ALU.add))
            then(V.tensor_tensor(gs[:].rearrange("p t g -> p (t g)"),m[:,0],m[:,1],ALU.add))
            then(V.tensor_reduce(gb[:],gs[:],AX.X,ALU.max))
            then(V.tensor_tensor(gs[:],gs[:],up(gb[:],GRP),ALU.is_equal))
            then(V.tensor_tensor(gs[:],gs[:],lead(ig[:],TT),ALU.mult))
            then(V.tensor_reduce(gi[:],gs[:],AX.X,ALU.min))
            then(V.tensor_tensor(goh[:],lead(ig[:],TT),up(gi[:],GRP),ALU.is_equal))
            gflat=goh[:].rearrange("p t g -> p (t g)")
            for q in range(2):
                then(V.tensor_tensor(v8(oh[:,q]),v8(oh[:,q]),up(gflat,EPG),ALU.mult))
                then(V.tensor_tensor(t8[:],oh[:,q],aff[:],ALU.mult))
                then(V.tensor_reduce(a12[:,q],t8[:],AX.X,ALU.add))
            then(V.tensor_tensor(asum[:],a12[:,0],a12[:,1],ALU.add))
            then(V.reciprocal(asum[:],asum[:]))
            for q in range(2): then(V.tensor_tensor(gates[:,q],a12[:,q],asum[:],ALU.mult))
            V.tensor_tensor(M[:],oh[:,0],oh[:,1],ALU.add).then_inc(chosen,1)
            dve.wait_ge(ranked,1)
            then(V.memset(carry[:,0],0.0))
            for t in range(TT):
                then(V.tensor_tensor(carry[:,t+1],carry[:,t],ps[:,1,t*NE:(t+1)*NE],ALU.add))
            then(V.tensor_tensor(cmp[:],up(carry[:,TT],S//128),lead(mi[:],NE),ALU.is_gt))
            then(V.tensor_reduce(nt[:],cmp[:],AX.X,ALU.add))
            then(V.tensor_tensor_scan(end[:],one[:],nt[:],0.0,ALU.mult,ALU.add))
            then(V.tensor_tensor(base[:],end[:],nt[:],ALU.subtract))
            then(V.tensor_scalar(base[:],base[:],128.0,None,ALU.mult))
            then(V.tensor_tensor(M[:],carry[:,0:TT],lead(base[:],TT),ALU.add))
            then(V.tensor_tensor(M[:].rearrange("p t e -> p (t e)"),M[:].rearrange("p t e -> p (t e)"),ps[:,0],ALU.add))
            for q in range(2):
                then(V.tensor_tensor(t8[:],oh[:,q],M[:],ALU.mult))
                then(V.tensor_reduce(sf[:,q],t8[:],AX.X,ALU.add))
            V.tensor_copy(slots[:],sf[:]).then_inc(slotted,1)
            ebc=end[0:1].rearrange("p (o e) -> p o e",o=1).to_broadcast([1,MT_ALL,NE]); tbc=ti[:].rearrange("p (t o) -> p t o",o=1).to_broadcast([1,MT_ALL,NE])
            then(V.tensor_tensor(tc[:],ebc,tbc,ALU.is_le))
            then(V.tensor_reduce(te[:],tc[:],AX.X,ALU.add))
            then(V.tensor_scalar(te[:],te[:],float(NE-1),None,ALU.min))
            then(V.tensor_copy(tile_expert[:],te[:]))
            then(V.memset(new_expert[:,0:1],1))
            then(V.tensor_scalar(ti[:],ti[:],end[0:1,NE-1:NE],None,ALU.is_lt))
            then(V.tensor_tensor(tf[:,1:],te[:,1:],te[:,0:MT_ALL-1],ALU.is_gt))
            then(V.tensor_tensor(new_expert[:,1:],tf[:,1:],ti[:,1:],ALU.mult))
            then(V.tensor_copy(tiles_used[:,0:1],end[0:1,NE-1:NE]))
            then(V.tensor_scalar(tiles_used[:,1:2],end[0:1,NE-1:NE],-1.0,None,ALU.add))
            then(V.tensor_scalar(tiles_used[:,2:3],end[0:1,NE-1:NE],-1.0,float(MT_ALL-1),ALU.mult,ALU.add))

def experts(nc, xn, ffn_cols, mod, w_gate_up, w_down, token_of_slot, tile_expert, new_expert, tiles_used, ys):
    KF=FF//128; GC=8
    yst=ys.rearrange("(t p) d -> t p d",p=128)
    wgv=w_gate_up.rearrange("l e (k p) n -> p (l e k) n",p=128); wdv=w_down.rearrange("l e (k p) n -> p (l e k) n",p=128)
    with ExitStack() as ctx:
        sb=lambda n,s,d=F32: ctx.enter_context(nc.sbuf_tensor("ex_"+n,s,d))
        sem=semaphores(nc,ctx,"ex")
        wg=sb("w_gate_up",[128,KD,2*FF]); wd=sb("w_down",[128,KF,D]); xg=sb("x",[128,2,D]); xT=sb("xT",[128,2,KD,128]); g2=sb("gate2",[128,D]); idx=sb("token_idx",[128,MT_ALL],I32); ic=sb("tile_idx",[128,2],I32)
        sg=sb("sigmoid",[128,FF]); gu=sb("gate_sig",[128,FF]); a=sb("act",[128,FF]); aT=sb("actT",[128,KF,128]); yo=sb("y",[128,D]); zero=sb("zero",[128,512]); ident=sb("ident",[128,128])
        ps=ctx.enter_context(nc.psum_tensor("ex_ps",[128,8,512],F32)); GU,TR,DN=0,2,4
        made=sem("made"); rows=sem("rows_loaded"); wg_l=[sem(f"wg_loaded{i}") for i in range(GC)]; wd_l=[sem(f"wd_loaded{i}") for i in range(KF)]; wg_used=sem("wg_used"); wd_used=sem("wd_used")
        idx_ready=sem("idx_ready"); pool_waited=sem("pool_waited"); act_waited=sem("act_waited"); x_l=[sem(f"x_loaded{j}") for j in range(2)]; x_turned=sem("x_turned"); x_part=sem("x_part_turned"); xT_act=sem("xT_act"); xT_dve=sem("xT_dve"); gu_ready=sem("gu_ready"); sig=sem("sig_ready"); gated=sem("gated"); a_ready=sem("act_ready")
        a_turned=sem("act_turned"); aT_ready=sem("actT_ready"); dn_ready=sem("down_ready"); y_ready=sem("y_ready"); y_st=sem("y_stored"); zero_st=sem("zeros_stored")
        block=ctx.enter_context(nc.Block())
        def tiles(eng,step,last,reg):
            step(0,0,True)
            used=eng.value_load(tiles_used[0:1,0:1],min_val=1,max_val=MT)
            with eng.Fori(0,(MT-1)//2) as g:
                for j,d in ((1,1),(0,2)):
                    t=g*2+d
                    with eng.If(t<used): step(t,j,False)
            last(used,eng.value_load(tiles_used[0:1,1:2],min_val=0,max_val=MT-1))
        @block.sync
        def _(sp):
            with nc.allow_non_contiguous_dma(reason="a slot's token is one word"):
                sp.dma_start(idx[:],token_of_slot.rearrange("(t p) o -> p (t o)",p=128)).then_inc(rows,16)
            sp.dma_start(g2[:],mod[:,5*D:6*D].to_broadcast([128,D])).then_inc(rows,16)
            def weights(t,pieces,piece_size,used,w_sb,w_view,loaded,kept):
                e=sp.value_load(tile_expert[0:1,bass.ds(t,1)],min_val=0,max_val=NE-1)
                def each(load):
                    for i in range(pieces):
                        sp.wait_ge(used,t*pieces+(i+1))
                        k=slice(i*piece_size,(i+1)*piece_size)
                        if load: sp.dma_start(w_sb[:,k],w_view[:,bass.ds(e*(pieces*piece_size)+i*piece_size,piece_size)]).then_inc(loaded[i],16)
                        else: sp.sem_inc(loaded[i],16)
                if not kept: each(True)
                else:
                    fresh=sp.value_load(new_expert[0:1,bass.ds(t,1)],min_val=0,max_val=1)
                    with sp.If(fresh>0): each(True)
                    with sp.If(fresh<1): each(False)
            gate_up_w=lambda t,kept: weights(t,GC,KD//GC,wg_used,wg,wgv,wg_l,kept)
            down_w=lambda t,kept: weights(t,KF,1,wd_used,wd,wdv,wd_l,kept)
            gate_up_w(0,False)
            def step(t,j,first):
                if first: down_w(0,False)
                gate_up_w(t+1,True)
                if not first: down_w(t,True)
            tiles(sp,step,lambda used,final: None,None)
        @block.gpsimd
        def _(pool):
            identity_tile(nc,pool,ident,made)
            pool.wait_ge(rows,32)
            def gather(t,j,n):
                pool.tensor_copy(ic[:,j:j+1],idx[:,bass.ds(t,1)]).then_inc(idx_ready,1)
                pool.wait_ge(idx_ready,t+1); pool.sem_inc(pool_waited,1)
                pool.indirect_dma_start(out=xg[:,j],out_offset=None,in_=xn,in_offset=bass.IndirectOffsetOnAxis(ap=ic[:,j:j+1],axis=0)).then_inc(x_l[j],16)
            gather(0,0,0)
            pool.memset(zero[:],0.0).then_inc(made,1)
            pool.wait_ge(made,3)
            unused=pool.value_load(tiles_used[0:1,2:3],min_val=0,max_val=MT_ALL-2)
            def clear(t): pool.dma_start(yst[t].rearrange("p (r n) -> p r n",n=512),zero[:].rearrange("p (o n) -> p o n",o=1).to_broadcast([128,4,512])).then_inc(zero_st,16)
            clear(MT_ALL-1)
            with pool.Fori(0,MT_ALL-2) as u:
                with pool.If(u<unused): clear((MT_ALL-2)-u)
            def step(t,j,first):
                pool.wait_ge(x_turned,t)
                gather(t+1,1-j,0)
            def last(used,_):
                pool.wait_ge(x_turned,used+1)
                pool.wait_ge(zero_st,unused*16+16); pool.sem_inc(pool_waited,1)
            tiles(pool,step,last,None)
        @block.tensor
        def _(pe):
            pe.wait_ge(made,2)
            pe.sem_inc(wg_used,GC); pe.sem_inc(wd_used,KF)
            def turn_x(t,j,n2):
                pe.wait_ge(x_l[j],n2)
                if not (isinstance(t,int) and t==0): pe.wait_ge(aT_ready,t-1)
                for i in range(4):
                    pe.wait_ge((xT_act,xT_dve)[i%2],t*2+(i//2+1))
                    for q in range(4):
                        m=nc.tensor.transpose(ps[:,TR+i%2,q*128:q*128+128],xg[:,j,(4*i+q)*128:(4*i+q+1)*128],ident[:])
                    if i<3: m.then_inc(x_part,1)
                    else: m.then_inc(x_turned,1)
            def gate_up(t,j):
                pe.wait_ge(xT_act,t*2+3); pe.wait_ge(xT_dve,t*2+3)
                pe.wait_ge(gated,t)
                pe.wait_ge(a_ready,t)
                for i in range(GC):
                    pe.wait_ge(wg_l[i],t*16+16)
                    for k in (2*i,2*i+1):
                        for n in range(2):
                            m=nc.tensor.matmul(ps[:,GU+n],xT[:,j,k],wg[:,k,n*512:(n+1)*512],start=(k==0),stop=(k==KD-1))
                    m.then_inc(wg_used,1)
            def turn_a(t):
                pe.wait_ge(a_ready,t+1)
                pe.wait_ge(xT_act,t*2+5)
                for k in range(KF):
                    m=nc.tensor.transpose(ps[:,TR,k*128:(k+1)*128],a[:,k*128:(k+1)*128],ident[:])
                m.then_inc(a_turned,1)
            def down(t):
                pe.wait_ge(aT_ready,t+1); pe.wait_ge(y_ready,t*4+1)
                for k in range(KF):
                    pe.wait_ge(wd_l[k],t*16+16)
                    for n in range(4):
                        m=nc.tensor.matmul(ps[:,DN+n],aT[:,k],wd[:,k,n*512:(n+1)*512],start=(k==0),stop=(k==KF-1))
                        if n==3: m.then_inc(wd_used,1)
            def step(t,j,first):
                if first: turn_x(0,0,16)
                gate_up(t,j)
                n2=16 if first else (t+1-(1-j))*8+16
                turn_x(t+1,1-j,n2)
                if not first: down(t-1)
                turn_a(t)
            tiles(pe,step,lambda used,final: down(final),None)
        @block.scalar
        def _(act):
            act.sem_inc(y_st,16)
            act.sem_inc(xT_act,1)
            def copy_x(t,j,part):
                for i in (0,2):
                    if i==0: act.wait_ge(wg_used,t*GC); act.wait_ge(x_part,t*3+1)
                    else: act.wait_ge(x_part,t*3+3)
                    for k in range(4*i,4*i+4):
                        m=nc.scalar.activation(xT[:,j,k],ps[:,TR,(k-4*i)*128:(k-4*i)*128+128],ACT.Identity,scale=ffn_cols[:,k:k+1],bias=ffn_cols[:,KD+k:KD+k+1])
                    m.then_inc(xT_act,1)
            def store(t):
                act.wait_ge(y_ready,t*4+4+1)
                act.dma_start(yst[t],yo[:]).then_inc(y_st,16)
            def step(t,j,first):
                if first: copy_x(0,0,0)
                act.wait_ge(wg_used,t*GC+2*GC); act.wait_ge(gated,t)
                nc.scalar.activation(sg[:],ps[:,GU],ACT.Sigmoid).then_inc(sig,1)
                copy_x(t+1,1-j,0)
                act.wait_ge(a_turned,t+1); act.wait_ge(wd_used,t*KF+KF)
                nc.scalar.copy(aT[:].rearrange("p k n -> p (k n)"),ps[:,TR]).then_inc(aT_ready,1)
                if not first: store(t-1)
            def last(used,final):
                store(final)
                act.wait_ge(y_st,used*16+16); act.sem_inc(act_waited,1)
            tiles(act,step,last,None)
        @block.vector
        def _(dve):
            dve.sem_inc(y_ready,1)
            dve.sem_inc(xT_dve,1)
            dve.wait_ge(rows,32)
            def copy_x(t,j):
                for i in (1,3):
                    if i==1: dve.wait_ge(x_part,t*3+2); dve.wait_ge(wg_used,t*GC)
                    else: dve.wait_ge(x_turned,t+1)
                    for k in range(4*i,4*i+4):
                        m=nc.vector.tensor_scalar(xT[:,j,k],ps[:,TR+1,(k-4*i)*128:(k-4*i)*128+128],ffn_cols[:,k:k+1],ffn_cols[:,KD+k:KD+k+1],ALU.mult,ALU.add)
                    m.then_inc(xT_dve,1)
            def y_out(t):
                dve.wait_ge(wd_used,t*KF+2*KF); dve.wait_ge(y_st,t*16+16)
                for n in range(4):
                    nc.vector.tensor_tensor(yo[:,n*512:(n+1)*512],ps[:,DN+n],g2[:,n*512:(n+1)*512],ALU.mult).then_inc(y_ready,1)
            def step(t,j,first):
                if first: copy_x(0,0)
                dve.wait_ge(sig,t+1)
                nc.vector.tensor_tensor(gu[:],ps[:,GU],sg[:],ALU.mult).then_inc(gated,1)
                dve.wait_ge(gated,t+1); dve.wait_ge(a_turned,t)
                nc.vector.tensor_tensor(a[:],ps[:,GU+1],gu[:],ALU.mult).then_inc(a_ready,1)
                copy_x(t+1,1-j)
                if not first: y_out(t-1)
            tiles(dve,step,lambda used,final: y_out(final),None)
    
def combine(nc, x1, ys, slots, gates, final_g, out):
    x1t=x1.rearrange("(t p) d -> t p d",p=128); ot=out.rearrange("b (t p) d -> (b t) p d",p=128)
    NB=2
    with ExitStack() as ctx:
        sb=lambda n,s,d=F32: ctx.enter_context(nc.sbuf_tensor("co_"+n,s,d))
        sem=semaphores(nc,ctx,"co")
        xb=sb("x",[128,NB,D]); y1=sb("y1",[128,NB,D]); y2=sb("y2",[128,NB,D]); g=sb("final_g",[128,D]); ic=sb("slot_idx",[128,2,NB],I32); ss=sb("ss",[128,NB]); eps=sb("eps",[128,1])
        g_l=sem("g_loaded"); made=sem("made"); x_l=[sem(f"x_loaded{j}") for j in range(NB)]; y_l=[sem(f"y_loaded{j}") for j in range(NB)]
        y1s=sem("y1_scaled"); ysum=sem("y_sum"); xs=sem("x_sum"); sse=sem("ss_steps"); done=sem("out_ready"); st=[sem(f"stored{j}") for j in range(NB)]
        block=ctx.enter_context(nc.Block())
        def loop(eng,f):
            with eng.Fori(0,TT//NB) as q:
                for j in range(NB): f(q,q*NB+j,j)
        @block.sync
        def _(sp):
            sp.dma_start(g[:],final_g.rearrange("(o d) -> o d",o=1).to_broadcast([128,D])).then_inc(g_l,16)
            for j in range(NB): sp.dma_start(xb[:,j],x1t[j]).then_inc(x_l[j],16)
            def store(t,j):
                sp.wait_ge(done,t+1)
                sp.dma_start(ot[t],y1[:,j]).then_inc(st[j],16)
            with sp.Fori(0,TT//NB-1) as q:
                for j in range(NB):
                    store(q*NB+j,j)
                    sp.dma_start(xb[:,j],x1t[q*NB+(j+NB)]).then_inc(x_l[j],16)
            for j in range(NB): store(TT-NB+j,j)
            for j in range(NB): sp.wait_ge(st[j],16*TT//NB)
        @block.gpsimd
        def _(pool):
            pool.memset(eps[:],EPS).then_inc(made,1)
            def f(q,t,j):
                pool.wait_ge(st[j],q*16); 
                pool.indirect_dma_start(out=y1[:,j],out_offset=None,in_=ys,in_offset=bass.IndirectOffsetOnAxis(ap=slots[:,0,t:t+1],axis=0)).then_inc(y_l[j],16)
                pool.indirect_dma_start(out=y2[:,j],out_offset=None,in_=ys,in_offset=bass.IndirectOffsetOnAxis(ap=slots[:,1,t:t+1],axis=0)).then_inc(y_l[j],16)
            for t in range(TT): f(t//NB,t,t%NB)
        @block.scalar
        def _(act):
            act.wait_ge(made,1)
            def f(q,t,j):
                act.wait_ge(y_l[j],q*32+32)
                nc.scalar.activation(y1[:,j],y1[:,j],ACT.Copy,scale=gates[:,0,bass.ds(t,1)]).then_inc(y1s,1)
                act.wait_ge(xs,t+1)
                nc.scalar.activation(y2[:,j],xb[:,j],ACT.Square,scale=float(D)**-0.5,accum_out=ss[:,j:j+1]).then_inc(sse,1)
                act.wait_ge(sse,t*3+1)
                nc.scalar.activation(ss[:,j:j+1],ss[:,j:j+1],ACT.Ln,bias=eps[:]).then_inc(sse,1)
                act.wait_ge(sse,t*3+2)
                nc.scalar.activation(ss[:,j:j+1],ss[:,j:j+1],ACT.Exp,scale=-0.5).then_inc(sse,1)
            loop(act,f)
        @block.vector
        def _(dve):
            dve.wait_ge(g_l,16)
            def f(q,t,j):
                dve.wait_ge(y1s,t+1)
                nc.vector.scalar_tensor_tensor(out=y1[:,j],in0=y2[:,j],scalar=gates[:,1,bass.ds(t,1)],in1=y1[:,j],op0=ALU.mult,op1=ALU.add).then_inc(ysum,1)
                dve.wait_ge(ysum,t+1); dve.wait_ge(x_l[j],q*16+16)
                nc.vector.tensor_tensor(xb[:,j],xb[:,j],y1[:,j],ALU.add).then_inc(xs,1)
                dve.wait_ge(sse,t*3+3)
                nc.vector.scalar_tensor_tensor(out=y1[:,j],in0=xb[:,j],scalar=ss[:,j:j+1],in1=g[:],op0=ALU.mult,op1=ALU.mult).then_inc(done,1)
            loop(dve,f)

def hybrid_layer(nc, x, c, ada_w, ada_b, mix_norm_g, w_in, cq_norm_g, ckv_norm_g, w_uq, w_uk, w_uv, w_qidx,
                 mlstm_i_b, mlstm_f_b, mlstm_norm_g, w_out, ffn_norm_g, router_w, router_b, w_gate_up, w_down,
                 final_norm_g, out):
    scratch = lambda name, shape, dtype=F32: nc.dram_tensor(name, shape, dtype).ap()
    mod = scratch("mod", [1, 6 * D])
    h_tiles = scratch("h_tiles", [TT, 128, KD, 128])
    z = scratch("z", [S, D_IN])
    y = scratch("y", [S, D])
    x1 = scratch("x1", [S, D])
    xn = scratch("x1_normed", [S, D])
    token_of_slot = scratch("token_of_slot", [SLOTS_, 1], I32)
    ys = scratch("ys", [SLOTS_, D])
    modulation(nc, c, ada_w, ada_b, mod)
    in_projection(nc, x, mod, mix_norm_g, w_in, z, h_tiles)
    dsa(nc, z, h_tiles, w_in, cq_norm_g, ckv_norm_g, w_uq, w_uk, w_uv, w_qidx, y)
    mlstm(nc, z, mlstm_i_b, mlstm_f_b, mlstm_norm_g, y)
    with ExitStack() as ctx:
        sb = lambda n, s, d=F32: ctx.enter_context(nc.sbuf_tensor(n, s, d))
        logits = sb("logits", [128, TT, NE])
        slots = sb("slots", [128, 2, TT], I32)
        gates = sb("gates", [128, 2, TT])
        tile_expert = sb("tile_expert", [1, MT_ALL], I32)
        new_expert = sb("new_expert", [1, MT_ALL], I32)
        ffn_cols = sb("ffn_cols", [128, 2 * KD])
        tiles_used = sb("tiles_used", [1, 3], I32)
        out_projection(nc, y, x, mod, w_out, ffn_norm_g, router_w, x1, xn, ffn_cols, logits)
        routing(nc, logits, router_b, token_of_slot, slots, gates, tile_expert, new_expert, tiles_used)
        experts(nc, xn, ffn_cols, mod, w_gate_up, w_down, token_of_slot, tile_expert, new_expert, tiles_used, ys)
        combine(nc, x1, ys, slots, gates, final_norm_g, out)


_INS = ["x", "c", "ada_w", "ada_b", "mix_norm_g", "w_in", "cq_norm_g", "ckv_norm_g", "w_uq", "w_uk", "w_uv", "w_qidx",
        "mlstm_i_b", "mlstm_f_b", "mlstm_norm_g", "w_out", "ffn_norm_g", "router_w", "router_b", "w_gate_up", "w_down",
        "final_norm_g"]
_OUTS = [((1, S, D), "float32")]


def kernel(**inputs):
    import numpy as _np
    import concourse.bacc as _bacc
    from concourse import mybir as _mybir
    from concourse.bass_utils import run_bass_kernel_spmd as _run

    nc = _bacc.Bacc("TRN2", target_bir_lowering=False, num_devices=1)
    arrays, args = {}, []
    for name in _INS:
        a = _np.ascontiguousarray(inputs[name])
        arrays[f"in_{name}_dram"] = a
        args.append(nc.dram_tensor(f"in_{name}_dram", a.shape, _mybir.dt.from_np(a.dtype), kind="ExternalInput").ap())
    for i, (shape, dtype) in enumerate(_OUTS):
        dt = _mybir.dt.from_np(_np.dtype(dtype))
        args.append(nc.dram_tensor(f"out_{i}_dram", shape, dt, kind="ExternalOutput").ap())
    hybrid_layer(nc, *args)
    r = _run(nc, [arrays], core_ids=[0])
    got = tuple(r.results[0][f"out_{i}_dram"] for i in range(len(_OUTS)))
    return got[0]
```

```python
from contextlib import ExitStack

import concourse.bass as bass
from concourse import mybir
F32=mybir.dt.float32
ALU=mybir.AluOpType
ACT=mybir.ActivationFunctionType
AX=mybir.AxisListType
D=2048
KD=16

def semaphores(nc, ctx, stage):
    held = []

    def close():
        nc.clear_and_free_semaphores(held)
        nc.all_engine_barrier()

    def sem(name):
        held.append(nc.alloc_semaphore(f"{stage}_{name}"))
        return held[-1]

    ctx.callback(close)
    return sem

MB=512
def ada_blocks(ada_w): return ada_w.rearrange("l (p k) n -> p (l k) n", k=KD)

def modulation(nc, c, ada_w, ada_b, mod, s_col):
    N=MB
    NB=2*D//N
    SLOTS=4
    w_view=ada_blocks(ada_w)
    with ExitStack() as ctx:
        sb=lambda n, s, d=F32: ctx.enter_context(nc.sbuf_tensor("mod_"+n, s, d))
        sem=semaphores(nc, ctx, "mod")
        c_col=sb("c_col", [128, KD])
        e_col=sb("e_col", [128, KD])
        w=sb("ada_w_ring", [128, SLOTS, KD, N])
        row=sb("mod_row", [1, 2*D])
        acc=ctx.enter_context(nc.psum_tensor("mod_mod_acc", [128, SLOTS, 512], F32))
        c_loaded=sem("c_loaded")
        b_loaded=sem("b_loaded")
        w_loaded=[sem(f"w_loaded{i}") for i in range(SLOTS)]
        w_used=sem("w_used")
        acc_free=sem("acc_free")
        c_exp=sem("c_exp")
        c_step=sem("c_step")
        mod_stored=sem("mod_stored")
        block=ctx.enter_context(nc.Block())
        @block.sync
        def _(sp):
            sp.dma_start(c_col[:], c.rearrange("b (p k) -> p (b k)", k=KD)).then_inc(c_loaded, 16)
            sp.dma_start(row[:], ada_b[:, 0:2*D]).then_inc(b_loaded, 16)
            for j in range(SLOTS):
                sp.dma_start(w[:, j], w_view[:, :, j*N:(j+1)*N]).then_inc(w_loaded[j], 16)
            with sp.Fori(1, NB//SLOTS) as g:
                for j in range(SLOTS):
                    sp.wait_ge(w_used, g*SLOTS+(j-SLOTS+1))
                    sp.dma_start(w[:, j], w_view[:, :, bass.ds(g*(SLOTS*N)+j*N, N)]).then_inc(w_loaded[j], 16)
            sp.wait_ge(acc_free, NB+SLOTS)
            sp.dma_start(mod[:, 0:2*D], row[:]).then_inc(mod_stored, 16)
            sp.wait_ge(mod_stored, 16)
        @block.scalar
        def _(act):
            act.wait_ge(c_loaded, 16)
            nc.scalar.activation(e_col[:], c_col[:], ACT.Exp, scale=-1.0).then_inc(c_exp, 1)
        @block.vector
        def _(dve):
            dve.wait_ge(c_exp, 1)
            nc.vector.tensor_scalar_add(e_col[:], e_col[:], 1.0).then_inc(c_step, 1)
            dve.wait_ge(c_step, 1)
            nc.vector.reciprocal(e_col[:], e_col[:]).then_inc(c_step, 1)
            dve.wait_ge(c_step, 2)
            nc.vector.tensor_tensor(s_col[:], e_col[:], c_col[:], ALU.mult).then_inc(c_step, 1)
            dve.wait_ge(b_loaded, 16)
            dve.sem_inc(acc_free, SLOTS)
            with dve.Fori(0, NB//SLOTS) as g:
                for j in range(SLOTS):
                    dve.wait_ge(w_used, g*SLOTS+(j+1))
                    nc.vector.tensor_tensor(row[:, bass.ds(g*(SLOTS*N)+j*N, N)], acc[0:1, j], row[:, bass.ds(g*(SLOTS*N)+j*N, N)], ALU.add).then_inc(acc_free, 1)
        @block.tensor
        def _(pe):
            pe.wait_ge(c_step, 3)
            with pe.Fori(0, NB//SLOTS) as g:
                for j in range(SLOTS):
                    pe.wait_ge(w_loaded[j], g*16+16)
                    pe.wait_ge(acc_free, g*SLOTS+(j+1))
                    for k in range(KD):
                        mm=nc.tensor.matmul(acc[0:1, j], s_col[:, k:k+1], w[:, j, k], start=(k==0), stop=(k==KD-1))
                    mm.then_inc(w_used, 1)

S=2048
TT=S//128
D_IN=3920
ZN=420
ZB=2
ZA=ZN*ZB
ZN2=440
ZB2=(D_IN-ZA)//ZN2
EPS=1e-6

def identity_tile(nc, pool, ident, made):
    pool.memset(ident[:], 0.0).then_inc(made, 1)
    pool.wait_ge(made, 1)
    pool.affine_select(out=ident[:], in_=ident[:], compare_op=ALU.not_equal, fill=1.0, base=0, pattern=[[-1, 128]], channel_multiplier=1).then_inc(made, 1)

def in_projection(nc, x, mod, norm_g, w_in, z, h_tiles):
    xt=x.rearrange("b (t p) d -> (b t) p d", p=128)
    zt=z.rearrange("(t p) n -> t p n", p=128)
    wv=w_in.rearrange("l (k p) n -> p (l k) n", p=128)
    modv=mod.rearrange("l (s k p) -> s (l k) p", s=6, p=128)
    with ExitStack() as ctx:
        sb=lambda n, s, d=F32: ctx.enter_context(nc.sbuf_tensor("in_"+n, s, d))
        sem=semaphores(nc, ctx, "in")
        hT=sb("hT", [128, KD, S])
        w=sb("w_in_ring", [128, 2, KD, ZN])
        ident=sb("ident", [128, 128])
        rows=sb("param_rows", [3*KD, 128])
        cols=sb("param_cols", [128, 3*KD])
        xb=w[:, 1].rearrange("p k n -> p (k n)")[:, 0:2*D].rearrange("p (s d) -> p s d", s=2)
        stage=sb("z_stage", [128, 4, ZN])
        ss=sb("sum_squares", [128, 2])
        rstd=sb("rstd", [128, 2])
        eps=sb("eps", [128, 1])
        squares_out=sb("squares", [128, D], mybir.dt.bfloat16)
        FREE=2
        acc=ctx.enter_context(nc.psum_tensor("in_acc", [128, 8, 512], F32))
        ZBK=4
        xn=xb
        params_loaded=sem("params_loaded")
        ident_made=sem("ident_made")
        params_turned=sem("params_turned")
        params_ready=sem("params_ready")
        x_loaded=[sem(f"x_loaded{i}") for i in range(2)]
        ss_ready=sem("ss_ready")
        rms_ready=sem("rms_ready")
        rstd_ready=sem("rstd_ready")
        xn_ready=sem("xn_ready")
        turned=sem("turned")
        hT_act=sem("hT_act")
        hT_dve=sem("hT_dve")
        w_loaded=[sem(f"w_loaded{i}") for i in range(2)]
        z_acc=sem("z_acc")
        h_stored=sem("h_stored")
        z_act=sem("z_act")
        z_dve=sem("z_dve")
        stored=[sem(f"z_stored{i}") for i in range(4)]
        block=ctx.enter_context(nc.Block())
        HK=KD//2
        @block.gpsimd
        def _(pool):
            identity_tile(nc, pool, ident, ident_made)
            pool.memset(eps[:], EPS).then_inc(ident_made, 1)
        @block.sync
        def _(sp):
            for s in stored: sp.sem_inc(s, 16)
            sp.dma_start(rows[0:KD], norm_g.rearrange("l (k p) -> (l k) p", p=128)).then_inc(params_loaded, 16)
            sp.dma_start(rows[KD:2*KD], modv[1]).then_inc(params_loaded, 16)
            sp.dma_start(rows[2*KD:3*KD], modv[0]).then_inc(params_loaded, 16)
            def load(t, j): sp.dma_start(xb[:, j], xt[t]).then_inc(x_loaded[j], 16)
            load(0, 0)
            load(1, 1)
            def tile(t, half, j, jj, more):
                if more:
                    sp.wait_ge(turned, t+2)
                    load(t+2, j)
                sp.wait_ge((z_act, z_dve)[j], half+(1+FREE))
                sp.dma_start(zt[t, :, 0:ZN], stage[:, jj]).then_inc(stored[jj], 16)
                sp.dma_start(h_tiles[t], hT[:, :, bass.ds(t*128, 128)]).then_inc(h_stored, 16)
            with sp.Fori(0, TT//4-1) as g:
                for q in range(4): tile(g*4+q, g*2+q//2, q%2, q, True)
            for q in range(4): tile(TT-4+q, TT//2-2+q//2, q%2, q, q<2)
            for m in range(TT):
                sp.wait_ge((z_act, z_dve)[m%2], TT//2+(m//2+1+FREE))
                sp.dma_start(zt[m, :, ZN:2*ZN], stage[:, m%4]).then_inc(stored[m%4], 16)
            sp.wait_ge(h_stored, 16*TT)
            for s in range(4): sp.wait_ge(stored[s], 16*ZB*TT//4+16)
        @block.scalar
        def _(act):
            act.sem_inc(hT_act, 1)
            act.dma_start(w[:, 0], wv[:, :, 0:ZN]).then_inc(w_loaded[0], 16)
            act.wait_ge(ident_made, 3)
            def squares(t, j):
                act.wait_ge(x_loaded[j], t*16+16)
                nc.scalar.activation(squares_out[:], xb[:, j], ACT.Square, accum_out=ss[:, j:j+1]).then_inc(ss_ready, 1)
            def root(t2, j):
                act.wait_ge(ss_ready, t2*2+j+1)
                nc.scalar.activation(rstd[:, j:j+1], ss[:, j:j+1], ACT.Sqrt, bias=eps[:], scale=1.0/D).then_inc(rms_ready, 1)
            def evac(t2, j):
                act.wait_ge(turned, t2*2+j+1+1)
                for k in range(HK):
                    i=nc.scalar.activation(hT[:, k, bass.ds(t2*256+j*128, 128)], acc[:, k//4, (k%4)*128:(k%4)*128+128], ACT.Identity, scale=cols[:, k:k+1], bias=cols[:, 2*KD+k:2*KD+k+1])
                i.then_inc(hT_act, 1)
            act.wait_ge(params_ready, 2)
            act.sem_inc(z_act, FREE)
            def z_evac(count, m, st):
                act.wait_ge(z_acc, count+1)
                act.wait_ge(stored[m%4], st*16+16)
                nc.scalar.copy(stage[:, m%4], acc[:, ZBK+m%4, 0:ZN]).then_inc(z_act, 1)
            def tile(g, q, z):
                t2=g*2+q//2
                j=q%2
                squares(t2, j)
                root(t2, j)
                evac(t2, j)
                if z and j==1: z_evac(g*4+(q-1), q-1, g)
            with act.Fori(0, TT//4) as g:
                for q in range(4): tile(g, q, True)
            act.wait_ge(turned, TT+1)
            act.dma_start(w[:, 1], wv[:, :, ZN:2*ZN]).then_inc(w_loaded[1], 16)
            for m in range(0, TT, 2): z_evac(TT+m, m, TT//4+m//4)
        @block.vector
        def _(dve):
            dve.sem_inc(hT_dve, 1)
            dve.wait_ge(params_turned, 1)
            nc.vector.tensor_copy(cols[:], acc[:, 0, 0:3*KD]).then_inc(params_ready, 1)
            dve.wait_ge(params_ready, 1)
            nc.vector.scalar_tensor_tensor(out=cols[:, 0:KD], in0=cols[:, KD:2*KD], scalar=1.0, in1=cols[:, 0:KD], op0=ALU.add, op1=ALU.mult).then_inc(params_ready, 1)
            dve.wait_ge(params_ready, 2)
            dve.sem_inc(z_dve, FREE)
            def z_evac(count, m, st):
                dve.wait_ge(z_acc, count+1)
                dve.wait_ge(stored[m%4], st*16+16)
                nc.vector.tensor_copy(stage[:, m%4], acc[:, ZBK+m%4, 0:ZN]).then_inc(z_dve, 1)
            def tile(g, q, z):
                t2=g*2+q//2
                j=q%2
                dve.wait_ge(rms_ready, t2*2+j+1)
                nc.vector.reciprocal(rstd[:, j:j+1], rstd[:, j:j+1]).then_inc(rstd_ready, 1)
                dve.wait_ge(rstd_ready, t2*2+j+1)
                nc.vector.tensor_scalar(xn[:, j], xb[:, j], rstd[:, j:j+1], None, ALU.mult).then_inc(xn_ready, 1)
                dve.wait_ge(turned, t2*2+j+1+1)
                for k in range(HK, KD):
                    i=nc.vector.tensor_scalar(hT[:, k, bass.ds(t2*256+j*128, 128)], acc[:, k//4, (k%4)*128:(k%4)*128+128], cols[:, k:k+1], cols[:, 2*KD+k:2*KD+k+1], ALU.mult, ALU.add)
                i.then_inc(hT_dve, 1)
                if z and j==0: z_evac(z_of(g, q-1), (q-1)%4, g if q else g-1)
            z_of=lambda g, q: g*4+q
            for q in range(4): tile(0, q, q>0)
            with dve.Fori(1, TT//4) as g:
                for q in range(4): tile(g, q, True)
            z_evac(TT-1, 3, TT//4-1)
            for m in range(1, TT, 2): z_evac(TT+m, m, TT//4+m//4)
        @block.tensor
        def _(pe):
            pe.sem_inc(turned, 1)
            pe.wait_ge(ident_made, 2)
            pe.wait_ge(params_loaded, 48)
            nc.tensor.transpose(acc[:, 0, 0:3*KD], rows[:], ident[0:3*KD, 0:3*KD]).then_inc(params_turned, 1)
            pe.wait_ge(params_ready, 1)
            def turn(t, j):
                pe.wait_ge(xn_ready, t+1)
                pe.wait_ge(hT_act, t+1)
                pe.wait_ge(hT_dve, t+1)
                for k in range(KD):
                    m=nc.tensor.transpose(acc[:, k//4, (k%4)*128:(k%4)*128+128], xn[:, j, k*128:(k+1)*128], ident[:])
                m.then_inc(turned, 1)
            def multiply(n, m):
                pe.wait_ge((z_act, z_dve)[m%2], n*(TT//2)+m//2+1)
                for k in range(KD):
                    mm=nc.tensor.matmul(acc[:, ZBK+m%4, 0:ZN], hT[:, k, m*128:(m+1)*128], w[:, n, k], start=(k==0), stop=(k==KD-1))
                mm.then_inc(z_acc, 1)
            turn(0, 0)
            pe.wait_ge(w_loaded[0], 16)
            for t in range(TT):
                if t+1<TT: turn(t+1, (t+1)%2)
                else:
                    pe.wait_ge(hT_act, TT+1)
                    pe.wait_ge(hT_dve, TT+1)
                multiply(0, t)
            pe.wait_ge(w_loaded[1], 16)
            for t in range(TT): multiply(1, t)

NH=4
DK=128
DV=256
DVA=DV+1
C=128
NC=S//C
Z_CQ, Z_CKV, Z_KI, Z_WI, Z_MQ, Z_MK, Z_MV, Z_MO, Z_MI, Z_MF=0, 512, 768, 832, 840, 1352, 1864, 2888, 3912, 3916
BIG=1e30

def mlstm(nc, z, i_b, f_b, norm_g, y):
    zt=z.rearrange("(t p) n -> p t n", p=128)
    zc=z.rearrange("(t p) n -> t p n", p=128)
    yc=y.rearrange("(t p) n -> t p n", p=128)
    with ExitStack() as ctx:
        sb=lambda n, s, d=F32: ctx.enter_context(nc.sbuf_tensor("ml_"+n, s, d))
        sem=semaphores(nc, ctx, "ml")
        ident=sb("ident", [128, 128])
        sel=sb("head_rows", [NH, NH, 128])
        mask=sb("future_mask", [128, 128])
        A=sb("A", [NH, S])
        gcols=sb("gate_cols", [128, 4, NC, NH])
        wold=sb("wold", [128, NH, NC])
        gbc=sb("norm_g_rows", [128, NH*DV])
        with ExitStack() as gctx:
            gsb=lambda n, s, d=F32: gctx.enter_context(nc.sbuf_tensor("mlg_"+n, s, d))
            gsem=semaphores(nc, gctx, "mlg")
            zg=gsb("gates_in", [128, NC, 8])
            bias=gsb("gate_bias", [NH, 2])
            I=gsb("I", [NH, S])
            Fg=gsb("F", [NH, S])
            E=gsb("E", [NH, S])
            L=gsb("L", [NH, S])
            b=gsb("b", [NH, S])
            reset=gsb("reset", [NH, S])
            step=gsb("step", [NH, S])
            a=gsb("a", [NH, S])
            Mp=gsb("m_prev", [NH, NC])
            Wo=gsb("w_old", [NH, NC])
            win=gsb("w_inter", [NH, S])
            en=gsb("exp_neg_m", [NH, S])
            ws=gsb("w_s", [NH, S])
            ps=gctx.enter_context(nc.psum_tensor("ml_gates_ps", [128, 8, 512], F32))
            loaded=gsem("gates_loaded")
            made=gsem("consts_made")
            turned=gsem("gates_turned")
            biased=gsem("gates_biased")
            absd=gsem("abs_ready")
            ln1p=gsem("ln_ready")
            v=gsem("vector_done")
            expd=gsem("exp_ready")
            cols_ps=gsem("cols_in_psum")
            cdone=gsem("cols_copied")
            block=gctx.enter_context(nc.Block())
            ch=lambda t: t[:].rearrange("h (c j) -> h c j", j=C)
            @block.sync
            def _(sp):
                with nc.allow_non_contiguous_dma(reason="short rows of gates"):
                    sp.dma_start(zg[:], zt[:, :, Z_MI:Z_MI+8]).then_inc(loaded, 16)
                    sp.dma_start(bias[:, 0:1], i_b.rearrange("l h -> h l")).then_inc(loaded, 16)
                    sp.dma_start(bias[:, 1:2], f_b.rearrange("l h -> h l")).then_inc(loaded, 16)
                sp.dma_start(gbc[:], norm_g.rearrange("l h v -> l (h v)").to_broadcast([128, NH*DV])).then_inc(loaded, 16)
                sp.wait_ge(loaded, 64)
            @block.gpsimd
            def _(pool):
                identity_tile(nc, pool, ident, made)
                pool.memset(mask[:], 0.0).then_inc(made, 1)
                pool.memset(sel[:], 1.0).then_inc(made, 1)
                pool.wait_ge(made, 4)
                pool.affine_select(out=mask[:], in_=mask[:], compare_op=ALU.is_ge, fill=BIG, base=0, pattern=[[1, 128]], channel_multiplier=-1).then_inc(made, 1)
                pool.affine_select(out=sel[:], in_=sel[:], compare_op=ALU.is_equal, fill=0.0, base=0, pattern=[[-1, NH], [0, 128]], channel_multiplier=1).then_inc(made, 1)
                pool.memset(reset[:], 1.0).then_inc(made, 1)
                pool.memset(step[:], 0.0).then_inc(made, 1)
                pool.memset(Mp[:], 0.0).then_inc(made, 1)
                pool.wait_ge(made, 7)
                pool.memset(ch(reset)[:, :, 0:1], 0.0).then_inc(made, 1)
            @block.tensor
            def _(pe):
                pe.wait_ge(loaded, 64)
                pe.wait_ge(made, 10)
                for c in range(NC):
                    nc.tensor.transpose(ps[0:NH, c//4, (c%4)*128:(c%4)*128+128], zg[:, c, 0:4], ident[:])
                    t=nc.tensor.transpose(ps[0:NH, 4+c//4, (c%4)*128:(c%4)*128+128], zg[:, c, 4:8], ident[:])
                t.then_inc(turned, 1)
                pe.wait_ge(expd, 4)
                for q, r in enumerate((a, win, en, ws)):
                    for c in range(NC):
                        nc.tensor.transpose(ps[:, 0, (q*NC+c)*NH:(q*NC+c+1)*NH], r[:, c*C:(c+1)*C], ident[0:NH, 0:NH])
                for h in range(NH):
                    t=nc.tensor.matmul(ps[:, 1, h*NC:(h+1)*NC], sel[:, h], Wo[:], start=True, stop=True)
                t.then_inc(cols_ps, 1)
            @block.scalar
            def _(act):
                act.wait_ge(loaded, 64)
                act.wait_ge(turned, 1)
                nc.scalar.activation(I[:], ps[0:NH, 0:4].rearrange("h b n -> h (b n)"), ACT.Identity, bias=bias[:, 0:1]).then_inc(biased, 1)
                nc.scalar.activation(Fg[:], ps[0:NH, 4:8].rearrange("h b n -> h (b n)"), ACT.Identity, bias=bias[:, 1:2]).then_inc(biased, 1)
                act.wait_ge(biased, 2)
                nc.scalar.activation(E[:], Fg[:], ACT.Abs).then_inc(absd, 1)
                act.wait_ge(absd, 1)
                nc.scalar.activation(E[:], E[:], ACT.Exp, scale=-1.0).then_inc(ln1p, 1)
                act.wait_ge(ln1p, 1)
                nc.scalar.activation(L[:], E[:], ACT.Ln, bias=1.0).then_inc(ln1p, 1)
                act.wait_ge(v, 9)
                nc.scalar.activation(win[:], win[:], ACT.Exp).then_inc(expd, 1)
                act.wait_ge(v, 10)
                nc.scalar.activation(en[:], en[:], ACT.Exp, scale=-1.0).then_inc(expd, 1)
                act.wait_ge(v, 11)
                nc.scalar.activation(ws[:], ws[:], ACT.Exp).then_inc(expd, 1)
                act.wait_ge(v, 12)
                nc.scalar.activation(Wo[:], Wo[:], ACT.Exp).then_inc(expd, 1)
            @block.vector
            def _(dve):
                dve.wait_ge(ln1p, 2)
                dve.wait_ge(made, 10)
                nc.vector.scalar_tensor_tensor(out=L[:], in0=Fg[:], scalar=0.0, in1=L[:], op0=ALU.min, op1=ALU.subtract).then_inc(v, 1)
                dve.wait_ge(v, 1)
                nc.vector.tensor_tensor_scan(b[:], reset[:], L[:], 0.0, ALU.mult, ALU.add).then_inc(v, 1)
                dve.wait_ge(v, 2)
                nc.vector.tensor_tensor(a[:], I[:], b[:], ALU.subtract).then_inc(v, 1)
                nc.vector.tensor_copy(ch(step)[:, 1:NC, 0:1], ch(b)[:, 0:NC-1, C-1:C]).then_inc(v, 1)
                dve.wait_ge(v, 4)
                nc.vector.tensor_tensor_scan(A[:], step[:], a[:], 0.0, ALU.add, ALU.max).then_inc(v, 1)
                dve.wait_ge(v, 5)
                nc.vector.tensor_tensor(Mp[:, 1:NC], ch(b)[:, 0:NC-1, C-1], ch(A)[:, 0:NC-1, C-1], ALU.add).then_inc(v, 1)
                nc.vector.tensor_copy(Wo[:], ch(A)[:, :, C-1]).then_inc(v, 1)
                dve.wait_ge(v, 7)
                nc.vector.tensor_copy(reset[:, 0:1], b[:, 0:1]).then_inc(v, 1)
                nc.vector.tensor_tensor(ch(win), Mp[:].rearrange("h (c o) -> h c o", o=1).to_broadcast([NH, NC, C]), ch(A), ALU.subtract).then_inc(v, 1)
                nc.vector.tensor_tensor(en[:], b[:], A[:], ALU.add).then_inc(v, 1)
                nc.vector.tensor_tensor(ch(ws), ch(a), Wo[:].rearrange("h (c o) -> h c o", o=1).to_broadcast([NH, NC, C]), ALU.subtract).then_inc(v, 1)
                dve.wait_ge(v, 11)
                nc.vector.tensor_tensor(Wo[:], Mp[:], Wo[:], ALU.subtract).then_inc(v, 1)
                dve.wait_ge(cols_ps, 1)
                nc.vector.tensor_copy(gcols[:].rearrange("p q c h -> p (q c h)"), ps[:, 0, 0:4*NC*NH]).then_inc(cdone, 1)
                nc.vector.tensor_copy(wold[:].rearrange("p h c -> p (h c)"), ps[:, 1, 0:NH*NC]).then_inc(cdone, 1)
                dve.wait_ge(cdone, 2)
        ZS=4
        zq=sb("zq", [128, ZS, 2*NH*DK])
        va=sb("va", [128, ZS, NH, DVA])
        zo=sb("zo", [128, ZS, NH*DV])
        qT=sb("qT", [128, 2, NH, C])
        kT=sb("kT", [128, NH, C])
        kw=sb("kw", [128, 2, NH, DK])
        Dm=sb("Dm", [128, NH, C])
        Ex=sb("Ex", [128, NH, C])
        W=sb("W", [128, 2, NH, C])
        Cst=sb("C_state", [128, NH, DVA])
        intra=sb("intra", [128, NH, DVA])
        num=sb("num", [128, 2, NH, DVA])
        hn=sb("hn", [128, NH, DV])
        den=sb("den", [128, NH])
        ss=sb("ss", [128, NH])
        f=sb("f", [128, NH])
        sg=sb("sg", [128, NH*DV])
        yo=sb("yo", [128, 2, NH*DV])
        eps=sb("eps", [128, 1])
        ps=ctx.enter_context(nc.psum_tensor("ml_ps", [128, 8, 512], F32))
        TQ, TK, AB, SC, OUT=0, 1, 2, 3, 4
        z_loaded=[sem(f"z_loaded{j}") for j in range(ZS)]
        init=sem("state_zeroed")
        sp_waited=sem("sp_waited")
        qk_turned=sem("qk_turned")
        a_wide=sem("a_wide")
        q_ready=sem("q_ready")
        k_ready=sem("k_ready")
        scores=sem("scores")
        D_ready=sem("D_ready")
        E_ready=sem("E_ready")
        W_ready=sem("W_ready")
        kw_ready=sem("kw_ready")
        out_ready=sem("out_ready")
        intra_copied=sem("intra_copied")
        inter_used=sem("inter_used")
        state_used=sem("state_used")
        sg_ready=sem("sigmoid_ready")
        r_ready=sem("r_ready")
        ss_ready=sem("ss_ready")
        rs_ready=sem("rs_ready")
        sg_scaled=sem("sigmoid_scaled")
        f_ready=sem("f_ready")
        den_abs=sem("den_abs")
        y_ready=sem("y_ready")
        y_stored=[sem(f"y_stored{j}") for j in range(2)]
        block=ctx.enter_context(nc.Block())
        def chunks(eng, ahead, main):
            ahead(0, 0)
            with eng.Fori(0, NC//ZS-1) as g:
                for j in range(ZS): main(g*ZS+j, j, True)
            for j in range(ZS): main(NC-ZS+j, j, j+1<ZS)
        @block.sync
        def _(sp):
            for s in y_stored: sp.sem_inc(s, 16)
            def load(c, j):
                sp.dma_start(zq[:, j], zc[c, :, Z_MQ:Z_MV]).then_inc(z_loaded[j], 16)
                sp.dma_start(va[:, j, :, 0:DV], zc[c, :, Z_MV:Z_MO].rearrange("p (h v) -> p h v", h=NH)).then_inc(z_loaded[j], 16)
                sp.dma_start(zo[:, j], zc[c, :, Z_MO:Z_MI]).then_inc(z_loaded[j], 16)
            for j in range(ZS): load(j, j)
            def main(c, j, more):
                sp.wait_ge(y_ready, c+2)
                sp.sem_inc(sp_waited, 1)
                if more: load(c+ZS, j)
                sp.dma_start(yc[c, :, 1024:2048], yo[:, j%2]).then_inc(y_stored[j%2], 16)
            with sp.Fori(0, NC//ZS-1) as g:
                for j in range(ZS): main(g*ZS+j, j, True)
            for j in range(ZS): main(NC-ZS+j, j, False)
            for j in range(2): sp.wait_ge(y_stored[j], 16*NC//2+16)
        @block.gpsimd
        def _(pool):
            pool.memset(Cst[:], 0.0).then_inc(init, 1)
            pool.memset(va[:, :, :, DV:DVA], 1.0).then_inc(init, 1)
            pool.memset(eps[:], EPS).then_inc(init, 1)
        order=[(h, kind) for h in range(NH) for kind in range(3)]
        done_of=(intra_copied, inter_used, state_used)
        def per_slot(c, j, n, base):
            return (c-j)*(n//ZS)+base
        @block.tensor
        def _(pe):
            pe.sem_inc(scores, 1)
            pe.wait_ge(init, 3)
            def turn(c, j):
                pe.wait_ge(z_loaded[j], per_slot(c, j, 48, 48))
                pe.wait_ge(k_ready, c+1)
                pe.wait_ge(q_ready, c+1)
                for h in range(NH):
                    nc.tensor.transpose(ps[:, TQ, h*128:h*128+128], zq[:, j, h*128:h*128+128], ident[:])
                    t=nc.tensor.transpose(ps[:, TK, h*128:h*128+128], zq[:, j, NH*DK+h*128:NH*DK+h*128+128], ident[:])
                t.then_inc(qk_turned, 1)
                pe.wait_ge(D_ready, c+1)
                for h in range(NH):
                    t=nc.tensor.matmul(ps[:, AB, h*128:h*128+128], sel[:, h], A[:, bass.ds(c*C, C)], start=True, stop=True)
                t.then_inc(a_wide, 1)
            def score(c, j):
                pe.wait_ge(k_ready, c+2)
                pe.wait_ge(q_ready, c+2)
                pe.wait_ge(W_ready, c+1)
                for h in range(NH):
                    t=nc.tensor.matmul(ps[:, SC, h*128:h*128+128], kT[:, h], qT[:, j%2, h], start=True, stop=True)
                t.then_inc(scores, 1)
            def ahead(c, j):
                turn(c, j)
                score(c, j)
            def main(c, j, more):
                if more: turn(c+1, (j+1)%ZS)
                pe.wait_ge(state_used, c*4+4)
                pe.wait_ge(W_ready, c+2)
                pe.wait_ge(kw_ready, c+1)
                for n, (h, kind) in enumerate(order):
                    ph, pk=order[(n-4)%12]
                    pe.wait_ge(done_of[pk], c*4+(ph+1+(4 if n>=4 else 0)))
                    lhs, rhs=((W[:, j%2, h], va[:, j, h]), (qT[:, j%2, h], Cst[:, h]), (kw[:, j%2, h], va[:, j, h]))[kind]
                    nc.tensor.matmul(ps[:, OUT+n%4, 0:DVA], lhs, rhs, start=True, stop=True).then_inc(out_ready, 1)
                    if n==5 and more: score(c+1, (j+1)%ZS)
            chunks(pe, ahead, main)
        @block.scalar
        def _(act):
            act.sem_inc(E_ready, 1)
            act.sem_inc(q_ready, 1)
            act.wait_ge(init, 3)
            act.sem_inc(intra_copied, 4)
            def col(c, q, h): return gcols[:, q, bass.ds(c, 1), h]
            def ahead_q(c, j):
                act.wait_ge(qk_turned, c+1)
                nc.scalar.activation(qT[:, j%2].rearrange("p h c -> p (h c)"), ps[:, TQ], ACT.Copy, scale=float(DK)**-0.5).then_inc(q_ready, 1)
            def ahead_e(c, j):
                act.wait_ge(D_ready, c+2)
                act.wait_ge(W_ready, c+1)
                for h in range(NH):
                    t=nc.scalar.activation(Ex[:, h], Dm[:, h], ACT.Exp, scale=-1.0, bias=col(c, 0, h))
                t.then_inc(E_ready, 1)
                act.wait_ge(z_loaded[j], per_slot(c, j, 48, 48))
                for h in range(NH):
                    t=nc.scalar.activation(kw[:, j%2, h], zq[:, j, NH*DK+h*128:NH*DK+h*128+128], ACT.Copy, scale=col(c, 3, h))
                t.then_inc(kw_ready, 1)
            def ahead(c, j):
                ahead_q(c, j)
                ahead_e(c, j)
            def main(c, j, more):
                if more: ahead_q(c+1, (j+1)%ZS)
                def copy(h):
                    act.wait_ge(out_ready, c*12+(3*h+1))
                    act.wait_ge(inter_used, c*4+(h+1))
                    nc.scalar.copy(intra[:, h], ps[:, OUT+(3*h)%4, 0:DVA]).then_inc(intra_copied, 1)
                copy(0)
                copy(1)
                if more: ahead_e(c+1, (j+1)%ZS)
                copy(2)
                copy(3)
                act.wait_ge(y_ready, c+1)
                act.wait_ge(z_loaded[j], per_slot(c, j, 48, 48))
                nc.scalar.activation(sg[:], zo[:, j], ACT.Sigmoid).then_inc(sg_ready, 1)
                act.wait_ge(inter_used, c*4+8)
                act.wait_ge(f_ready, c*2+1)
                nc.scalar.activation(den[:], num[:, j%2, :, DV], ACT.Abs).then_inc(den_abs, 1)
                act.wait_ge(r_ready, c+1)
                for h in range(NH):
                    nc.scalar.activation(hn[:, h], num[:, j%2, h, 0:DV], ACT.Square, scale=den[:, h:h+1], accum_out=ss[:, h:h+1]).then_inc(ss_ready, 1)
                act.wait_ge(ss_ready, c*4+4)
                nc.scalar.activation(ss[:], ss[:], ACT.Ln, scale=1.0/DV, bias=eps[:]).then_inc(rs_ready, 1)
                act.wait_ge(rs_ready, c*2+1)
                nc.scalar.activation(ss[:], ss[:], ACT.Exp, scale=-0.5).then_inc(rs_ready, 1)
            chunks(act, ahead, main)
        @block.vector
        def _(dve):
            dve.sem_inc(D_ready, 1)
            dve.sem_inc(W_ready, 1)
            dve.sem_inc(f_ready, 1)
            dve.sem_inc(k_ready, 1)
            dve.sem_inc(y_ready, 1)
            dve.wait_ge(init, 3)
            dve.sem_inc(inter_used, 4)
            dve.sem_inc(state_used, 4)
            def ahead_k(c, j):
                dve.wait_ge(qk_turned, c+1)
                dve.wait_ge(scores, c+1)
                nc.vector.tensor_copy(kT[:].rearrange("p h c -> p (h c)"), ps[:, TK]).then_inc(k_ready, 1)
                dve.wait_ge(a_wide, c+1)
                dve.wait_ge(E_ready, c+1)
                nc.vector.tensor_tensor(Dm[:], ps[:, AB].rearrange("p (h c) -> p h c", h=NH), mask[:].rearrange("p (o c) -> p o c", o=1).to_broadcast([128, NH, C]), ALU.add).then_inc(D_ready, 1)
            def ahead_w(c, j):
                dve.wait_ge(scores, c+2)
                dve.wait_ge(E_ready, c+2)
                nc.vector.tensor_tensor(W[:, j%2].rearrange("p h c -> p (h c)"), ps[:, SC], Ex[:].rearrange("p h c -> p (h c)"), ALU.mult).then_inc(W_ready, 1)
            def ahead(c, j):
                ahead_k(c, j)
                ahead_w(c, j)
            def main(c, j, more):
                if more: ahead_k(c+1, (j+1)%ZS)
                for h in range(NH):
                    n=3*h+1
                    dve.wait_ge(out_ready, c*12+(n+1))
                    dve.wait_ge(intra_copied, c*4+(h+5))
                    nc.vector.scalar_tensor_tensor(out=num[:, j%2, h], in0=ps[:, OUT+n%4, 0:DVA], scalar=gcols[:, 1, bass.ds(c, 1), h], in1=intra[:, h], op0=ALU.mult, op1=ALU.add).then_inc(inter_used, 1)
                    dve.wait_ge(out_ready, c*12+(n+2))
                    nc.vector.scalar_tensor_tensor(out=Cst[:, h], in0=Cst[:, h], scalar=wold[:, h, bass.ds(c, 1)], in1=ps[:, OUT+(n+1)%4, 0:DVA], op0=ALU.mult, op1=ALU.add).then_inc(state_used, 1)
                if more: ahead_w(c+1, (j+1)%ZS)
                dve.wait_ge(den_abs, c+1)
                nc.vector.tensor_tensor(den[:], den[:], gcols[:, 2, bass.ds(c, 1), :].rearrange("p o h -> p (o h)"), ALU.max).then_inc(f_ready, 1)
                dve.wait_ge(f_ready, c*2+2)
                nc.vector.reciprocal(den[:], den[:]).then_inc(r_ready, 1)
                dve.wait_ge(sg_ready, c+1)
                nc.vector.tensor_tensor(sg[:], sg[:], gbc[:], ALU.mult).then_inc(sg_scaled, 1)
                dve.wait_ge(rs_ready, c*2+2)
                dve.wait_ge(r_ready, c+1)
                nc.vector.tensor_tensor(f[:], den[:], ss[:], ALU.mult).then_inc(f_ready, 1)
                dve.wait_ge(f_ready, c*2+3)
                dve.wait_ge(y_stored[j%2], per_slot(c, j, 32, 16+16*(j//2)))
                dve.wait_ge(sg_scaled, c+1)
                for h in range(NH):
                    t=nc.vector.scalar_tensor_tensor(out=yo[:, j%2, h*DV:(h+1)*DV], in0=num[:, j%2, h, 0:DV], scalar=f[:, h:h+1], in1=sg[:, h*DV:(h+1)*DV], op0=ALU.mult, op1=ALU.mult)
                t.then_inc(y_ready, 1)
            chunks(dve, ahead, main)

QR=512
KR=256
NIH=8
ID=64
TOPK=256
NAH=8
HD=128
BF=mybir.dt.bfloat16
QK_=QR//128
KK=KR//128
WIDTH=[(b+1)*128 for b in range(TT)]
MOFF=[sum(WIDTH[:b]) for b in range(TT)]
MTOT=sum(WIDTH)
TAKEN=-3e38
UNSEEN=-1e30

def dsa(nc, s_col, ada_w, ada_b, mod, z, h_tiles, w_in, cq_g, ckv_g, w_uq, w_uk, w_uv, w_qidx, y, ys):
    zt=z.rearrange("(t p) n -> t p n", p=128)
    yt=y.rearrange("(t p) n -> t p n", p=128)
    with ExitStack() as ctx:
        sb=lambda n, s, d=F32: ctx.enter_context(nc.sbuf_tensor("dsa_"+n, s, d))
        cqT=sb("cqT", [128, QK_, S])
        ckvT=sb("ckvT", [128, KK, S])
        bias=sb("select_bias", [128, MTOT], BF)
        ident=sb("ident", [128, 128])
        with ExitStack() as ictx:
            kiT=ictx.enter_context(nc.sbuf_tensor("kiT", [128, S], F32))
            wi=ictx.enter_context(nc.sbuf_tensor("w_idx", [128, TT, NIH], F32))
            latents(nc, zt, z, cq_g, ckv_g, cqT, ckvT, kiT, wi, ident, s_col, ada_w, ada_b, mod)
            indexer(nc, w_qidx, cqT, kiT, wi, bias, h_tiles, w_in, zt)
        attention(nc, w_uq, w_uk, w_uv, cqT, ckvT, bias, ident, yt, ys)

def latents(nc, zt, z, cq_g, ckv_g, cqT, ckvT, kiT, wi, ident, s_col, ada_w, ada_b, mod):
    M0=2*D//MB
    assert 6*D//MB-M0==TT
    ada_v=ada_blocks(ada_w)
    NL=QR+KR
    NT=QK_+KK+1
    with ExitStack() as ctx:
        sb=lambda n, s, d=F32: ctx.enter_context(nc.sbuf_tensor("lat_"+n, s, d))
        sem=semaphores(nc, ctx, "lat")
        zl=sb("z_latents", [128, 2, NL+2*ID])
        xn=sb("latents_normed", [128, 2, NL])
        junk=sb("squares", [128, 2, NL])
        ss=sb("ss", [128, 2, 2])
        rs=sb("rs", [128, 2, 2])
        eps=sb("eps", [128, 1])
        aw=sb("ada_w_ring", [128, 2, KD, MB])
        ab=sb("ada_b_ring", [1, 2, MB])
        mrow=sb("mod_row", [1, 2, MB])
        aw_l=[sem(f"ada_loaded{j}") for j in range(2)]
        m_acc=sem("mod_acc")
        m_ready=sem("mod_ready")
        m_st=[sem(f"mod_stored{j}") for j in range(2)]
        grow=sb("gain_rows", [QK_+KK, 128])
        gcol=sb("gain_cols", [128, QK_+KK])
        ps=ctx.enter_context(nc.psum_tensor("lat_ps", [128, 8, 512], F32))
        loaded=[sem(f"loaded{j}") for j in range(2)]
        const_loaded=sem("const_loaded")
        made=sem("made")
        gturned=sem("gains_turned")
        gready=sem("gains_ready")
        wi_ready=sem("wi_ready")
        ss_ready=sem("ss_ready")
        ln_ready=sem("ln_ready")
        rs_ready=sem("rs_ready")
        xn_ready=sem("xn_ready")
        turned=sem("turned")
        act_ev=sem("act_evacuated")
        dve_ev=sem("dve_evacuated")
        block=ctx.enter_context(nc.Block())
        @block.gpsimd
        def _(pool):
            identity_tile(nc, pool, ident, made)
            pool.memset(eps[:], EPS).then_inc(made, 1)
        @block.sync
        def _(sp):
            sp.dma_start(grow[0:QK_], cq_g.rearrange("l (k p) -> (l k) p", p=128)).then_inc(const_loaded, 16)
            sp.dma_start(grow[QK_:], ckv_g.rearrange("l (k p) -> (l k) p", p=128)).then_inc(const_loaded, 16)
            with nc.allow_non_contiguous_dma(reason="short rows"):
                sp.dma_start(wi[:], z.rearrange("(t p) n -> p t n", p=128)[:, :, Z_WI:Z_WI+NIH]).then_inc(const_loaded, 16)
            with sp.Fori(0, TT//2) as g:
                for j in range(2):
                    sp.wait_ge(turned, g*2+j+1)
                    sp.dma_start(zl[:, j, 0:NL+ID], zt[g*2+j, :, 0:NL+ID]).then_inc(loaded[j], 16)
                    sp.dma_start(zl[:, j, NL+ID:], zt[g*2+j, :, Z_KI:Z_KI+ID]).then_inc(loaded[j], 16)
                    sp.wait_ge(m_ready, g*2+j+1)
                    sp.dma_start(aw[:, j], ada_v[:, :, bass.ds(g*(2*MB)+(M0+j)*MB, MB)]).then_inc(aw_l[j], 16)
                    sp.dma_start(ab[:, j], ada_b[:, bass.ds(g*(2*MB)+(M0+j)*MB, MB)]).then_inc(aw_l[j], 16)
        @block.tensor
        def _(pe):
            pe.sem_inc(turned, 2)
            pe.wait_ge(made, 3)
            pe.wait_ge(const_loaded, 48)
            nc.tensor.transpose(ps[:, 0, 0:QK_+KK], grow[:], ident[0:QK_+KK, 0:QK_+KK]).then_inc(gturned, 1)
            pe.wait_ge(gready, 1)
            with pe.Fori(0, TT//2) as g:
                for j in range(2):
                    pe.wait_ge(aw_l[j], g*32+32)
                    pe.wait_ge(m_ready, g*2+j+1)
                    for k in range(KD):
                        t=nc.tensor.matmul(ps[0:1, 4*j+2], s_col[:, k:k+1], aw[:, j, k], start=(k==0), stop=(k==KD-1))
                    t.then_inc(m_acc, 1)
                    pe.wait_ge(xn_ready, g*2+j+1+1)
                    pe.wait_ge(act_ev, g*2+1)
                    pe.wait_ge(dve_ev, g*2+1)
                    for k in range(NT):
                        src=xn[:, j, k*128:(k+1)*128] if k<NT-1 else zl[:, j, NL:]
                        t=nc.tensor.transpose(ps[:, 4*j+k//4, (k%4)*128:(k%4)*128+128], src, ident[:])
                    t.then_inc(turned, 1)
        @block.scalar
        def _(act):
            act.sem_inc(act_ev, 1)
            act.sem_inc(rs_ready, 1)
            for j in range(2): act.sem_inc(m_st[j], 16)
            act.wait_ge(made, 3)
            act.wait_ge(gready, 1)
            with act.Fori(0, TT//2) as g:
                for j in range(2):
                    act.wait_ge(loaded[j], g*32+32)
                    act.wait_ge(rs_ready, g*2+1)
                    nc.scalar.activation(junk[:, j, 0:QR], zl[:, j, 0:QR], ACT.Square, scale=float(QR)**-0.5, accum_out=ss[:, j, 0:1]).then_inc(ss_ready, 1)
                    nc.scalar.activation(junk[:, j, QR:], zl[:, j, QR:NL], ACT.Square, scale=float(KR)**-0.5, accum_out=ss[:, j, 1:2]).then_inc(ss_ready, 1)
                    act.wait_ge(ss_ready, g*4+j*2+2)
                    nc.scalar.activation(ss[:, j], ss[:, j], ACT.Ln, bias=eps[:]).then_inc(ln_ready, 1)
                    act.wait_ge(ln_ready, g*2+j+1)
                    act.wait_ge(xn_ready, g*2+1)
                    nc.scalar.activation(rs[:, j], ss[:, j], ACT.Exp, scale=-0.5).then_inc(rs_ready, 1)
                    act.wait_ge(turned, g*2+j+1+2)
                    for k in range(QK_):
                        t=nc.scalar.activation(cqT[:, k, bass.ds(g*256+j*128, 128)], ps[:, 4*j, k*128:k*128+128], ACT.Copy, scale=gcol[:, k:k+1])
                    t.then_inc(act_ev, 1)
                    act.wait_ge(m_ready, g*2+j+1+2)
                    act.dma_start(mod[:, bass.ds(g*(2*MB)+(M0+j)*MB, MB)], mrow[:, j]).then_inc(m_st[j], 16)
            for j in range(2): act.wait_ge(m_st[j], 16*TT//2+16)
        @block.vector
        def _(dve):
            dve.sem_inc(dve_ev, 1)
            dve.sem_inc(xn_ready, 1)
            dve.sem_inc(m_ready, 2)
            dve.wait_ge(gturned, 1)
            nc.vector.tensor_copy(gcol[:], ps[:, 0, 0:QK_+KK]).then_inc(gready, 1)
            dve.wait_ge(const_loaded, 48)
            nc.vector.tensor_scalar(wi[:], wi[:], float(NIH)**-0.5*float(ID)**-0.5, None, ALU.mult).then_inc(wi_ready, 1)
            dve.wait_ge(gready, 1)
            with dve.Fori(0, TT//2) as g:
                for j in range(2):
                    dve.wait_ge(rs_ready, g*2+j+1+1)
                    dve.wait_ge(turned, g*2+j+1)
                    dve.wait_ge(loaded[j], g*32+32)
                    nc.vector.tensor_scalar(xn[:, j, 0:QR], zl[:, j, 0:QR], rs[:, j, 0:1], None, ALU.mult)
                    nc.vector.tensor_scalar(xn[:, j, QR:], zl[:, j, QR:NL], rs[:, j, 1:2], None, ALU.mult).then_inc(xn_ready, 1)
                    dve.wait_ge(m_acc, g*2+j+1)
                    dve.wait_ge(m_st[j], g*16+16)
                    nc.vector.tensor_tensor(mrow[:, j], ps[0:1, 4*j+2], ab[:, j], ALU.add).then_inc(m_ready, 1)
                    dve.wait_ge(turned, g*2+j+1+2)
                    for k in range(KK):
                        nc.vector.tensor_scalar(ckvT[:, k, bass.ds(g*256+j*128, 128)], ps[:, 4*j+1, k*128:k*128+128], gcol[:, QK_+k:QK_+k+1], None, ALU.mult)
                    nc.vector.tensor_copy(kiT[:, bass.ds(g*256+j*128, 128)], ps[:, 4*j+1, KK*128:KK*128+128]).then_inc(dve_ev, 1)
            dve.wait_ge(wi_ready, 1)

def indexer(nc, w_qidx, cqT, kiT, wi, bias, h_tiles, w_in, zt):
    RR=4
    CH=[[(c, min(512, WIDTH[b]-c)) for c in range(0, WIDTH[b], 512)] for b in range(TT)]
    FB=TOPK//128
    BLOCKS=list(range(FB, TT))
    with ExitStack() as ctx:
        sb=lambda n, s, d=F32: ctx.enter_context(nc.sbuf_tensor("idx_"+n, s, d))
        sem=semaphores(nc, ctx, "idx")
        w=sb("w_qidx_sb", [128, QK_, NIH*ID])
        qi=sb("q_idxT", [128, 2, NIH//2*128])
        relu=sb("relu", [128, RR, 512])
        isc=sb("isc", [128, S])
        m8=sb("max8", [128, 8])
        cmask=sb("causal", [128, 128])
        hT=sb("hT_tiles", [128, 2, KD, 128])
        wz=sb("w_in_ring", [128, 2, KD, ZN2])
        stage=sb("z_stage", [128, 2, ZN2])
        ps=ctx.enter_context(nc.psum_tensor("idx_ps", [128, 8, 512], F32))
        SB_, ZB_, PB=4, 4, 7
        w_loaded=sem("w_loaded")
        made=sem("made")
        proj=sem("proj")
        proj_copied=sem("proj_copied")
        scored=sem("scored")
        relu_ready=sem("relu_ready")
        summed=sem("summed")
        seen=sem("causal_done")
        found=sem("max8_found")
        waited=sem("waited")
        taken=sem("taken")
        biased=sem("bias_written")
        hT_l=[sem(f"hT_loaded{j}") for j in range(2)]
        wz_l=[sem(f"w_in_loaded{j}") for j in range(2)]
        z_acc=sem("z_acc")
        z_copied=sem("z_copied")
        z_st=[sem(f"z_stored{j}") for j in range(2)]
        block=ctx.enter_context(nc.Block())
        PAIRS=ZB2*TT//2
        done=[round(PAIRS*sum(WIDTH[FB:b])/sum(WIDTH[FB:])) for b in range(FB, TT+1)]
        def z_pairs(eng, b, each, first=lambda cb: None):
            p, end=done[b-FB], done[b-FB+1]
            while p<end:
                cb=p//(TT//2)
                p0=cb*(TT//2)
                stop=min(end, p0+TT//2)
                if p==p0: first(cb)
                loop_end=stop-1 if stop==p0+TT//2 else stop
                if loop_end-p==1: each(cb, p-p0)
                elif loop_end>p:
                    with eng.Fori(p-p0, loop_end-p0) as r: each(cb, r)
                if loop_end<stop: each(cb, loop_end-p0)
                p=stop
        wv=w_in.rearrange("l (k p) n -> p (l k) n", p=128)
        @block.sync
        def _(sp):
            sp.dma_start(w[:], w_qidx.rearrange("l (k p) n -> p (l k) n", p=128)).then_inc(w_loaded, 16)
            for j in range(2): sp.sem_inc(z_st[j], 16)
            def load_w(cb): sp.dma_start(wz[:, cb%2], wv[:, :, ZA+cb*ZN2:ZA+(cb+1)*ZN2]).then_inc(wz_l[cb%2], 16)
            load_w(0)
            for j in range(2): sp.dma_start(hT[:, j], h_tiles[j]).then_inc(hT_l[j], 16)
            load_w(1)
            def first(cb):
                if cb>=1 and cb+1<ZB2:
                    sp.wait_ge(z_acc, cb*TT+2)
                    load_w(cb+1)
            def each(cb, p):
                for j in range(2):
                    u=cb*TT+j
                    sp.wait_ge(z_acc, p*2+(u+1+2))
                    wrap=isinstance(p, int) and p==TT//2-1
                    sp.dma_start(hT[:, j], h_tiles[j] if wrap else h_tiles[p*2+(j+2)]).then_inc(hT_l[j], 16)
                    sp.wait_ge(z_copied, p*2+(u+1+2))
                    sp.dma_start(zt[p*2+j, :, ZA+cb*ZN2:ZA+(cb+1)*ZN2], stage[:, j]).then_inc(z_st[j], 16)
            for b in BLOCKS: z_pairs(sp, b, each, first)
            for j in range(2):
                sp.wait_ge(z_st[j], 16*PAIRS+16)
                sp.wait_ge(hT_l[j], 16*PAIRS+16)
        @block.gpsimd
        def _(pool):
            pool.memset(cmask[:], 0.0).then_inc(made, 1)
            pool.wait_ge(made, 1)
            pool.affine_select(out=cmask[:], in_=cmask[:], compare_op=ALU.is_ge, fill=UNSEEN, base=0, pattern=[[-1, 128]], channel_multiplier=1).then_inc(made, 1)
        @block.tensor
        def _(pe):
            pe.wait_ge(w_loaded, 16)
            pe.sem_inc(z_acc, 2)
            def project(i, b):
                if i: pe.wait_ge(proj_copied, i)
                for p in range(NIH//2):
                    for k in range(QK_):
                        t=nc.tensor.matmul(ps[:, PB, p*128:(p+1)*128], w[:, k, p*128:(p+1)*128], cqT[:, k, b*128:(b+1)*128], start=(k==0), stop=(k==QK_-1))
                t.then_inc(proj, 1)
            def each(cb, p):
                for j in range(2):
                    u=cb*TT+j
                    pe.wait_ge(hT_l[j], p*16+(u//2*16+16))
                    pe.wait_ge(z_copied, p*2+(u+1))
                    for k in range(KD):
                        t=nc.tensor.matmul(ps[:, ZB_+j, 0:ZN2], hT[:, j, k], wz[:, cb%2, k], start=(k==0), stop=(k==KD-1))
                    t.then_inc(z_acc, 1)
            project(0, FB)
            n=0
            for i, b in enumerate(BLOCKS):
                pe.wait_ge(proj_copied, i+1)
                for c, wd in CH[b]:
                    for h in range(NIH):
                        if n>=SB_: pe.wait_ge(relu_ready, n-SB_+1)
                        r=(h%2)*ID
                        q=h//2*128
                        nc.tensor.matmul(ps[:, n%SB_, 0:wd], qi[r:r+ID, b%2, q:q+128], kiT[r:r+ID, c:c+wd], start=True, stop=True).then_inc(scored, 1)
                        n+=1
                if b+1<TT: project(i+1, b+1)
                z_pairs(pe, b, each, lambda cb: pe.wait_ge(wz_l[cb%2], cb//2*16+16))
        @block.scalar
        def _(act):
            act.sem_inc(z_copied, 2)
            def copy_q(i, b):
                act.wait_ge(proj, i+1)
                nc.scalar.copy(qi[:, b%2], ps[:, PB]).then_inc(proj_copied, 1)
            def each(cb, p):
                for j in range(2):
                    u=cb*TT+j
                    act.wait_ge(z_acc, p*2+(u+1+2))
                    act.wait_ge(z_st[j], p*16+(u//2*16+16))
                    nc.scalar.copy(stage[:, j], ps[:, ZB_+j, 0:ZN2]).then_inc(z_copied, 1)
            copy_q(0, FB)
            n=0
            for i, b in enumerate(BLOCKS):
                for c, wd in CH[b]:
                    for h in range(NIH):
                        act.wait_ge(scored, n+1)
                        if n>=RR: act.wait_ge(summed, n-RR+1)
                        nc.scalar.activation(relu[:, n%RR, 0:wd], ps[:, n%SB_, 0:wd], ACT.Relu).then_inc(relu_ready, 1)
                        n+=1
                if b+1<TT: copy_q(i+1, b+1)
                z_pairs(act, b, each)
        @block.vector
        def _(dve):
            dve.sem_inc(taken, 1)
            dve.wait_ge(made, 2)
            for b in range(FB):
                if b: nc.vector.memset(bias[:, MOFF[b]:MOFF[b]+b*128], 0.0)
                nc.vector.tensor_copy(bias[:, MOFF[b]+b*128:MOFF[b]+WIDTH[b]], cmask[:]).then_inc(biased, 1)
            n=0
            for i, b in enumerate(BLOCKS):
                if i: dve.wait_ge(biased, FB+i)
                for c, wd in CH[b]:
                    for h in range(NIH):
                        dve.wait_ge(relu_ready, n+1)
                        o=isc[:, c:c+wd]
                        if h==0: nc.vector.tensor_scalar(o, relu[:, n%RR, 0:wd], wi[:, b, h:h+1], None, ALU.mult).then_inc(summed, 1)
                        else:
                            dve.wait_ge(summed, n)
                            nc.vector.scalar_tensor_tensor(out=o, in0=relu[:, n%RR, 0:wd], scalar=wi[:, b, h:h+1], in1=o, op0=ALU.mult, op1=ALU.add).then_inc(summed, 1)
                        n+=1
                dve.wait_ge(summed, n)
                nc.vector.tensor_tensor(isc[:, b*128:WIDTH[b]], isc[:, b*128:WIDTH[b]], cmask[:], ALU.add).then_inc(seen, 1)
                dve.wait_ge(seen, i+1)
                v=isc[:, 0:WIDTH[b]]
                base=i*(TOPK//8)
                with dve.Fori(0, TOPK//8) as r:
                    dve.wait_ge(taken, r+(base+1))
                    dve.sem_inc(waited, 1)
                    nc.vector.max(m8[:], v).then_inc(found, 1)
                    dve.wait_ge(found, r+(base+1))
                    dve.sem_inc(waited, 1)
                    nc.vector.match_replace(v, m8[:], v, TAKEN).then_inc(taken, 1)
                dve.wait_ge(taken, base+TOPK//8+1)
                nc.vector.tensor_scalar(bias[:, MOFF[b]:MOFF[b]+WIDTH[b]], v, -2e38, UNSEEN, ALU.is_gt, ALU.mult).then_inc(biased, 1)

def attention(nc, w_uq, w_uk, w_uv, cqT, ckvT, bias, ident, yt, ys):
    SCALE=float(HD)**-0.5
    HG=4
    SR=3
    TR=2
    CH=[[(c, min(512, WIDTH[b]-c)) for c in range(0, WIDTH[b], 512)] for b in range(TT)]
    NCH=sum(len(c) for c in CH)
    C0=[sum(len(c) for c in CH[:b]) for b in range(TT)]
    TQ4=S//512
    with ExitStack() as ctx:
        sb=lambda n, s, d=F32: ctx.enter_context(nc.sbuf_tensor("att_"+n, s, d))
        sem=semaphores(nc, ctx, "att")
        wq=sb("w_uq_h", [128, 2, QK_, HD])
        wk=sb("w_uk_h", [128, 2, KK, HD])
        wv=sb("w_uv_g", [128, KK, HG*HD])
        qT=sb("qT", [128, 2, S])
        kT=sb("kT", [128, 2, S])
        V=sb("V", [128, TT, HG*HD])
        Sc=sb("scores", [128, 2, S])
        PT=sb("probsT", [128, 2, TT, 128])
        cm=sb("chunk_max", [128, 2, 4])
        nm=sb("neg_max", [128, 2])
        rsum=sb("row_sum", [128, 2])
        rinv=sb("row_inv", [128, 2])
        zero=sb("zero", [128, 512])
        zero_made=sem("zero_made")
        cleared=sem("ys_cleared")
        o=sb("o", [128, 4, HD])
        ps=ctx.enter_context(nc.psum_tensor("att_ps", [128, 8, 512], F32))
        PJ, OB=6, 7
        wq_l=[sem(f"wqk_loaded{j}") for j in range(2)]
        wv_l=sem("wv_loaded")
        proj=sem("projected")
        pcopy=sem("proj_copied")
        v_ps=sem("v_in_psum")
        v_copy=sem("v_copied")
        scored=sem("scored")
        masked=sem("masked")
        waited=sem("waited")
        maxed=sem("maxed")
        mx=sem("mx")
        expd=sem("exp_done")
        pturned=sem("probs_turned")
        pt_act=sem("probsT_act")
        pt_dve=sem("probsT_dve")
        pv=sem("pv_done")
        inv=sem("row_inv_ready")
        o_ready=sem("o_ready")
        stored=[sem(f"o_stored{j}") for j in range(4)]
        block=ctx.enter_context(nc.Block())
        wqv=w_uq.rearrange("l (k p) n -> p (l k) n", p=128)
        wkv=w_uk.rearrange("l (k p) h d -> p (l k) (h d)", p=128)
        wvv=w_uv.rearrange("l (k p) h d -> p (l k) (h d)", p=128)
        PC=2*TQ4
        G=[(b, t0, min(4, b+1-t0)) for b in range(TT) for t0 in range(0, b+1, 4)]
        NG=len(G)
        G0=[sum(1 for g in G if g[0]<b) for b in range(TT)]
        assert NAH//HG==2 and PC==TQ4*2<=TT
        def loops(eng, body):
            with eng.Fori(0, NAH//HG) as gg:
                for hh in range(HG): body(gg, hh)
        def following(gg, hh):
            return gg*HG+(hh+1) if hh<HG-1 else gg*(-HG)+HG
        @block.gpsimd
        def _(pool):
            yst=ys.rearrange("(t p) d -> t p d", p=128)
            clear_from=2*S//128
            n_tiles=yst.shape[0]
            pool.memset(zero[:], 0.0).then_inc(zero_made, 1)
            pool.wait_ge(zero_made, 1)
            with pool.Fori(clear_from, n_tiles) as t:
                pool.dma_start(yst[t].rearrange("p (r n) -> p r n", n=512), zero[:].rearrange("p (o n) -> p o n", o=1).to_broadcast([128, D//512, 512])).then_inc(cleared, 16)
            pool.wait_ge(cleared, 16*(n_tiles-clear_from))
        @block.sync
        def _(sp):
            for s in stored: sp.sem_inc(s, 16)
            sp.dma_start(wq[:, 0], wqv[:, :, 0:HD]).then_inc(wq_l[0], 16)
            sp.dma_start(wk[:, 0], wkv[:, :, 0:HD]).then_inc(wq_l[0], 16)
            def body(gg, hh):
                j=hh%2
                if hh==0:
                    sp.wait_ge(v_ps, gg*TT+1)
                    sp.dma_start(wv[:], wvv[:, :, bass.ds(gg*(HG*HD), HG*HD)]).then_inc(wv_l, 16)
                sp.wait_ge(proj, (gg*HG+hh)*PC+1)
                nh=following(gg, hh)
                sp.dma_start(wq[:, 1-j], wqv[:, :, bass.ds(nh*HD, HD)]).then_inc(wq_l[1-j], 16)
                sp.dma_start(wk[:, 1-j], wkv[:, :, bass.ds(nh*HD, HD)]).then_inc(wq_l[1-j], 16)
                for b in range(TT):
                    sp.wait_ge(o_ready, (gg*HG+hh)*TT+(b+1)+1)
                    sp.dma_start(yt[b, :, bass.ds((gg*HG+hh)*HD, HD)], o[:, b%4]).then_inc(stored[b%4], 16)
            loops(sp, body)
            for j in range(4): sp.wait_ge(stored[j], 16*NAH*TT//4+16)
        @block.tensor
        def _(pe):
            pe.sem_inc(pturned, 1)
            pe.sem_inc(proj, 1)
            pe.sem_inc(scored, 1)
            pe.sem_inc(v_ps, 1)
            def project(n, nj, count):
                pe.wait_ge(pcopy, count+1)
                s, c=(wq, n) if n<TQ4 else (wk, n-TQ4)
                K_=QK_ if n<TQ4 else KK
                src=cqT if n<TQ4 else ckvT
                for k in range(K_):
                    m=nc.tensor.matmul(ps[:, PJ], s[:, nj, k], src[:, k, c*512:(c+1)*512], start=(k==0), stop=(k==K_-1))
                m.then_inc(proj, 1)
            pe.wait_ge(wq_l[0], 32)
            for n in range(PC): project(n, 0, n)
            def body(gg, hh):
                H=gg*HG+hh
                j=hh%2
                if hh==0:
                    pe.wait_ge(wv_l, gg*16+16)
                    pe.wait_ge(pv, gg*(HG*TT)+2)
                    pe.wait_ge(pcopy, gg*(HG*PC)+PC+1)
                    pe.wait_ge(o_ready, gg*(HG*TT)+1)
                    for t in range(TT):
                        pe.wait_ge(v_copy, gg*TT+t+1)
                        for k in range(KK):
                            m=nc.tensor.matmul(ps[:, PJ+t%2], ckvT[:, k, t*128:(t+1)*128], wv[:, k], start=(k==0), stop=(k==KK-1))
                        m.then_inc(v_ps, 1)
                    pe.wait_ge(v_copy, gg*TT+TT+2)
                pe.wait_ge(pcopy, H*PC+PC+1)
                def scores(b):
                    for i, (c, wd) in enumerate(CH[b]):
                        pe.wait_ge(masked, H*NCH+(C0[b]+i+1))
                        nc.tensor.matmul(ps[:, (C0[b]+i)%4, 0:wd], qT[:, j, b*128:(b+1)*128], kT[:, j, c:c+wd], start=True, stop=True).then_inc(scored, 1)
                groups=lambda b: range(G0[b], G0[b]+(b+4)//4)
                def turn(b, gi):
                    _, t0, nt=G[gi]
                    pe.wait_ge((pt_act, pt_dve)[gi%2], H*(NG//2)+(gi//2+1))
                    for t in range(nt):
                        m=nc.tensor.transpose(ps[:, 4+gi%2, t*128:(t+1)*128], Sc[:, b%2, (t0+t)*128:(t0+t+1)*128], ident[:])
                    m.then_inc(pturned, 1)
                def values(b, gi):
                    _, t0, nt=G[gi]
                    if t0==0: pe.wait_ge(o_ready, H*TT+b+1)
                    pe.wait_ge((pt_act, pt_dve)[gi%2], H*(NG//2)+(gi//2+2))
                    for t in range(nt):
                        m=nc.tensor.matmul(ps[:, OB, 0:HD], PT[:, b%2, t0+t], V[:, t0+t, hh*HD:(hh+1)*HD], start=(t0+t==0), stop=(t0+t==b))
                    if t0+nt==b+1: m.then_inc(pv, 1)
                scores(0)
                for b in range(TT):
                    if b+1<TT: scores(b+1)
                    if b==0: pe.wait_ge(wq_l[1-j], (gg*(HG//2)+(hh+1)//2)*32+32)
                    if b<PC: project(b, 1-j, H*PC+(b+PC))
                    pe.wait_ge(expd, H*TT+b+1+1)
                    before=list(groups(b-1)) if b else []
                    for i, gi in enumerate(groups(b)):
                        turn(b, gi)
                        if i%2:
                            for q in before[:2]: values(b-1, q)
                            before=before[2:]
                    for q in before: values(b-1, q)
                for q in groups(TT-1): values(TT-1, q)
            loops(pe, body)
        @block.scalar
        def _(act):
            act.sem_inc(expd, 1)
            act.sem_inc(pt_act, 1)
            act.sem_inc(pcopy, 1)
            def copy_projected(n, nj, count):
                act.wait_ge(proj, count+2)
                nc.scalar.copy((qT, kT)[n//TQ4][:, nj, (n%TQ4)*512:(n%TQ4)*512+512], ps[:, PJ]).then_inc(pcopy, 1)
            def body(gg, hh):
                H=gg*HG+hh
                j=hh%2
                if hh==0:
                    for t in range(0, TT, 2):
                        act.wait_ge(v_ps, gg*TT+t+1+1)
                        act.wait_ge(v_copy, gg*TT+t+2)
                        nc.scalar.copy(V[:, t], ps[:, PJ]).then_inc(v_copy, 1)
                for b in range(TT):
                    act.wait_ge(maxed, (H*TT+b)+1)
                    act.wait_ge(masked, H*NCH+(C0[b]+len(CH[b])+4))
                    act.wait_ge(inv, H*TT+(b+1))
                    nc.scalar.activation(Sc[:, b%2, 0:WIDTH[b]], Sc[:, b%2, 0:WIDTH[b]], ACT.Exp, bias=nm[:, b%2:b%2+1], scale=SCALE, accum_out=rsum[:, b%2:b%2+1]).then_inc(expd, 1)
                    for gi, (bb, t0, nt) in enumerate(G):
                        if bb!=b or gi%2: continue
                        act.wait_ge(pturned, H*NG+gi+1+1)
                        act.wait_ge(pv, H*TT+(b+1))
                        nc.scalar.copy(PT[:, b%2, t0:t0+nt].rearrange("p t n -> p (t n)"), ps[:, 4, 0:nt*128]).then_inc(pt_act, 1)
                    if b<PC: copy_projected(b, 1-j, H*PC+(b+PC))
            act.sem_inc(inv, 2)
            act.sem_inc(pv, 2)
            for n in range(PC): copy_projected(n, 0, n)
            loops(act, body)
        @block.vector
        def _(dve):
            dve.sem_inc(o_ready, 1)
            dve.sem_inc(v_copy, 2)
            dve.sem_inc(pt_dve, 1)
            dve.sem_inc(masked, 4)
            def body(gg, hh):
                H=gg*HG+hh
                if hh==0:
                    for t in range(1, TT, 2):
                        dve.wait_ge(v_ps, gg*TT+t+1+1)
                        dve.wait_ge(v_copy, gg*TT+t+2)
                        nc.vector.tensor_copy(V[:, t], ps[:, PJ+1]).then_inc(v_copy, 1)
                def mask(b):
                    dve.wait_ge(pturned, H*NG+(G0[b-1] if b else 0)+1)
                    dve.wait_ge(expd, H*TT+b+1)
                    for i, (c, wd) in enumerate(CH[b]):
                        dve.wait_ge(scored, H*NCH+(C0[b]+i+1)+1)
                        dve.sem_inc(waited, 1)
                        nc.vector.tensor_tensor_reduce(Sc[:, b%2, c:c+wd], ps[:, (C0[b]+i)%4, 0:wd], bias[:, MOFF[b]+c:MOFF[b]+c+wd], 1.0, -3e38, ALU.add, ALU.max, cm[:, b%2, i:i+1]).then_inc(masked, 1)
                    dve.wait_ge(masked, H*NCH+(C0[b]+len(CH[b])+4))
                    nc.vector.tensor_reduce(nm[:, b%2:b%2+1], cm[:, b%2, 0:len(CH[b])], AX.X, ALU.max).then_inc(mx, 1)
                    dve.wait_ge(mx, H*TT+b+1)
                    nc.vector.tensor_scalar(nm[:, b%2:b%2+1], nm[:, b%2:b%2+1], -SCALE, None, ALU.mult).then_inc(maxed, 1)
                def rest(b):
                    for gi, (bb, t0, nt) in enumerate(G):
                        if bb!=b or gi%2==0: continue
                        dve.wait_ge(pturned, H*NG+gi+1+1)
                        dve.wait_ge(pv, H*TT+(b+1))
                        nc.vector.tensor_copy(PT[:, b%2, t0:t0+nt].rearrange("p t n -> p (t n)"), ps[:, 5, 0:nt*128]).then_inc(pt_dve, 1)
                    dve.wait_ge(expd, H*TT+b+1+1)
                    if b>1: dve.wait_ge(o_ready, H*TT+b)
                    else: dve.wait_ge(o_ready, H*TT+1)
                    nc.vector.reciprocal(rinv[:, b%2:b%2+1], rsum[:, b%2:b%2+1]).then_inc(inv, 1)
                def finish(b):
                    dve.wait_ge(pv, H*TT+(b+3))
                    dve.wait_ge(inv, H*TT+(b+3))
                    dve.wait_ge(stored[b%4], (H*(TT//4)+b//4)*16+16)
                    nc.vector.tensor_scalar(o[:, b%4], ps[:, OB, 0:HD], rinv[:, b%2:b%2+1], None, ALU.mult).then_inc(o_ready, 1)
                mask(0)
                for b in range(TT):
                    if b+1<TT: mask(b+1)
                    rest(b)
                    if b: finish(b-1)
                finish(TT-1)
            loops(dve, body)

NE=32
GRP=4
EPG=8
FF=512
MT=63
SLOTS_=(MT+1)*128
U32=mybir.dt.uint32
I32=mybir.dt.int32

def out_projection(nc, y, x, mod, w_out, norm_g, router_w, x1, xn, ffn_cols, logits):
    yt=y.rearrange("(t p) d -> t p d", p=128)
    xt=x.rearrange("b (t p) d -> (b t) p d", p=128)
    x1t=x1.rearrange("(t p) d -> t p d", p=128)
    xnt=xn.rearrange("(t p) d -> t p d", p=128)
    modv=mod.rearrange("l (s k p) -> s (l k) p", s=6, p=128)
    row=lambda s: mod[:, s*D:(s+1)*D].to_broadcast([128, D])
    with ExitStack() as ctx:
        sb=lambda n, s, d=F32: ctx.enter_context(nc.sbuf_tensor("op_"+n, s, d))
        sem=semaphores(nc, ctx, "op")
        w=sb("w_out", [128, KD, D])
        yb=sb("y", [128, 2, D])
        xb=sb("x", [128, 2, D])
        g1=sb("gate1", [128, D])
        junk=sb("squares", [128, D], mybir.dt.bfloat16)
        gated=sb("gated", [128, 2, 512])
        rows=sb("param_rows", [3*KD, 128])
        yT=sb("yT", [128, 2, KD, 128])
        hT=sb("h2T", [128, KD, 128])
        rw=sb("router_w", [128, KD, NE])
        ident=sb("ident", [128, 128])
        ss=sb("ss", [128, 2])
        eps=sb("eps", [128, 1])
        ps=ctx.enter_context(nc.psum_tensor("op_ps", [128, 8, 512], F32))
        YB, HB, LB=4, 6, 7
        w_loaded=[sem(f"w_loaded{n}") for n in range(4)]
        rows_loaded=sem("rows_loaded")
        gate_loaded=sem("gate_loaded")
        rw_loaded=sem("router_w_loaded")
        made=sem("made")
        y_loaded=[sem(f"y_loaded{j}") for j in range(2)]
        x_loaded=[sem(f"x_loaded{j}") for j in range(2)]
        cols_turned=sem("cols_turned")
        cols_ready=sem("cols_ready")
        y_turned=sem("y_turned")
        yT_ev=sem("yT_copied")
        acc_ready=sem("acc_ready")
        acc_used=sem("acc_used")
        x1_ready=sem("x1_ready")
        ss_ready=sem("ss_ready")
        rs_ready=sem("rstd_ready")
        xn_ready=sem("xn_ready")
        xn_st=sem("xn_stored")
        h_turned=sem("h_turned")
        hT_ev=sem("hT_copied")
        lg_ready=sem("logits_ready")
        lg_copied=sem("logits_copied")
        x1_st=sem("x1_stored")
        sp_waited=sem("sp_waited")
        block=ctx.enter_context(nc.Block())
        def paired(eng, step):
            step(0, 0, first=True)
            with eng.Fori(0, TT//2-1) as g:
                step(g*2+1, 1)
                step(g*2+2, 0)
            step(TT-1, 1, last=True)
        @block.gpsimd
        def _(pool):
            identity_tile(nc, pool, ident, made)
            pool.memset(eps[:], EPS).then_inc(made, 1)
        @block.sync
        def _(sp):
            sp.dma_start(rows[0:KD], norm_g.rearrange("l (k p) -> (l k) p", p=128)).then_inc(rows_loaded, 16)
            sp.dma_start(rows[KD:2*KD], modv[4]).then_inc(rows_loaded, 16)
            sp.dma_start(rows[2*KD:3*KD], modv[3]).then_inc(rows_loaded, 16)
            sp.dma_start(yb[:, 0], yt[0]).then_inc(y_loaded[0], 16)
            wv=w_out.rearrange("l (k p) n -> p (l k) n", p=128)
            sp.dma_start(w[:, :, 0:512], wv[:, :, 0:512]).then_inc(w_loaded[0], 16)
            sp.dma_start(xb[:, 0], xt[0]).then_inc(x_loaded[0], 16)
            sp.dma_start(g1[:], row(2)).then_inc(gate_loaded, 16)
            sp.dma_start(yb[:, 1], yt[1]).then_inc(y_loaded[1], 16)
            for n in range(1, 4): sp.dma_start(w[:, :, n*512:(n+1)*512], wv[:, :, n*512:(n+1)*512]).then_inc(w_loaded[n], 16)
            sp.dma_start(xb[:, 1], xt[1]).then_inc(x_loaded[1], 16)
            sp.dma_start(rw[:], router_w.rearrange("(k p) n -> p k n", p=128)).then_inc(rw_loaded, 16)
            def step(t, j, more):
                if more:
                    sp.wait_ge(y_turned, t*4+8)
                    sp.dma_start(yb[:, j], yt[t+2]).then_inc(y_loaded[j], 16)
                sp.wait_ge(x1_ready, t*4+4)
                sp.dma_start(x1t[t], xb[:, j]).then_inc(x1_st, 16)
                sp.wait_ge(xn_ready, t+1)
                sp.dma_start(xnt[t], xb[:, j]).then_inc(xn_st, 16)
                if more:
                    sp.wait_ge(h_turned, t*4+4)
                    sp.sem_inc(sp_waited, 1)
                    sp.wait_ge(xn_st, t*16+16)
                    sp.dma_start(xb[:, j], xt[t+2]).then_inc(x_loaded[j], 16)
            with sp.Fori(0, TT//2-1) as g:
                for j in range(2): step(g*2+j, j, True)
            for j in range(2): step(TT-2+j, j, False)
            sp.wait_ge(xn_st, 16*TT)
            sp.wait_ge(x1_st, 16*TT)
        @block.tensor
        def _(pe):
            pe.sem_inc(lg_ready, 1)
            pe.wait_ge(made, 2)
            pe.wait_ge(rows_loaded, 48)
            nc.tensor.transpose(ps[:, LB, 0:3*KD], rows[:], ident[0:3*KD, 0:3*KD]).then_inc(cols_turned, 1)
            def y_turn(t, j, i):
                if i==0: pe.wait_ge(y_loaded[j], (t-j)*8+16)
                pe.wait_ge(yT_ev, t*4+i)
                for q in range(4):
                    m=nc.tensor.transpose(ps[:, YB+i%2, q*128:q*128+128], yb[:, j, (4*i+q)*128:(4*i+q+1)*128], ident[:])
                m.then_inc(y_turned, 1)
            def h_turn(t, j, i):
                if i==0: pe.wait_ge(xn_ready, t+1)
                pe.wait_ge(hT_ev, t*4+i+1)
                for q in range(4):
                    m=nc.tensor.transpose(ps[:, HB, q*128:q*128+128], xb[:, j, (4*i+q)*128:(4*i+q+1)*128], ident[:])
                m.then_inc(h_turned, 1)
            def router(t):
                pe.wait_ge(hT_ev, t*4+4+1)
                pe.wait_ge(lg_copied, t+1)
                for k in range(KD):
                    m=nc.tensor.matmul(ps[:, LB, 0:NE], hT[:, k], rw[:, k], start=(k==0), stop=(k==KD-1))
                m.then_inc(lg_ready, 1)
            def step(t, j, first=False, last=False):
                y=lambda i: None if last else y_turn(t+1, 1-j, i)
                h=lambda i: None if first else h_turn(t-1, 1-j, i)
                pe.wait_ge(yT_ev, t*4+5)
                for e in range(8):
                    n=e//2
                    if e%2==0:
                        if first: pe.wait_ge(w_loaded[n], 16)
                        pe.wait_ge(acc_used, t*4+(n+1))
                    for k in range(e%2*8, e%2*8+8):
                        m=nc.tensor.matmul(ps[:, n], yT[:, j, k], w[:, k, n*512:(n+1)*512], start=(k==0), stop=(k==KD-1))
                    if e%2: m.then_inc(acc_ready, 1)
                    if e==1: y(0)
                    if e==2:
                        y(1)
                        h(0)
                    if e==3:
                        y(2)
                        h(1)
                    if e==4:
                        y(3)
                        h(2)
                    if e==5: h(3)
                    if e==6 and first: pe.wait_ge(rw_loaded, 16)
                    if e==6 and not first: router(t-1)
            for i in range(4): y_turn(0, 0, i)
            paired(pe, step)
            for i in range(4): h_turn(TT-1, 1, i)
            router(TT-1)
        @block.scalar
        def _(act):
            act.sem_inc(hT_ev, 1)
            act.sem_inc(lg_copied, 1)
            act.wait_ge(made, 3)
            act.sem_inc(yT_ev, 1)
            def y_copy(t, j, i):
                act.wait_ge(y_turned, t*4+(i+1))
                nc.scalar.copy(yT[:, j, 4*i:4*i+4].rearrange("p k n -> p (k n)"), ps[:, YB+i%2]).then_inc(yT_ev, 1)
            def norm(t, j):
                act.wait_ge(x1_ready, t*4+4)
                nc.scalar.activation(junk[:], xb[:, j], ACT.Square, scale=float(D)**-0.5, accum_out=ss[:, j:j+1]).then_inc(ss_ready, 1)
                act.wait_ge(ss_ready, t*2+1)
                nc.scalar.activation(ss[:, j:j+1], ss[:, j:j+1], ACT.Ln, bias=eps[:]).then_inc(ss_ready, 1)
                act.wait_ge(ss_ready, t*2+2)
                nc.scalar.activation(ss[:, j:j+1], ss[:, j:j+1], ACT.Exp, scale=-0.5).then_inc(rs_ready, 1)
            def h_copy(t, j, i):
                if i==0: act.wait_ge(lg_ready, t+1)
                act.wait_ge(h_turned, t*4+(i+1))
                for k in range(4*i, 4*i+4):
                    m=nc.scalar.activation(hT[:, k], ps[:, HB, (k-4*i)*128:(k-4*i)*128+128], ACT.Identity, scale=ffn_cols[:, k:k+1], bias=ffn_cols[:, KD+k:KD+k+1])
                m.then_inc(hT_ev, 1)
            def logits_copy(t):
                act.wait_ge(lg_ready, t+2)
                nc.scalar.copy(logits[:, bass.ds(t, 1), :].rearrange("p o e -> p (o e)"), ps[:, LB, 0:NE]).then_inc(lg_copied, 1)
            def step(t, j, first=False, last=False):
                y=lambda i: None if last else y_copy(t+1, 1-j, i)
                h=lambda i: None if first else h_copy(t-1, 1-j, i)
                if not first:
                    norm(t-1, 1-j)
                    act.wait_ge(acc_ready, t*4)
                y(0)
                y(1)
                h(0)
                y(2)
                h(1)
                y(3)
                h(2)
                h(3)
                if not first: logits_copy(t-1)
            for i in range(4): y_copy(0, 0, i)
            act.wait_ge(cols_ready, 2)
            paired(act, step)
            norm(TT-1, 1)
            for i in range(4): h_copy(TT-1, 1, i)
            logits_copy(TT-1)
        @block.vector
        def _(dve):
            dve.sem_inc(acc_used, 4)
            dve.wait_ge(cols_turned, 1)
            nc.vector.tensor_copy(ffn_cols[:], ps[:, LB, KD:3*KD]).then_inc(cols_ready, 1)
            dve.wait_ge(cols_ready, 1)
            nc.vector.scalar_tensor_tensor(out=ffn_cols[:, 0:KD], in0=ffn_cols[:, 0:KD], scalar=1.0, in1=ps[:, LB, 0:KD], op0=ALU.add, op1=ALU.mult).then_inc(cols_ready, 1)
            dve.wait_ge(gate_loaded, 16)
            def step(t, j):
                dve.wait_ge(x_loaded[j], (t-j)*8+16)
                for n in range(4):
                    c=slice(n*512, (n+1)*512)
                    dve.wait_ge(acc_ready, t*4+(n+1))
                    nc.vector.tensor_tensor(gated[:, n%2], ps[:, n], g1[:, c], ALU.mult).then_inc(acc_used, 1)
                    dve.wait_ge(acc_used, t*4+(n+5))
                    nc.vector.tensor_tensor(xb[:, j, c], xb[:, j, c], gated[:, n%2], ALU.add).then_inc(x1_ready, 1)
                dve.wait_ge(rs_ready, t+1)
                dve.wait_ge(x1_st, t*16+16)
                nc.vector.tensor_scalar(xb[:, j], xb[:, j], ss[:, j:j+1], None, ALU.mult).then_inc(xn_ready, 1)
            with dve.Fori(0, TT//2) as g:
                for j in range(2): step(g*2+j, j)
            dve.wait_ge(lg_copied, TT+1)

MT_ALL=MT+1

def routing(nc, logits, router_b, token_of_slot, slots, gates, tile_expert, new_expert, tiles_used):
    with ExitStack() as ctx:
        sb=lambda n, s, d=F32: ctx.enter_context(nc.sbuf_tensor("rt_"+n, s, d))
        sem=semaphores(nc, ctx, "rt")
        NG_=TT*GRP
        E_=TT*NE
        rb=sb("router_b", [128, NE])
        aff=sb("affinity", [128, TT, NE])
        sel=sb("selection", [128, TT, NE])
        ie=sb("expert_iota_m8", [128, EPG])
        ig=sb("group_iota_m4", [128, GRP])
        tri=sb("before", [128, 128])
        ones=sb("ones", [128, 128])
        zeros=sb("zero_slots", [128, MT_ALL], I32)
        m=sb("best", [128, 2, NG_])
        i8=sb("first_index", [128, 2, NG_])
        t8=sb("tmp", [128, TT, NE])
        oh=sb("onehot", [128, 2, TT, NE])
        M=sb("chosen", [128, TT, NE])
        gs=sb("group_score", [128, TT, GRP])
        gb=sb("group_best", [128, TT])
        gi=sb("group_index", [128, TT])
        goh=sb("group_onehot", [128, TT, GRP])
        carry=sb("carry", [128, TT+1, NE])
        mi=sb("multiples_of_128", [128, S//128])
        cmp=sb("compare", [128, NE, S//128])
        nt=sb("tiles_of_expert", [128, NE])
        end=sb("end_tile", [128, NE])
        one=sb("one_row", [128, NE])
        base=sb("first_slot", [128, NE])
        ti=sb("tile_iota", [1, MT_ALL])
        tc=sb("tile_compare", [1, MT_ALL, NE])
        te=sb("tile_expert_f", [1, MT_ALL])
        tf=sb("tile_fresh", [1, MT_ALL])
        sf=sb("slots_f", [128, 2, TT])
        a12=sb("gates_raw", [128, 2, TT])
        asum=sb("gate_sum", [128, TT])
        ps=ctx.enter_context(nc.psum_tensor("rt_ps", [128, 2, 512], F32))
        made=sem("made")
        rb_loaded=sem("rb_loaded")
        zeroed=sem("zeroed")
        ex=sem("exp_ready")
        v=sem("vector_done")
        ranked=sem("ranked")
        chosen=sem("chosen")
        slotted=sem("slotted")
        block=ctx.enter_context(nc.Block())
        v8=lambda t: t.rearrange("p t (g e) -> p (t g) e", g=GRP)
        up=lambda ap, n: ap.rearrange("p (n o) -> p n o", o=1).to_broadcast([128, ap.shape[1], n])
        lead=lambda ap, n: ap.rearrange("p (o n) -> p o n", o=1).to_broadcast([ap.shape[0], n, ap.shape[1]])
        @block.sync
        def _(sp):
            sp.dma_start(rb[:], router_b.rearrange("(o e) -> o e", o=1).to_broadcast([128, NE])).then_inc(rb_loaded, 16)
            sp.wait_ge(made, 8)
            sp.dma_start(token_of_slot.rearrange("(p t) o -> p (t o)", p=128), zeros[:]).then_inc(zeroed, 16)
            sp.wait_ge(rb_loaded, 16)
        @block.gpsimd
        def _(pool):
            ap=dict(allow_small_or_imprecise_dtypes=True)
            pool.iota(ie[:], pattern=[[1, EPG]], base=-EPG, channel_multiplier=0, **ap).then_inc(made, 1)
            pool.iota(ig[:], pattern=[[1, GRP]], base=-GRP, channel_multiplier=0, **ap).then_inc(made, 1)
            pool.iota(mi[:], pattern=[[128, S//128]], base=0, channel_multiplier=0, **ap).then_inc(made, 1)
            pool.iota(ti[:], pattern=[[1, MT_ALL]], base=0, channel_multiplier=0, **ap).then_inc(made, 1)
            pool.memset(ones[:], 1.0).then_inc(made, 1)
            pool.memset(tri[:], 1.0).then_inc(made, 1)
            pool.memset(one[:], 1.0).then_inc(made, 1)
            pool.memset(zeros[:], 0).then_inc(made, 1)
            pool.wait_ge(made, 8)
            pool.affine_select(out=tri[:], in_=tri[:], compare_op=ALU.is_gt, fill=0.0, base=0, pattern=[[1, 128]], channel_multiplier=-1).then_inc(made, 1)
            pool.wait_ge(zeroed, 16)
        @block.scalar
        def _(act):
            nc.scalar.activation(aff[:].rearrange("p t e -> p (t e)"), logits[:].rearrange("p t e -> p (t e)"), ACT.Exp, scale=-1.0).then_inc(ex, 1)
        @block.tensor
        def _(pe):
            pe.wait_ge(made, 9)
            pe.wait_ge(chosen, 1)
            r=M[:].rearrange("p t e -> p (t e)")
            nc.tensor.matmul(ps[:, 0], tri[:], r, start=True, stop=True)
            nc.tensor.matmul(ps[:, 1], ones[:], r, start=True, stop=True).then_inc(ranked, 1)
        @block.vector
        def _(dve):
            n=[0]
            def then(ins):
                n[0]+=1
                ins.then_inc(v, 1)
                dve.wait_ge(v, n[0])
            V=nc.vector
            dve.wait_ge(ex, 1)
            dve.wait_ge(rb_loaded, 16)
            dve.wait_ge(made, 9)
            then(V.tensor_scalar(aff[:], aff[:], 1.0, None, ALU.add))
            then(V.reciprocal(aff[:], aff[:]))
            then(V.tensor_tensor(sel[:], aff[:], lead(rb[:], TT), ALU.add))
            for q in range(2):
                then(V.tensor_reduce(m[:, q], v8(sel[:]), AX.X, ALU.max))
                then(V.tensor_tensor(v8(t8[:]), v8(sel[:]), up(m[:, q], EPG), ALU.is_equal))
                then(V.tensor_tensor(v8(t8[:]), v8(t8[:]), lead(ie[:], NG_), ALU.mult))
                then(V.tensor_reduce(i8[:, q], v8(t8[:]), AX.X, ALU.min))
                then(V.tensor_tensor(v8(oh[:, q]), lead(ie[:], NG_), up(i8[:, q], EPG), ALU.is_equal))
                if q==0: then(V.scalar_tensor_tensor(out=sel[:], in0=oh[:, 0], scalar=-BIG, in1=sel[:], op0=ALU.mult, op1=ALU.add))
            then(V.tensor_tensor(gs[:].rearrange("p t g -> p (t g)"), m[:, 0], m[:, 1], ALU.add))
            then(V.tensor_reduce(gb[:], gs[:], AX.X, ALU.max))
            then(V.tensor_tensor(gs[:], gs[:], up(gb[:], GRP), ALU.is_equal))
            then(V.tensor_tensor(gs[:], gs[:], lead(ig[:], TT), ALU.mult))
            then(V.tensor_reduce(gi[:], gs[:], AX.X, ALU.min))
            then(V.tensor_tensor(goh[:], lead(ig[:], TT), up(gi[:], GRP), ALU.is_equal))
            gflat=goh[:].rearrange("p t g -> p (t g)")
            for q in range(2):
                then(V.tensor_tensor(v8(oh[:, q]), v8(oh[:, q]), up(gflat, EPG), ALU.mult))
                then(V.tensor_tensor(t8[:], oh[:, q], aff[:], ALU.mult))
                then(V.tensor_reduce(a12[:, q], t8[:], AX.X, ALU.add))
            then(V.tensor_tensor(asum[:], a12[:, 0], a12[:, 1], ALU.add))
            then(V.reciprocal(asum[:], asum[:]))
            for q in range(2): then(V.tensor_tensor(gates[:, q], a12[:, q], asum[:], ALU.mult))
            V.tensor_tensor(M[:], oh[:, 0], oh[:, 1], ALU.add).then_inc(chosen, 1)
            dve.wait_ge(ranked, 1)
            then(V.memset(carry[:, 0], 0.0))
            for t in range(TT):
                then(V.tensor_tensor(carry[:, t+1], carry[:, t], ps[:, 1, t*NE:(t+1)*NE], ALU.add))
            then(V.tensor_tensor(cmp[:], up(carry[:, TT], S//128), lead(mi[:], NE), ALU.is_gt))
            then(V.tensor_reduce(nt[:], cmp[:], AX.X, ALU.add))
            then(V.tensor_tensor_scan(end[:], one[:], nt[:], 0.0, ALU.mult, ALU.add))
            then(V.tensor_tensor(base[:], end[:], nt[:], ALU.subtract))
            then(V.tensor_scalar(base[:], base[:], 128.0, None, ALU.mult))
            then(V.tensor_tensor(M[:], carry[:, 0:TT], lead(base[:], TT), ALU.add))
            then(V.tensor_tensor(M[:].rearrange("p t e -> p (t e)"), M[:].rearrange("p t e -> p (t e)"), ps[:, 0], ALU.add))
            for q in range(2):
                then(V.tensor_tensor(t8[:], oh[:, q], M[:], ALU.mult))
                then(V.tensor_reduce(sf[:, q], t8[:], AX.X, ALU.add))
            V.tensor_copy(slots[:], sf[:]).then_inc(slotted, 1)
            ebc=end[0:1].rearrange("p (o e) -> p o e", o=1).to_broadcast([1, MT_ALL, NE])
            tbc=ti[:].rearrange("p (t o) -> p t o", o=1).to_broadcast([1, MT_ALL, NE])
            then(V.tensor_tensor(tc[:], ebc, tbc, ALU.is_le))
            then(V.tensor_reduce(te[:], tc[:], AX.X, ALU.add))
            then(V.tensor_scalar(te[:], te[:], float(NE-1), None, ALU.min))
            then(V.tensor_copy(tile_expert[:], te[:]))
            then(V.memset(new_expert[:, 0:1], 1))
            then(V.tensor_scalar(ti[:], ti[:], end[0:1, NE-1:NE], None, ALU.is_lt))
            then(V.tensor_tensor(tf[:, 1:], te[:, 1:], te[:, 0:MT_ALL-1], ALU.is_gt))
            then(V.tensor_tensor(new_expert[:, 1:], tf[:, 1:], ti[:, 1:], ALU.mult))
            then(V.tensor_copy(tiles_used[:, 0:1], end[0:1, NE-1:NE]))
            then(V.tensor_scalar(tiles_used[:, 1:2], end[0:1, NE-1:NE], -1.0, None, ALU.add))

def experts(nc, xn, ffn_cols, mod, w_gate_up, w_down, slots, token_of_slot, tile_expert, new_expert, tiles_used, ys):
    KF=FF//128
    GC=8
    yst=ys.rearrange("(t p) d -> t p d", p=128)
    wgv=w_gate_up.rearrange("l e (k p) n -> p (l e k) n", p=128)
    wdv=w_down.rearrange("l e (k p) n -> p (l e k) n", p=128)
    with ExitStack() as ctx:
        sb=lambda n, s, d=F32: ctx.enter_context(nc.sbuf_tensor("ex_"+n, s, d))
        sem=semaphores(nc, ctx, "ex")
        wg=sb("w_gate_up", [128, KD, 2*FF])
        wd=sb("w_down", [128, KF, D])
        xg=sb("x", [128, 2, D])
        xT=sb("xT", [128, 2, KD, 128])
        g2=sb("gate2", [128, D])
        idx=sb("token_idx", [128, MT_ALL], I32)
        ic=sb("tile_idx", [128, 2], I32)
        sg=sb("sigmoid", [128, FF])
        gu=sb("gate_sig", [128, FF])
        a=sb("act", [128, FF])
        aT=sb("actT", [128, KF, 128])
        yo=sb("y", [128, D])
        tok=sb("token_ids", [128, TT], I32)
        ident=sb("ident", [128, 128])
        ps=ctx.enter_context(nc.psum_tensor("ex_ps", [128, 8, 512], F32))
        GU, TR, DN=0, 2, 4
        made=sem("made")
        tok_made=sem("token_ids_made")
        scattered=sem("scattered")
        idx_loaded=sem("token_idx_loaded")
        rows=sem("gate2_loaded")
        wg_l=[sem(f"wg_loaded{i}") for i in range(GC)]
        wd_l=[sem(f"wd_loaded{i}") for i in range(KF)]
        wg_used=sem("wg_used")
        wd_used=sem("wd_used")
        idx_ready=sem("idx_ready")
        pool_waited=sem("pool_waited")
        act_waited=sem("act_waited")
        x_l=[sem(f"x_loaded{j}") for j in range(2)]
        x_turned=sem("x_turned")
        x_part=sem("x_part_turned")
        xT_act=sem("xT_act")
        xT_dve=sem("xT_dve")
        gu_ready=sem("gu_ready")
        sig=sem("sig_ready")
        gated=sem("gated")
        a_ready=sem("act_ready")
        a_turned=sem("act_turned")
        aT_ready=sem("actT_ready")
        dn_ready=sem("down_ready")
        y_ready=sem("y_ready")
        y_st=sem("y_stored")
        block=ctx.enter_context(nc.Block())
        def tiles(eng, step, last, reg):
            step(0, 0, True)
            used=eng.value_load(tiles_used[0:1, 0:1], min_val=1, max_val=MT)
            with eng.Fori(0, (MT-1)//2) as g:
                for j, d in ((1, 1), (0, 2)):
                    t=g*2+d
                    with eng.If(t<used): step(t, j, False)
            last(used, eng.value_load(tiles_used[0:1, 1:2], min_val=0, max_val=MT-1))
        @block.sync
        def _(sp):
            sp.dma_start(g2[:], mod[:, 5*D:6*D].to_broadcast([128, D])).then_inc(rows, 16)
            def weights(t, pieces, piece_size, used, w_sb, w_view, loaded, kept):
                e=sp.value_load(tile_expert[0:1, bass.ds(t, 1)], min_val=0, max_val=NE-1)
                def each(load):
                    for i in range(pieces):
                        sp.wait_ge(used, t*pieces+(i+1))
                        k=slice(i*piece_size, (i+1)*piece_size)
                        if load: sp.dma_start(w_sb[:, k], w_view[:, bass.ds(e*(pieces*piece_size)+i*piece_size, piece_size)]).then_inc(loaded[i], 16)
                        else: sp.sem_inc(loaded[i], 16)
                if not kept: each(True)
                else:
                    fresh=sp.value_load(new_expert[0:1, bass.ds(t, 1)], min_val=0, max_val=1)
                    with sp.If(fresh>0): each(True)
                    with sp.If(fresh<1): each(False)
            gate_up_w=lambda t, kept: weights(t, GC, KD//GC, wg_used, wg, wgv, wg_l, kept)
            down_w=lambda t, kept: weights(t, KF, 1, wd_used, wd, wdv, wd_l, kept)
            gate_up_w(0, False)
            def step(t, j, first):
                if first: down_w(0, False)
                gate_up_w(t+1, True)
                if not first: down_w(t, True)
            tiles(sp, step, lambda used, final: None, None)
        @block.gpsimd
        def _(pool):
            pool.iota(tok[:], pattern=[[128, TT]], base=0, channel_multiplier=1).then_inc(tok_made, 1)
            pool.wait_ge(tok_made, 1)
            for q in range(2):
                for t in range(TT):
                    pool.indirect_dma_start(out=token_of_slot, out_offset=bass.IndirectOffsetOnAxis(ap=slots[:, q, t:t+1], axis=0), in_=tok[:, t:t+1], in_offset=None).then_inc(scattered, 16)
            identity_tile(nc, pool, ident, made)
            pool.wait_ge(scattered, 32*TT)
            with nc.allow_non_contiguous_dma(reason="a slot's token is one word"):
                pool.dma_start(idx[:], token_of_slot.rearrange("(t p) o -> p (t o)", p=128)).then_inc(idx_loaded, 16)
            pool.wait_ge(idx_loaded, 16)
            def gather(t, j, n):
                pool.tensor_copy(ic[:, j:j+1], idx[:, bass.ds(t, 1)]).then_inc(idx_ready, 1)
                pool.wait_ge(idx_ready, t+1)
                pool.sem_inc(pool_waited, 1)
                pool.indirect_dma_start(out=xg[:, j], out_offset=None, in_=xn, in_offset=bass.IndirectOffsetOnAxis(ap=ic[:, j:j+1], axis=0)).then_inc(x_l[j], 16)
            gather(0, 0, 0)
            def step(t, j, first):
                pool.wait_ge(x_turned, t)
                gather(t+1, 1-j, 0)
            def last(used, _):
                pool.wait_ge(x_turned, used+1)
            tiles(pool, step, last, None)
        @block.tensor
        def _(pe):
            pe.wait_ge(made, 2)
            pe.sem_inc(wg_used, GC)
            pe.sem_inc(wd_used, KF)
            def turn_x(t, j, n2):
                pe.wait_ge(x_l[j], n2)
                if not (isinstance(t, int) and t==0): pe.wait_ge(aT_ready, t-1)
                for i in range(4):
                    pe.wait_ge((xT_act, xT_dve)[i%2], t*2+(i//2+1))
                    for q in range(4):
                        m=nc.tensor.transpose(ps[:, TR+i%2, q*128:q*128+128], xg[:, j, (4*i+q)*128:(4*i+q+1)*128], ident[:])
                    if i<3: m.then_inc(x_part, 1)
                    else: m.then_inc(x_turned, 1)
            def gate_up(t, j):
                pe.wait_ge(xT_act, t*2+3)
                pe.wait_ge(xT_dve, t*2+3)
                pe.wait_ge(gated, t)
                pe.wait_ge(a_ready, t)
                for i in range(GC):
                    pe.wait_ge(wg_l[i], t*16+16)
                    for k in (2*i, 2*i+1):
                        for n in range(2):
                            m=nc.tensor.matmul(ps[:, GU+n], xT[:, j, k], wg[:, k, n*512:(n+1)*512], start=(k==0), stop=(k==KD-1))
                    m.then_inc(wg_used, 1)
            def turn_a(t):
                pe.wait_ge(a_ready, t+1)
                pe.wait_ge(xT_act, t*2+5)
                for k in range(KF):
                    m=nc.tensor.transpose(ps[:, TR, k*128:(k+1)*128], a[:, k*128:(k+1)*128], ident[:])
                m.then_inc(a_turned, 1)
            def down(t):
                pe.wait_ge(aT_ready, t+1)
                pe.wait_ge(y_ready, t*4+1)
                for k in range(KF):
                    pe.wait_ge(wd_l[k], t*16+16)
                    for n in range(4):
                        m=nc.tensor.matmul(ps[:, DN+n], aT[:, k], wd[:, k, n*512:(n+1)*512], start=(k==0), stop=(k==KF-1))
                        if n==3: m.then_inc(wd_used, 1)
            def step(t, j, first):
                if first: turn_x(0, 0, 16)
                gate_up(t, j)
                n2=16 if first else (t+1-(1-j))*8+16
                turn_x(t+1, 1-j, n2)
                if not first: down(t-1)
                turn_a(t)
            tiles(pe, step, lambda used, final: down(final), None)
        @block.scalar
        def _(act):
            act.sem_inc(y_st, 16)
            act.sem_inc(xT_act, 1)
            def copy_x(t, j, part):
                for i in (0, 2):
                    if i==0:
                        act.wait_ge(wg_used, t*GC)
                        act.wait_ge(x_part, t*3+1)
                    else: act.wait_ge(x_part, t*3+3)
                    for k in range(4*i, 4*i+4):
                        m=nc.scalar.activation(xT[:, j, k], ps[:, TR, (k-4*i)*128:(k-4*i)*128+128], ACT.Identity, scale=ffn_cols[:, k:k+1], bias=ffn_cols[:, KD+k:KD+k+1])
                    m.then_inc(xT_act, 1)
            def store(t):
                act.wait_ge(y_ready, t*4+4+1)
                act.dma_start(yst[t], yo[:]).then_inc(y_st, 16)
            def step(t, j, first):
                if first: copy_x(0, 0, 0)
                act.wait_ge(wg_used, t*GC+2*GC)
                act.wait_ge(gated, t)
                nc.scalar.activation(sg[:], ps[:, GU], ACT.Sigmoid).then_inc(sig, 1)
                copy_x(t+1, 1-j, 0)
                act.wait_ge(a_turned, t+1)
                act.wait_ge(wd_used, t*KF+KF)
                nc.scalar.copy(aT[:].rearrange("p k n -> p (k n)"), ps[:, TR]).then_inc(aT_ready, 1)
                if not first: store(t-1)
            def last(used, final):
                store(final)
                act.wait_ge(y_st, used*16+16)
                act.sem_inc(act_waited, 1)
            tiles(act, step, last, None)
        @block.vector
        def _(dve):
            dve.sem_inc(y_ready, 1)
            dve.sem_inc(xT_dve, 1)
            dve.wait_ge(rows, 16)
            def copy_x(t, j):
                for i in (1, 3):
                    if i==1:
                        dve.wait_ge(x_part, t*3+2)
                        dve.wait_ge(wg_used, t*GC)
                    else: dve.wait_ge(x_turned, t+1)
                    for k in range(4*i, 4*i+4):
                        m=nc.vector.tensor_scalar(xT[:, j, k], ps[:, TR+1, (k-4*i)*128:(k-4*i)*128+128], ffn_cols[:, k:k+1], ffn_cols[:, KD+k:KD+k+1], ALU.mult, ALU.add)
                    m.then_inc(xT_dve, 1)
            def y_out(t):
                dve.wait_ge(wd_used, t*KF+2*KF)
                dve.wait_ge(y_st, t*16+16)
                for n in range(4):
                    nc.vector.tensor_tensor(yo[:, n*512:(n+1)*512], ps[:, DN+n], g2[:, n*512:(n+1)*512], ALU.mult).then_inc(y_ready, 1)
            def step(t, j, first):
                if first: copy_x(0, 0)
                dve.wait_ge(sig, t+1)
                nc.vector.tensor_tensor(gu[:], ps[:, GU], sg[:], ALU.mult).then_inc(gated, 1)
                dve.wait_ge(gated, t+1)
                dve.wait_ge(a_turned, t)
                nc.vector.tensor_tensor(a[:], ps[:, GU+1], gu[:], ALU.mult).then_inc(a_ready, 1)
                copy_x(t+1, 1-j)
                if not first: y_out(t-1)
            tiles(dve, step, lambda used, final: y_out(final), None)
    
def combine(nc, x1, ys, slots, gates, final_g, out):
    x1t=x1.rearrange("(t p) d -> t p d", p=128)
    ot=out.rearrange("b (t p) d -> (b t) p d", p=128)
    NB=4
    with ExitStack() as ctx:
        sb=lambda n, s, d=F32: ctx.enter_context(nc.sbuf_tensor("co_"+n, s, d))
        sem=semaphores(nc, ctx, "co")
        xb=sb("x", [128, NB, D])
        y1=sb("y1", [128, NB, D])
        y2=sb("y2", [128, NB, D])
        g=sb("final_g", [128, D])
        ic=sb("slot_idx", [128, 2, NB], I32)
        ss=sb("ss", [128, NB])
        eps=sb("eps", [128, 1])
        g_l=sem("g_loaded")
        made=sem("made")
        x_l=[sem(f"x_loaded{j}") for j in range(NB)]
        y_l=[sem(f"y_loaded{j}") for j in range(NB)]
        y1s=sem("y1_scaled")
        ysum=sem("y_sum")
        xs=sem("x_sum")
        sse=sem("ss_steps")
        done=sem("out_ready")
        st=[sem(f"stored{j}") for j in range(NB)]
        block=ctx.enter_context(nc.Block())
        def loop(eng, f):
            with eng.Fori(0, TT//NB) as q:
                for j in range(NB): f(q, q*NB+j, j)
        @block.sync
        def _(sp):
            sp.dma_start(g[:], final_g.rearrange("(o d) -> o d", o=1).to_broadcast([128, D])).then_inc(g_l, 16)
            for j in range(NB): sp.dma_start(xb[:, j], x1t[j]).then_inc(x_l[j], 16)
            def store(t, j):
                sp.wait_ge(done, t+1)
                sp.dma_start(ot[t], y1[:, j]).then_inc(st[j], 16)
            with sp.Fori(0, TT//NB-1) as q:
                for j in range(NB):
                    store(q*NB+j, j)
                    sp.dma_start(xb[:, j], x1t[q*NB+(j+NB)]).then_inc(x_l[j], 16)
            for j in range(NB): store(TT-NB+j, j)
            for j in range(NB): sp.wait_ge(st[j], 16*TT//NB)
        @block.gpsimd
        def _(pool):
            pool.memset(eps[:], EPS).then_inc(made, 1)
            def f(q, t, j):
                pool.wait_ge(st[j], q*16)
                pool.indirect_dma_start(out=y1[:, j], out_offset=None, in_=ys, in_offset=bass.IndirectOffsetOnAxis(ap=slots[:, 0, t:t+1], axis=0)).then_inc(y_l[j], 16)
                pool.indirect_dma_start(out=y2[:, j], out_offset=None, in_=ys, in_offset=bass.IndirectOffsetOnAxis(ap=slots[:, 1, t:t+1], axis=0)).then_inc(y_l[j], 16)
            for t in range(TT): f(t//NB, t, t%NB)
        @block.scalar
        def _(act):
            act.wait_ge(made, 1)
            def f(q, t, j):
                act.wait_ge(y_l[j], q*32+32)
                nc.scalar.activation(y1[:, j], y1[:, j], ACT.Copy, scale=gates[:, 0, bass.ds(t, 1)]).then_inc(y1s, 1)
                act.wait_ge(xs, t+1)
                nc.scalar.activation(y2[:, j], xb[:, j], ACT.Square, scale=float(D)**-0.5, accum_out=ss[:, j:j+1]).then_inc(sse, 1)
                act.wait_ge(sse, t*3+1)
                nc.scalar.activation(ss[:, j:j+1], ss[:, j:j+1], ACT.Ln, bias=eps[:]).then_inc(sse, 1)
                act.wait_ge(sse, t*3+2)
                nc.scalar.activation(ss[:, j:j+1], ss[:, j:j+1], ACT.Exp, scale=-0.5).then_inc(sse, 1)
            loop(act, f)
        @block.vector
        def _(dve):
            dve.wait_ge(g_l, 16)
            def f(q, t, j):
                dve.wait_ge(y1s, t+1)
                nc.vector.scalar_tensor_tensor(out=y1[:, j], in0=y2[:, j], scalar=gates[:, 1, bass.ds(t, 1)], in1=y1[:, j], op0=ALU.mult, op1=ALU.add).then_inc(ysum, 1)
                dve.wait_ge(ysum, t+1)
                dve.wait_ge(x_l[j], q*16+16)
                nc.vector.tensor_tensor(xb[:, j], xb[:, j], y1[:, j], ALU.add).then_inc(xs, 1)
                dve.wait_ge(sse, t*3+3)
                nc.vector.scalar_tensor_tensor(out=y1[:, j], in0=xb[:, j], scalar=ss[:, j:j+1], in1=g[:], op0=ALU.mult, op1=ALU.mult).then_inc(done, 1)
            loop(dve, f)

def hybrid_layer(nc, x, c, ada_w, ada_b, mix_norm_g, w_in, cq_norm_g, ckv_norm_g, w_uq, w_uk, w_uv, w_qidx,
                 mlstm_i_b, mlstm_f_b, mlstm_norm_g, w_out, ffn_norm_g, router_w, router_b, w_gate_up, w_down,
                 final_norm_g, out):
    scratch = lambda name, shape, dtype=F32: nc.dram_tensor(name, shape, dtype).ap()
    mod = scratch("mod", [1, 6 * D])
    h_tiles = scratch("h_tiles", [TT, 128, KD, 128])
    z = scratch("z", [S, D_IN])
    y = scratch("y", [S, D])
    x1 = scratch("x1", [S, D])
    xn = scratch("x1_normed", [S, D])
    token_of_slot = scratch("token_of_slot", [SLOTS_, 1], I32)
    ys = scratch("ys", [SLOTS_, D])
    with nc.sbuf_tensor("silu_c", [128, KD], F32) as s_col:
        modulation(nc, c, ada_w, ada_b, mod, s_col)
        in_projection(nc, x, mod, mix_norm_g, w_in, z, h_tiles)
        dsa(nc, s_col, ada_w, ada_b, mod, z, h_tiles, w_in, cq_norm_g, ckv_norm_g, w_uq, w_uk, w_uv, w_qidx, y, ys)
    mlstm(nc, z, mlstm_i_b, mlstm_f_b, mlstm_norm_g, y)
    with ExitStack() as ctx:
        sb = lambda n, s, d=F32: ctx.enter_context(nc.sbuf_tensor(n, s, d))
        logits = sb("logits", [128, TT, NE])
        slots = sb("slots", [128, 2, TT], I32)
        gates = sb("gates", [128, 2, TT])
        tile_expert = sb("tile_expert", [1, MT_ALL], I32)
        new_expert = sb("new_expert", [1, MT_ALL], I32)
        ffn_cols = sb("ffn_cols", [128, 2 * KD])
        tiles_used = sb("tiles_used", [1, 2], I32)
        out_projection(nc, y, x, mod, w_out, ffn_norm_g, router_w, x1, xn, ffn_cols, logits)
        routing(nc, logits, router_b, token_of_slot, slots, gates, tile_expert, new_expert, tiles_used)
        experts(nc, xn, ffn_cols, mod, w_gate_up, w_down, slots, token_of_slot, tile_expert, new_expert, tiles_used, ys)
        combine(nc, x1, ys, slots, gates, final_norm_g, out)


_INS = ["x", "c", "ada_w", "ada_b", "mix_norm_g", "w_in", "cq_norm_g", "ckv_norm_g", "w_uq", "w_uk", "w_uv", "w_qidx",
        "mlstm_i_b", "mlstm_f_b", "mlstm_norm_g", "w_out", "ffn_norm_g", "router_w", "router_b", "w_gate_up", "w_down",
        "final_norm_g"]
_OUTS = [((1, S, D), "float32")]


def kernel(**inputs):
    import numpy as _np
    import concourse.bacc as _bacc
    from concourse import mybir as _mybir
    from concourse.bass_utils import run_bass_kernel_spmd as _run

    nc = _bacc.Bacc("TRN2", target_bir_lowering=False, num_devices=1)
    arrays, args = {}, []
    for name in _INS:
        a = _np.ascontiguousarray(inputs[name])
        arrays[f"in_{name}_dram"] = a
        args.append(nc.dram_tensor(f"in_{name}_dram", a.shape, _mybir.dt.from_np(a.dtype), kind="ExternalInput").ap())
    for i, (shape, dtype) in enumerate(_OUTS):
        dt = _mybir.dt.from_np(_np.dtype(dtype))
        args.append(nc.dram_tensor(f"out_{i}_dram", shape, dt, kind="ExternalOutput").ap())
    hybrid_layer(nc, *args)
    r = _run(nc, [arrays], core_ids=[0])
    got = tuple(r.results[0][f"out_{i}_dram"] for i in range(len(_OUTS)))
    return got[0]
```
